# Optimizing a Trainium2 kernel written in Bass

```python
import jax
import jax.numpy as jnp
from jax import lax
import numpy as np

D_MODEL = 1024
BATCH = 1
SEQ = 256
DEPTH = 2
DEC_BATCH = 8
DEC_SEQ = 1
PAST_LEN = 2048
PAGE_SIZE = 128

MLA_HEADS = 4
QK_NOPE = 64
QK_ROPE = 32
QK_HEAD = QK_NOPE + QK_ROPE
V_HEAD = 128
Q_RANK = 384
KV_RANK = 256
ROPE_THETA = 10000.0
GLA_HEADS = 4
GLA_DK = 32
GLA_DV = 64
GLA_GATE_RANK = 16
GLA_TAU = 16.0
GLA_CHUNK = 64
POOL_WINDOWS = (2, 4, 8, 16)
POOL_GROUP = 64
POOL_WIDTH = POOL_GROUP * len(POOL_WINDOWS)
POOL_BUF = max(POOL_WINDOWS) - 1
MLA_OUT = MLA_HEADS * V_HEAD
GLA_OUT = GLA_HEADS * GLA_DV
D_MIX = MLA_OUT + GLA_OUT + POOL_WIDTH
IN_SIZES = (Q_RANK, KV_RANK, QK_ROPE, GLA_HEADS * GLA_DK, GLA_HEADS * GLA_DK, GLA_HEADS * GLA_DV, GLA_GATE_RANK, GLA_OUT, POOL_WIDTH)
D_IN = sum(IN_SIZES)
N_MEM = 256
XA_HEADS = 4
XA_HEAD = D_MODEL // XA_HEADS
D_FF = 4 * D_MODEL
Q_BLOCK = 128
EPS = 1e-6

kernel_name = 'hybrid_mla_gla_pool_decoder_step'

def _rmsnorm(x, g):
    xf = x.astype(jnp.float32)
    y = xf * lax.rsqrt(jnp.mean(xf * xf, axis=-1, keepdims=True) + EPS)
    return (y * g.astype(jnp.float32)).astype(x.dtype)

def _rope(x, pos):
    half = x.shape[-1] // 2
    inv = ROPE_THETA ** (-jnp.arange(half, dtype=jnp.float32) / half)
    ang = pos.astype(jnp.float32)[:, None] * inv[None, :]
    cos = jnp.cos(ang)[:, None, :]
    sin = jnp.sin(ang)[:, None, :]
    xf = x.astype(jnp.float32)
    x1, x2 = xf[..., :half], xf[..., half:]
    return jnp.concatenate([x1 * cos - x2 * sin, x2 * cos + x1 * sin], axis=-1).astype(x.dtype)

def _split_in(z):
    parts, off = [], 0
    for size in IN_SIZES:
        parts.append(z[..., off:off + size])
        off += size
    return parts

def _causal_attend(q, k, v, q_pos, k_pos, scale):
    def attend(qb, qpb):
        s = jnp.einsum('bqhd,bkhd->bhqk', qb, k, preferred_element_type=jnp.float32) * scale
        mask = k_pos[None, :] <= qpb[:, None]
        s = jnp.where(mask[None, None], s, -jnp.inf)
        p = jax.nn.softmax(s, axis=-1).astype(v.dtype)
        return jnp.einsum('bhqk,bkhd->bqhd', p, v)
    B, Tq, H, dq = q.shape
    dv = v.shape[-1]
    if Tq > Q_BLOCK and Tq % Q_BLOCK == 0:
        nb = Tq // Q_BLOCK
        qb = q.reshape(B, nb, Q_BLOCK, H, dq).transpose(1, 0, 2, 3, 4)
        pb = q_pos.reshape(nb, Q_BLOCK)
        out = lax.map(lambda a: attend(a[0], a[1]), (qb, pb))
        return out.transpose(1, 0, 2, 3, 4).reshape(B, Tq, H, dv)
    return attend(q, q_pos)

def _mla(c_q, c_kv, k_rope_raw, pos_new, past_latent, past_krope, pos_past,
         g_q_lat, w_uq, g_kv_lat, w_uk, w_uv, g_qk_q, g_qk_k):
    B, T, _ = c_q.shape
    latent_new = _rmsnorm(c_kv, g_kv_lat)
    q = jnp.einsum('btr,rhd->bthd', _rmsnorm(c_q, g_q_lat), w_uq)
    q = _rmsnorm(q, g_qk_q)
    q = jnp.concatenate([q[..., :QK_NOPE], _rope(q[..., QK_NOPE:], pos_new)], axis=-1)
    latent = jnp.concatenate([past_latent.astype(latent_new.dtype), latent_new], axis=1)
    krope = jnp.concatenate([past_krope.astype(k_rope_raw.dtype), k_rope_raw], axis=1)
    pos_k = jnp.concatenate([pos_past, pos_new])
    S = latent.shape[1]
    k_nope = jnp.einsum('bsc,chd->bshd', latent, w_uk)
    v = jnp.einsum('bsc,chd->bshd', latent, w_uv)
    k = jnp.concatenate([k_nope, jnp.broadcast_to(krope[:, :, None, :], (B, S, MLA_HEADS, QK_ROPE))], axis=-1)
    k = _rmsnorm(k, g_qk_k)
    k = jnp.concatenate([k[..., :QK_NOPE], _rope(k[..., QK_NOPE:], pos_k)], axis=-1)
    o = _causal_attend(q, k, v, pos_new, pos_k, QK_HEAD ** -0.5)
    return o.reshape(B, T, MLA_OUT), latent_new

def _gla_scan(q, k, v, log_a, s0):
    B, T, H, DK = q.shape
    DV = v.shape[-1]
    C = min(GLA_CHUNK, T)
    n = -(-T // C)
    pad = n * C - T

    def chunks(a):
        a = jnp.pad(a.astype(jnp.float32), ((0, 0), (0, pad), (0, 0), (0, 0)))
        return a.reshape(B, n, C, H, a.shape[-1]).transpose(1, 0, 3, 2, 4)

    causal = jnp.tril(jnp.ones((C, C), dtype=bool))

    def step(S, inp):
        qc, kc, vc, ac = inp
        b = jnp.cumsum(ac, axis=2)
        b_last = b[:, :, -1:, :]
        q_dec = qc * jnp.exp(b)
        k_dec = kc * jnp.exp(-b)
        att = jnp.where(causal, jnp.einsum('bhtk,bhsk->bhts', q_dec, k_dec), 0.0)
        o = jnp.einsum('bhts,bhsv->bhtv', att, vc) + jnp.einsum('bhtk,bhkv->bhtv', q_dec, S)
        S = jnp.exp(b_last[:, :, 0, :])[..., None] * S + jnp.einsum('bhsk,bhsv->bhkv', kc * jnp.exp(b_last - b), vc)
        return S, o

    s_fin, o = lax.scan(step, s0.astype(jnp.float32), (chunks(q), chunks(k), chunks(v), chunks(log_a)))
    o = o.transpose(1, 0, 3, 2, 4).reshape(B, n * C, H, DV)[:, :T]
    return o, s_fin

def _gla(gq, gk, gv, g_low, g_r, s0, w_gate_up, b_gate, g_gla_out):
    B, T, _ = gq.shape
    q = gq.reshape(B, T, GLA_HEADS, GLA_DK) * (GLA_DK ** -0.5)
    k = gk.reshape(B, T, GLA_HEADS, GLA_DK)
    v = gv.reshape(B, T, GLA_HEADS, GLA_DV)
    log_a = jax.nn.log_sigmoid((g_low @ w_gate_up + b_gate).astype(jnp.float32)) / GLA_TAU
    log_a = log_a.reshape(B, T, GLA_HEADS, GLA_DK)
    o, s_new = _gla_scan(q, k, v, log_a, s0)
    o = _rmsnorm(o.astype(gv.dtype), g_gla_out).reshape(B, T, GLA_OUT)
    return o * jax.nn.silu(g_r), s_new

def _pool_mix(u_ext, n_prev, start_pos, w_pool, pool_scale):
    B, L, W = u_ext.shape
    T = L - n_prev
    cs = jnp.cumsum(u_ext.astype(jnp.float32), axis=1)
    cs = jnp.concatenate([jnp.zeros((B, 1, W), jnp.float32), cs], axis=1)
    hi = n_prev + jnp.arange(T) + 1
    pos = start_pos + jnp.arange(T)
    u_new = u_ext[:, n_prev:].astype(jnp.float32)
    outs = []
    for gi, w in enumerate(POOL_WINDOWS):
        lo = jnp.maximum(hi - w, 0)
        c0, c1 = gi * POOL_GROUP, (gi + 1) * POOL_GROUP
        s = cs[:, hi, c0:c1] - cs[:, lo, c0:c1]
        cnt = jnp.minimum(w, pos + 1).astype(jnp.float32)
        outs.append(s / cnt[None, :, None] - u_new[:, :, c0:c1])
    pooled = jnp.stack(outs, axis=2)
    y = jnp.einsum('btgc,gcd->btgd', pooled, w_pool.astype(jnp.float32)).reshape(B, T, POOL_WIDTH)
    return (y * pool_scale.astype(jnp.float32)).astype(u_ext.dtype)

def _memory_kv(mem, norm_mem, w_xk, w_xv, g_xk):
    B, N, _ = mem.shape
    m = _rmsnorm(mem, norm_mem)
    k = _rmsnorm((m @ w_xk).reshape(B, N, XA_HEADS, XA_HEAD), g_xk)
    v = (m @ w_xv).reshape(B, N, XA_HEADS, XA_HEAD)
    return k, v

def _cross_attend(h, mem_k, mem_v, w_xq, g_xq, w_xo):
    B, T, _ = h.shape
    q = _rmsnorm((h @ w_xq).reshape(B, T, XA_HEADS, XA_HEAD), g_xq)
    s = jnp.einsum('bthd,bnhd->bhtn', q, mem_k, preferred_element_type=jnp.float32) * (XA_HEAD ** -0.5)
    p = jax.nn.softmax(s, axis=-1).astype(mem_v.dtype)
    o = jnp.einsum('bhtn,bnhd->bthd', p, mem_v)
    return o.reshape(B, T, XA_HEADS * XA_HEAD) @ w_xo

def _layer(x, mem_k, mem_v, pos_new, past_latent, past_krope, pos_past, gla_s0, pool_buf, start_pos, lw):
    (norm_mix, w_in, g_q_lat, w_uq, g_kv_lat, w_uk, w_uv, g_qk_q, g_qk_k,
     w_gate_up, b_gate, g_gla_out, w_pool, pool_scale, w_out,
     norm_xa, w_xq, g_xq, w_xo, norm_mlp, w_ff1, w_ff2) = lw
    h = _rmsnorm(x, norm_mix)
    c_q, c_kv, k_rope, gq, gk, gv, g_low, g_r, u = _split_in(h @ w_in)
    mla_o, latent_new = _mla(c_q, c_kv, k_rope, pos_new, past_latent, past_krope, pos_past,
                             g_q_lat, w_uq, g_kv_lat, w_uk, w_uv, g_qk_q, g_qk_k)
    gla_o, gla_s = _gla(gq, gk, gv, g_low, g_r, gla_s0, w_gate_up, b_gate, g_gla_out)
    u_ext = jnp.concatenate([pool_buf.astype(u.dtype), u], axis=1)
    pool_o = _pool_mix(u_ext, pool_buf.shape[1], start_pos, w_pool, pool_scale)
    mix = jnp.concatenate([mla_o, gla_o.astype(mla_o.dtype), pool_o.astype(mla_o.dtype)], axis=-1)
    x = x + mix @ w_out
    x = x + _cross_attend(_rmsnorm(x, norm_xa), mem_k, mem_v, w_xq, g_xq, w_xo)
    hm = _rmsnorm(x, norm_mlp)
    x = x + jnp.square(jax.nn.relu(hm @ w_ff1)) @ w_ff2
    return x, latent_new, k_rope, gla_s, u_ext[:, -POOL_BUF:]

def setup_inputs(seed: int = 0) -> dict:
    key = jax.random.key(seed)
    ks = iter(jax.random.split(key, 64))
    f32 = jnp.float32

    def nrm(shape, scale=1.0):
        return jax.random.normal(next(ks), shape, f32) * scale

    def gain(shape):
        return 1.0 + 0.02 * jax.random.normal(next(ks), shape, f32)

    n_pages = PAST_LEN // PAGE_SIZE
    n_phys = (DEC_BATCH * n_pages * 5) // 4
    page_table = jax.random.permutation(next(ks), n_phys)[: DEC_BATCH * n_pages].reshape(DEC_BATCH, n_pages).astype(jnp.int32)
    inputs = {
        'x_prompt': nrm((BATCH, SEQ, D_MODEL)),
        'x_sample': nrm((DEC_BATCH, DEC_SEQ, D_MODEL)),
        'mem_prompt': nrm((BATCH, N_MEM, D_MODEL)),
        'cache_mla_latent': nrm((n_phys, DEPTH, PAGE_SIZE, KV_RANK)),
        'cache_mla_krope': nrm((n_phys, DEPTH, PAGE_SIZE, QK_ROPE)),
        'state_gla': nrm((DEC_BATCH, DEPTH, GLA_HEADS, GLA_DK, GLA_DV)),
        'state_pool': nrm((DEC_BATCH, DEPTH, POOL_BUF, POOL_WIDTH)),
        'cache_mem_k': nrm((DEC_BATCH, DEPTH, N_MEM, XA_HEADS, XA_HEAD)),
        'cache_mem_v': nrm((DEC_BATCH, DEPTH, N_MEM, XA_HEADS, XA_HEAD)),
        'page_table': page_table,
        'norm_mix': gain((DEPTH, D_MODEL)),
        'w_in': nrm((DEPTH, D_MODEL, D_IN), D_MODEL ** -0.5),
        'g_q_lat': gain((DEPTH, Q_RANK)),
        'w_uq': nrm((DEPTH, Q_RANK, MLA_HEADS, QK_HEAD), Q_RANK ** -0.5),
        'g_kv_lat': gain((DEPTH, KV_RANK)),
        'w_uk': nrm((DEPTH, KV_RANK, MLA_HEADS, QK_NOPE), KV_RANK ** -0.5),
        'w_uv': nrm((DEPTH, KV_RANK, MLA_HEADS, V_HEAD), KV_RANK ** -0.5),
        'g_qk_q': gain((DEPTH, QK_HEAD)),
        'g_qk_k': gain((DEPTH, QK_HEAD)),
        'w_gate_up': nrm((DEPTH, GLA_GATE_RANK, GLA_HEADS * GLA_DK), GLA_GATE_RANK ** -0.5),
        'b_gate': nrm((DEPTH, GLA_HEADS * GLA_DK), 0.1),
        'g_gla_out': gain((DEPTH, GLA_DV)),
        'w_pool': nrm((DEPTH, len(POOL_WINDOWS), POOL_GROUP, POOL_GROUP), POOL_GROUP ** -0.5),
        'pool_scale': gain((DEPTH, POOL_WIDTH)),
        'w_out': nrm((DEPTH, D_MIX, D_MODEL), D_MIX ** -0.5),
        'norm_xa': gain((DEPTH, D_MODEL)),
        'norm_mem': gain((DEPTH, D_MODEL)),
        'w_xq': nrm((DEPTH, D_MODEL, D_MODEL), D_MODEL ** -0.5),
        'w_xk': nrm((DEPTH, D_MODEL, D_MODEL), D_MODEL ** -0.5),
        'w_xv': nrm((DEPTH, D_MODEL, D_MODEL), D_MODEL ** -0.5),
        'g_xq': gain((DEPTH, XA_HEAD)),
        'g_xk': gain((DEPTH, XA_HEAD)),
        'w_xo': nrm((DEPTH, D_MODEL, D_MODEL), D_MODEL ** -0.5),
        'norm_mlp': gain((DEPTH, D_MODEL)),
        'w_ff1': nrm((DEPTH, D_MODEL, D_FF), D_MODEL ** -0.5),
        'w_ff2': nrm((DEPTH, D_FF, D_MODEL), D_FF ** -0.5),
    }
    return inputs

def reference(x_prompt, x_sample, mem_prompt, cache_mla_latent, cache_mla_krope, state_gla, state_pool,
              cache_mem_k, cache_mem_v, page_table, norm_mix, w_in, g_q_lat, w_uq, g_kv_lat, w_uk, w_uv,
              g_qk_q, g_qk_k, w_gate_up, b_gate, g_gla_out, w_pool, pool_scale, w_out, norm_xa, norm_mem,
              w_xq, w_xk, w_xv, g_xq, g_xk, w_xo, norm_mlp, w_ff1, w_ff2):
    n_prompt, seq, _ = x_prompt.shape
    n_dec, dec_seq, _ = x_sample.shape
    n_pages = page_table.shape[1]
    past = n_pages * PAGE_SIZE
    dt = x_prompt.dtype
    pos_prompt = jnp.arange(seq, dtype=jnp.int32)
    pos_sample = past + jnp.arange(dec_seq, dtype=jnp.int32)
    pos_past = jnp.arange(past, dtype=jnp.int32)
    no_pos = jnp.zeros((0,), jnp.int32)
    no_latent = jnp.zeros((n_prompt, 0, KV_RANK), dt)
    no_krope = jnp.zeros((n_prompt, 0, QK_ROPE), dt)
    no_buf = jnp.zeros((n_prompt, 0, POOL_WIDTH), dt)
    gla_zero = jnp.zeros((n_prompt, GLA_HEADS, GLA_DK, GLA_DV), jnp.float32)
    y_p, y_s = x_prompt, x_sample
    p_lat, p_rope, p_gla, p_pool, p_mk, p_mv = [], [], [], [], [], []
    s_lat, s_rope, s_gla, s_pool = [], [], [], []
    for l in range(DEPTH):
        lw = (norm_mix[l], w_in[l], g_q_lat[l], w_uq[l], g_kv_lat[l], w_uk[l], w_uv[l], g_qk_q[l], g_qk_k[l],
              w_gate_up[l], b_gate[l], g_gla_out[l], w_pool[l], pool_scale[l], w_out[l],
              norm_xa[l], w_xq[l], g_xq[l], w_xo[l], norm_mlp[l], w_ff1[l], w_ff2[l])
        mk, mv = _memory_kv(mem_prompt, norm_mem[l], w_xk[l], w_xv[l], g_xk[l])
        y_p, lat, kr, gs, buf = _layer(y_p, mk, mv, pos_prompt, no_latent, no_krope, no_pos, gla_zero, no_buf, 0, lw)
        p_lat.append(lat)
        p_rope.append(kr)
        p_gla.append(gs)
        p_pool.append(buf)
        p_mk.append(mk)
        p_mv.append(mv)
        past_lat = cache_mla_latent[page_table, l].reshape(n_dec, past, KV_RANK)
        past_kr = cache_mla_krope[page_table, l].reshape(n_dec, past, QK_ROPE)
        y_s, lat, kr, gs, buf = _layer(y_s, cache_mem_k[:, l], cache_mem_v[:, l], pos_sample, past_lat, past_kr,
                                       pos_past, state_gla[:, l], state_pool[:, l], past, lw)
        s_lat.append(lat)
        s_rope.append(kr)
        s_gla.append(gs)
        s_pool.append(buf)
    return (y_p, y_s,
            jnp.stack(p_lat, axis=1), jnp.stack(p_rope, axis=1), jnp.stack(p_gla, axis=1), jnp.stack(p_pool, axis=1),
            jnp.stack(p_mk, axis=1), jnp.stack(p_mv, axis=1),
            jnp.stack(s_lat, axis=1), jnp.stack(s_rope, axis=1), jnp.stack(s_gla, axis=1), jnp.stack(s_pool, axis=1))


_drawn_inputs = setup_inputs


def setup_inputs(seed=0):
    import zlib

    import numpy as np

    out = dict(_drawn_inputs(seed))
    spreads = {}
    factors = {'cache_mla_krope': 3.694,
     'g_q_lat': 8.0,
     'g_kv_lat': 2.987,
     'g_qk_q': 8.0,
     'g_qk_k': 8.0,
     'g_gla_out': 7.63,
     'pool_scale': 5.452,
     'norm_xa': 8.0,
     'norm_mem': 2.901,
     'g_xq': 8.0}
    for name, (base, spread) in spreads.items():
        noise = np.random.default_rng([zlib.crc32(name.encode()), seed]).standard_normal(out[name].shape)
        drawn = base * np.exp(spread * noise) if base else spread * noise
        out[name] = jnp.asarray(drawn.astype(out[name].dtype))
    for name, factor in factors.items():
        out[name] = (out[name] * factor).astype(out[name].dtype)
    return out
```

```python
import concourse.bass as bass
from concourse import mybir
from contextlib import ExitStack

FP32 = mybir.dt.float32
ALU = mybir.AluOpType
ACT = mybir.ActivationFunctionType
AXX = mybir.AxisListType.X
DEPTH, D, P = 2, 1024, 128
KD = D // P
TP, B = 256, 8
T = TP + B
H = 4
NOPE, ROPE = 64, 32
QK = NOPE + ROPE
PG, PAGES = 128, 16
S_PAGES = PAGES + 1
NM = 256
EPS = 1e-6
NEG = -1e30
SLOTS = 4
UNIT = 2048
U_IN, U_MK, U_MV, U_OUT, U_XQ, U_XK, U_XV, U_XO, U_FF1, U_FF2 = 8, 4, 4, 4, 4, 8, 8, 4, 16, 16
UNITS = U_IN + U_MK + U_MV + U_OUT + U_XQ + U_XK + U_XV + U_XO + U_FF1 + U_FF2
CQ, CKV, KR, GQ, GK, GV, GLOW, GR, UU, NZ = 0, 3, 5, 6, 7, 8, 10, 11, 13, 15
G_MIX, G_XA, G_MLP, G_MEM, G_QL, G_KV, G_Q, G_K, G_KR4, B_GATE, G_GLA, G_POOL, G_XQ, G_XK, NG = \
    0, 8, 16, 24, 32, 35, 37, 38, 39, 40, 41, 42, 44, 46, 48
M_UQ, M_UK, M_UV, M_UKT, M_GATE, M_POOL, NMAT = 0, 1152, 1664, 2688, 3712, 3840, 4096
C_ID, C_MASK, C_B64, C_REP, C_SWAP, C_SWAP4, C_COS, C_SIN, C_COS4, C_SIN4, C_HM, C_BM, C_TRI, C_INV, NC = \
    0, 128, 512, 640, 768, 896, 1024, 1288, 1552, 2064, 2576, 2580, 2836, 3092, 3620


class Count:

    def __init__(self, sem, per_layer, start):
        self.sem, self.per_layer, self.start = sem, per_layer, start
        self.base, self.n, self.done = start, 0, 0

    def next(self, k=1):
        self.n += k
        return self.base + self.n

    def free(self, k=1):
        return self.next(k) - self.start

    @property
    def slot(self):
        return (self.done + self.n - 1) % 4


class Counts:

    def __init__(self, sems, table):
        self.all = {name: Count(sems[name], *table[name]) for name in table}

    def __getitem__(self, name):
        return self.all[name]

    def layer(self, l):
        for c in self.all.values():
            c.base, c.n, c.done = l * c.per_layer + c.start, 0, 0

    def end_layer(self):
        for name, c in self.all.items():
            assert c.n in (0, c.per_layer), (name, c.n, c.per_layer)

    def enter(self, i, **per):
        self.kept = {name: (c.base, c.n) for name, c in self.all.items()}
        self.per = per
        for name, k in per.items():
            c = self.all[name]
            c.base, c.done, c.n = c.base + c.n + i * k, c.n, 0

    def leave(self, times):
        for name, c in self.all.items():
            base, n = self.kept[name]
            if name in self.per:
                assert c.n == self.per[name], (name, c.n, self.per[name])
                c.base, c.n, c.done = base, n + times * self.per[name], 0
            else:
                assert c.n == n, name


TILES, MOMENTS = 212, 10 + B
SIGNALS = dict(
    tile_ready=(TILES, 0),
    unit_used=(UNITS, SLOTS),
    pair_ready=(64, 8),
    mean_ready=(3, 0),
    x_sq=(3, 0), lat_sq=(1, 0), qk_sq=(2, 0), gla_sq=(1, 0), mem_sq=(1, 0), km_sq=(1, 0), xq_sq=(1, 0),
    kr_sq=(B, 1), pair_sq=(64, 2), ff_done=(32, 4),
    root=(MOMENTS, 0),
    gate_soft=(1, 0), gate_exp=(1, 0), soft_exp=(1, 0), dec_exp=(B, 0), x_exp=(1, 0), xs_exp=(1, 0),
    tile_free=(TILES, 4),
    lat_used=(B, 2),
    pair_sc=(64, 2), pair_sum=(64, 2),
    moment=(MOMENTS, 0),
    x_new=(3, 1), xg_ready=(24, 0), ssum_ready=(4, 0),
    z_ready=(15, 0), lat_ready=(1, 0), qk_raw=(2, 0), qk_norm=(1, 0), qk_ready=(1, 0), small_ready=(1, 0), vp_ready=(1, 0),
    soft_in=(1, 0), soft_p=(1, 0), soft_t=(1, 0), mla_done=(1, 0),
    gate_in=(1, 0), gate_la=(1, 0), gate_dec=(1, 0), gla_nat=(1, 0), gvs_ready=(1, 0), gla_state=(1, 0), gla_raw=(1, 0),
    mix_side=(1, 0), seq_in=(B, 0), kr_scaled=(B, 1), kr_rot=(B, 0), dec_max=(B, 0), dec_in=(B, 0), dec_sum=(B, 0),
    dec_out=(1, 0), mg_ready=(1, 0), mix_ready=(1, 0), km_raw=(1, 0), km_ready=(1, 0),
    xq_raw=(1, 0), xq_ready=(1, 0), x_in=(1, 0), x_p=(1, 0), x_t=(1, 0), xs_max=(1, 0), xs_in=(1, 0), xs_sum=(1, 0), xo_ready=(1, 0),
    ff_in=(32, 0),
    pooled_ready=(1, 0), dec_amax=(B, 0), xs_amax=(1, 0),
)
POOL_STEPS, ACT_STEPS, DVE_STEPS, DEC_STEPS = 16, 20, 300, 38


def decoder(nc, units, xt, memt, pages, krope, table, gains, mats, consts, gstate, pstate, pstate_nat,
            o_y, o_lat, o_kr, o_glap, o_glas, o_u, o_pool, o_mk, o_mv, gvs):
    ctx = ExitStack()
    with ctx:
        def sb(name, shape, dt=FP32):
            return ctx.enter_context(nc.sbuf_tensor(name, shape, dt))

        def sem(name):
            return ctx.enter_context(nc.semaphore(name))

        ring = sb("ring", [P, SLOTS, UNIT])
        xT = sb("xT", [P, KD, T])
        xg = sb("xg", [P, KD, T])
        sq = sb("sq", [P, KD, T])
        rB = sb("rB", [P, T])
        z = sb("z", [P, NZ, T])
        qkA = sb("qkA", [P, 8, T])
        qkB = sb("qkB", [P, 8, T])
        mix = sb("mix", [P, KD, T])
        mat = sb("mat", [P, NMAT])
        con = sb("con", [P, NC])
        gall = sb("gall", [P, DEPTH, NG])
        gain = sb("gain", [P, NG])
        ones = sb("ones", [P, P])
        latT = sb("latT", [P, PAGES, 256])
        big = sb("big", [P, 34 * T])
        krT = sb("krT", [P, 4, PG])
        krQ = sb("krQ", [P, 4, PG])
        gvs_n = sb("gvs_n", [B, 256])
        m = sb("m", [P, 4 * T])
        y = sb("y", [P, 4 * T])
        tmp = sb("tmp", [P, 4 * T])
        rBm = sb("rBm", [P, NM + 2])
        wuq_b = sb("wuq_b", [P, 2, 2, 260])
        qt = sb("qt", [P, 2, B, H])
        qblk = sb("qblk", [P, B, 4, H])
        snew = sb("snew", [1, H, B])
        ssn = sb("ssn", [P, PAGES, H])
        ssr = sb("ssr", [P, PAGES])
        sc = sb("sc", [P, S_PAGES, H])
        pr = sb("pr", [P, S_PAGES, H])
        mxp = sb("mxp", [P, 32])
        mx = sb("mx", [P, 32])
        rs = sb("rs", [P, 32])
        den = sb("den", [P, 32])
        olat = sb("olat", [P, 2, B, H])
        qg = sb("qg", [NOPE, H, B])
        qbs = sb("qbs", [P, 2, 16])
        sprod = sb("sprod", [QK, H, B])
        ptab = sb("ptab", [1, B * PAGES], mybir.dt.int32)
        nmx = sb("nmx", [P, H, 2])
        psum_p = sb("psum_p", [P, H, 2])
        bl = sb("bl", [P, 4])
        ea = sb("ea", [P, B])
        qsb = sb("qsb", [P, B, H])
        xs = sb("xs", [P, B, 2, H])
        ue = sb("ue", [P, 2, 400])

        ps = ctx.enter_context(nc.psum_tensor("ps", [P, 8, 512], FP32))


        def within(t, at, *shape):
            names = "abc"[:len(shape)]
            n = 1
            for k in shape:
                n *= k
            v = t[:, at:at + n]
            return v.rearrange(f"p ({' '.join(names)}) -> p {' '.join(names)}", **dict(zip(names, shape)))

        sq_f, qkA_f, qkB_f = (v[:, :, :].rearrange("p k t -> p (k t)") for v in (sq, qkA, qkB))
        latT_f = latT[:, :, :].rearrange("p g c -> p (g c)")
        lat = within(big, 0, 2, PAGES, 256)
        ffh = within(big, 0, 32, T)
        gvn, S, vb, gst, kendn, pooled = (within(big, 4096, 4, 256), within(big, 5120, 4, 256), within(big, 6144, B, 64),
                                          within(big, 6656, B, 64), within(big, 7168, 4, P), within(big, 7680, 2, T))
        kmT, vm = within(latT_f, 0, 8, NM), within(latT_f, 2048, 2, D)
        kraw = within(qkA_f, 0, 8, NM)
        vp = within(m, 0, 2, 512)
        sS, pT = within(sq_f, 0, 4, 384), within(qkA_f, 0, 4, 384)
        qbd, att = within(y, 0, 4, TP), within(qkA_f, 0, 4, 256)
        psq = within(qkA_f, 0, 2, 512)
        krS, krC = within(qkB_f, 0, 4, PG), within(qkB_f, 512, 4, PG)
        wa, wb = within(qkB_f, 0, 2, 400), within(qkB_f, 800, 2, 400)
        xS, xP = within(qkA_f, 0, 4, 2, NM), within(qkB_f, 0, 4, 2, NM)
        mg = xg
        L_BC, L_EB, L_ENB, L_EKE, L_QD, L_KD, L_KE, L_A = range(8)
        ident, swap, swap4, b64, rep = (con[:, c:c + P] for c in (C_ID, C_SWAP, C_SWAP4, C_B64, C_REP))
        hm = con[:, C_HM:C_HM + 4]
        cos, sin = con[0:QK, C_COS:C_COS + T], con[0:QK, C_SIN:C_SIN + T]
        w_uq = within(mat, M_UQ, 3, H, QK)
        w_uk, w_uv, w_ukt, w_pool = (within(mat, c, n, k) for c, n, k in
                                     ((M_UK, 2, 256), (M_UV, 2, 512), (M_UKT, 4, 256), (M_POOL, 2, P)))

        sems = {name: sem(name) for name in SIGNALS}
        dve_step, act_step, pool_step = sem("dve_step"), sem("act_own"), sem("pool_step")
        unit_in = [sem(f"unit_in{s}") for s in range(SLOTS)]
        lt_in = [sem(f"lt_in{g}") for g in range(4)]
        lat_in = [sem(f"lat_in{s}") for s in range(2)]
        STORES = 7
        kr_in, once_in, layer_in, mg_in = (sem(n) for n in ("kr_in", "once_in", "layer_in", "mg_in"))
        y_out = sem("y_out")
        passed = {e: sem(f"passed_{e}") for e in ("pool", "sp", "pe", "dve")}
        stored, copied, gvs_out, gvs_in, tab_in = (sem(n) for n in ("stored", "copied", "gvs_out", "gvs_in", "tab_in"))
        block = ctx.enter_context(nc.Block())

        @block.sync
        def _(sp):
            at = Counts(sems, SIGNALS)
            sp.dma_start(ptab[:, :], table).then_inc(tab_in, 16)
            sp.wait_ge(tab_in, 16)
            with sp.Fori(0, DEPTH) as l:
                at.layer(l)

                def load_units(n):
                    first = at["unit_used"].n
                    with sp.Fori(0, n // SLOTS) as i:
                        at.enter(i, unit_used=SLOTS)
                        for s in range(SLOTS):
                            sp.wait_ge(sems["unit_used"], at["unit_used"].free())
                            sp.dma_start(ring[:, s, :], units[bass.ds(l * UNITS + first + i * SLOTS + s, 1), :, :]
                                         .rearrange("a p n -> p (a n)")).then_inc(unit_in[s], 16)
                    at.leave(n // SLOTS)

                load_units(U_IN)
                sp.wait_ge(sems["x_new"], 3 * l + 1)
                sp.sem_inc(passed["sp"], 1)
                with sp.Fori(0, B // 2) as i:
                    at.enter(i, pair_ready=PAGES, lat_used=2)
                    for s in range(2):
                        for pg in range(PAGES):
                            page = sp.value_load(ptab[0:1, bass.ds(i * 2 * PAGES + s * PAGES + pg, 1)],
                                                 min_val=0, max_val=pages.shape[0] // DEPTH - 1)
                            src = pages[bass.ds(page * DEPTH + l, 1), :, :].rearrange("a p n -> p (a n)")
                            if pg % 2 == 0:
                                sp.wait_ge(sems["pair_ready"], at["pair_ready"].free())
                            sp.dma_start(latT[:, pg, :], src[:, 0:256]).then_inc(lt_in[pg // 4], 16)
                            if pg == 0:
                                sp.wait_ge(sems["lat_used"], at["lat_used"].free())
                                sp.sem_inc(passed["sp"], 1)
                                if s == 1:
                                    sp.wait_ge(sems["mix_side"], l + 1)
                                    sp.wait_ge(stored, 16 * (STORES * l + 5))
                            sp.dma_start(lat[:, s, pg, :], src[:, 256:512]).then_inc(lat_in[s], 16)
                at.leave(B // 2)
                load_units(UNITS - U_IN)
                at.end_layer()
            sp.wait_ge(sems["x_new"], 3 * DEPTH + 1)
            sp.dma_start(o_y, xT[:, :, :]).then_inc(y_out, 16)
            sp.wait_ge(y_out, 16)

        @block.gpsimd
        def _(pool):
            at = Counts(sems, SIGNALS)
            steps = [0]

            def wait_ge(semaphore, value):
                pool.wait_ge(semaphore, value)
                pool.sem_inc(passed["pool"], 1)

            def step(ins):
                ins.then_inc(pool_step, 1)
                steps[0] += 1
                wait_ge(pool_step, at_step(steps[0]))

            at_step = lambda n: n
            step(pool.memset(ones[:, :], 1.0))
            step(pool.memset(ue[:, :, 0:16], 0.0))
            STEP0 = steps[0]
            pool.dma_start(xT[:, :, :], xt).then_inc(once_in, 16)
            pool.dma_start(con[:, :], consts).then_inc(once_in, 16)
            pool.dma_start(gall[:, :, :], gains).then_inc(once_in, 16)
            with pool.Fori(0, DEPTH) as l:
                at.layer(l)
                steps[0] = 0
                at_step = lambda n: STEP0 + l * POOL_STEPS + n
                wait_ge(sems["x_new"], 3 * l + 1)
                pool.dma_start(mat[:, :], mats[bass.ds(l, 1), :, :].rearrange("a p n -> p (a n)")).then_inc(layer_in, 16)
                pool.dma_start(gst[:, :, :], gstate[bass.ds(l, 1), :, :, :].rearrange("a p b v -> p (a b) v")).then_inc(layer_in, 16)
                for c in range(2):
                    pool.dma_start(ue[:, c, 272:400].rearrange("p (b j) -> p b j", b=B)[:, :, 0:15],
                                   pstate[bass.ds(l, 1), :, c, :, :].rearrange("a p b j -> p (a b) j")).then_inc(layer_in, 16)
                pool.dma_start(o_pool[bass.ds(l, 1), :, :, :].rearrange("a b j c -> (a b) j c"),
                               pstate_nat[bass.ds(l, 1), :, :, :].rearrange("a b j c -> (a b) j c")).then_inc(copied, 16)

                wait_ge(sems["z_ready"], 15 * l + 15)
                wait_ge(layer_in, 64 * (l + 1))
                step(pool.tensor_copy(ue[:, :, 16:272], z[:, UU:UU + 2, 0:TP]))
                step(pool.tensor_copy(ue[:, :, 272:400].rearrange("p c (b j) -> p c b j", b=B)[:, :, :, 15],
                                      z[:, UU:UU + 2, TP:T]))
                wait_ge(sems["mla_done"], l + 1)
                step(pool.tensor_tensor(wa[:, :, 1:400], ue[:, :, 1:400], ue[:, :, 0:399], ALU.add))
                src = wa
                for g, w in enumerate((2, 4, 8, 16)):
                    c, r = g // 2, 64 * (g % 2)
                    if g:
                        dst = wb if src is wa else wa
                        step(pool.tensor_tensor(dst[:, :, w - 1:400], src[:, :, w - 1:400],
                                                src[:, :, w // 2 - 1:400 - w // 2], ALU.add))
                        src = dst
                    step(pool.tensor_copy(pooled[r:r + 64, c, 0:TP], src[r:r + 64, c, 16:272]))
                    step(pool.tensor_copy(pooled[r:r + 64, c, TP:T],
                                          src[r:r + 64, c, 272:400].rearrange("p (b j) -> p b j", b=B)[:, :, 15]))
                inv = con[:, C_INV:C_INV + 2 * T].rearrange("p (c t) -> p c t", c=2)
                step(pool.tensor_tensor(pooled[:, :, :], pooled[:, :, :], inv, ALU.mult))
                step(pool.tensor_tensor(pooled[:, :, :], pooled[:, :, :], z[:, UU:UU + 2, :], ALU.subtract))
                pool.sem_inc(sems["pooled_ready"], 1)

                wait_ge(sems["gvs_ready"], l + 1)
                pool.dma_start(gvs, gvs_n[:, :]).then_inc(gvs_out, 16)
                wait_ge(gvs_out, 16 * (l + 1))
                for h in range(H):
                    pool.dma_start(vb[32 * h:32 * h + 32, :, :],
                                   gvs[:, 64 * h:64 * h + 64].unsqueeze(0).broadcast_to([32, B, 64])).then_inc(gvs_in, 16)

                wait_ge(sems["mix_side"], l + 1)
                pool.dma_start(mg[:, :, 0:NM], memt).then_inc(mg_in, 16)
                with pool.Fori(0, B) as b:
                    at.enter(b, kr_sq=1, kr_scaled=1, dec_max=1)
                    wait_ge(sems["kr_sq"], at["kr_sq"].free())
                    wait_ge(sems["kr_scaled"], at["kr_scaled"].free())
                    for pg in range(PAGES):
                        page = pool.value_load(ptab[0:1, bass.ds(b * PAGES + pg, 1)], min_val=0,
                                               max_val=pages.shape[0] // DEPTH - 1)
                        pool.dma_start(krT[32 * (pg % 4):32 * (pg % 4) + 32, pg // 4, :],
                                       krope[bass.ds(page * DEPTH + l, 1), :, :].rearrange("a p n -> p (a n)")).then_inc(kr_in, 16)
                    wait_ge(sems["dec_max"], at["dec_max"].next())
                    pool.partition_all_reduce(mx[:, 0:4], mxp[:, 0:4], P, bass.bass_isa.ReduceOp.max).then_inc(sems["dec_amax"], 1)
                at.leave(B)
                wait_ge(sems["xs_max"], l + 1)
                pool.partition_all_reduce(mx[:, :], mxp[:, :], P, bass.bass_isa.ReduceOp.max).then_inc(sems["xs_amax"], 1)
                assert steps[0] == POOL_STEPS, steps
            wait_ge(copied, 16 * DEPTH)

        @block.scalar
        def _(act):
            at = Counts(sems, SIGNALS)
            act.preload_act_table_set("natural_log_exp_and_others")
            own = Count(act_step, ACT_STEPS, 0)

            def f(out, in_, func, **kw):
                return nc.scalar.activation(out, in_, func, **kw)

            def step(ins):
                ins.then_inc(act_step, 1)
                act.wait_ge(act_step, own.next())

            def power(rows, cols):
                act.wait_ge(sems["moment"], at["moment"].next())
                step(f(y[0:rows, 0:cols], m[0:rows, 0:cols], ACT.Ln))
                f(y[0:rows, 0:cols], y[0:rows, 0:cols], ACT.Exp, scale=-0.5).then_inc(sems["root"], 1)
                at["root"].next()

            def square_x():
                act.wait_ge(sems["x_new"], at["x_new"].free())
                f(sq[:, :, :], xT[:, :, :], ACT.Square).then_inc(sems["x_sq"], 1)
                power(P, T)

            act.sem_inc(sems["pair_sq"], 2)
            act.sem_inc(sems["kr_sq"], 1)
            act.sem_inc(sems["ff_done"], 4)
            with act.Fori(0, DEPTH) as l:
                at.layer(l)
                own.base, own.n = l * ACT_STEPS, 0
                square_x()
                act.wait_ge(sems["z_ready"], 15 * l + 15)
                f(xg[:, 0:5, :], z[:, 0:5, :], ACT.Square).then_inc(sems["lat_sq"], 1)
                power(P, 2 * T)
                act.wait_ge(sems["lat_ready"], l + 1)
                act.dma_start(o_lat[bass.ds(l, 1), :, :, :].rearrange("a p c t -> (a p) c t"), z[:, CKV:CKV + 2, :]).then_inc(stored, 16)
                act.dma_start(o_kr[bass.ds(l, 1), :, :].rearrange("a p t -> (a p) t"), z[NOPE:QK, KR, :]).then_inc(stored, 16)
                act.dma_start(o_u[bass.ds(l, 1), :, :, :].rearrange("a p c t -> (a p) c t"), z[:, UU:UU + 2, :]).then_inc(stored, 16)
                for j in range(2):
                    act.wait_ge(sems["qk_raw"], 2 * l + j + 1)
                    f(sq[0:QK, 4 * j:4 * j + 4, :], qkA[0:QK, 4 * j:4 * j + 4, :], ACT.Square).then_inc(sems["qk_sq"], 1)
                power(QK, 4 * T)
                power(QK, 4 * T)
                act.wait_ge(sems["soft_in"], l + 1)
                for h in range(H):
                    for a, (c0, c1) in enumerate(((0, P), (P, 384))):
                        last = f(sS[:, h, c0:c1], sS[:, h, c0:c1], ACT.Exp, bias=nmx[:, h, a:a + 1],
                                 scale=QK ** -0.5, accum_out=psum_p[:, h, a:a + 1])
                last.then_inc(sems["soft_exp"], 1)
                act.wait_ge(sems["gate_in"], l + 1)
                step(f(y[:, 0:T], m[:, 0:T], ACT.Abs))
                step(f(y[:, 0:T], y[:, 0:T], ACT.Exp, scale=-1.0))
                f(y[:, 0:T], y[:, 0:T], ACT.Ln, bias=1.0).then_inc(sems["gate_soft"], 1)
                act.wait_ge(sems["gate_la"], l + 1)
                f(xg[:, L_EB, 0:TP], xg[:, L_BC, 0:TP], ACT.Exp, scale=1 / 16)
                f(xg[:, L_ENB, 0:TP], xg[:, L_BC, 0:TP], ACT.Exp, scale=-1 / 16)
                for c in range(4):
                    f(xg[:, L_EKE, 64 * c:64 * c + 64], xg[:, L_BC, 64 * c:64 * c + 64], ACT.Exp, bias=bl[:, c:c + 1], scale=-1 / 16)
                f(sq[:, 4:6, :], z[:, GR:GR + 2, :], ACT.Exp, scale=-1.0)
                f(ea[:, :], xg[:, L_A, TP:T], ACT.Exp, scale=1 / 16).then_inc(sems["gate_exp"], 1)
                act.wait_ge(sems["gla_raw"], l + 1)
                f(sq[:, 0:2, :], z[:, GV:GV + 2, :], ACT.Square).then_inc(sems["gla_sq"], 1)
                act.dma_start(o_glap[bass.ds(l, 1), :, :].rearrange("a p n -> (a p) n"), S[:, 3, :]).then_inc(stored, 16)
                act.dma_start(o_glas[bass.ds(l, 1), :, :, :].rearrange("a p b v -> (a p) b v"), gst[:, :, :]).then_inc(stored, 16)
                power(P, 2 * T)

                with act.Fori(0, B // 2) as i:
                    per = dict(pair_ready=16, pair_sum=16, pair_sq=16, moment=2, root=2, dec_in=2, dec_exp=2, kr_sq=2)
                    at.enter(i, **per)
                    base, n = own.base, own.n
                    own.base, own.n = base + n + i * 2, 0
                    for s in range(2):
                        for pair in range(PAGES // 2):
                            act.wait_ge(sems["pair_ready"], at["pair_ready"].next())
                            act.wait_ge(sems["pair_sum"], at["pair_sum"].free())
                            q = pair % 2
                            f(psq[:, q, :].rearrange("p (g c) -> p g c", g=2), ps[:, 4 + 2 * q:6 + 2 * q, 0:256],
                              ACT.Square).then_inc(sems["pair_sq"], 1)
                            at["pair_sq"].next()
                            if pair == 4:
                                act.wait_ge(kr_in, 256 * (l * B + i * 2 + s + 1))
                                f(krQ[:, :, :], krT[:, :, :], ACT.Square).then_inc(sems["kr_sq"], 1)
                                at["kr_sq"].next()
                        power(P, 64)
                        act.wait_ge(sems["dec_in"], at["dec_in"].next())
                        f(pr[:, :, :], sc[:, :, :], ACT.Exp, scale=QK ** -0.5).then_inc(sems["dec_exp"], 1)
                        at["dec_exp"].next()
                    assert own.n == 2
                at.leave(B // 2)
                own.base, own.n = base, n + B

                act.wait_ge(mg_in, 16 * (l + 1))
                f(sq[:, :, 0:NM], mg[:, :, 0:NM], ACT.Square).then_inc(sems["mem_sq"], 1)
                power(P, NM + 2)
                act.wait_ge(sems["km_raw"], l + 1)
                f(sq[:, :, 0:NM], kraw[:, :, :], ACT.Square).then_inc(sems["km_sq"], 1)
                power(P, 4 * NM)
                act.wait_ge(sems["km_ready"], l + 1)
                act.dma_start(o_mk[bass.ds(l, 1), :, :, :].rearrange("a p c n -> (a p) c n"), kmT[:, :, :]).then_inc(stored, 16)
                act.dma_start(o_mv[bass.ds(l, 1), :, :, :].rearrange("a p c n -> (a p) c n"), vm[:, :, :]).then_inc(stored, 16)
                square_x()
                act.wait_ge(sems["xq_raw"], l + 1)
                f(sq[:, :, :], z[:, 0:8, :], ACT.Square).then_inc(sems["xq_sq"], 1)
                power(P, 4 * T)
                act.wait_ge(sems["x_in"], l + 1)
                for h in range(H):
                    for a in range(2):
                        last = f(xS[:, h, a, :], xS[:, h, a, :], ACT.Exp, bias=nmx[:, h, a:a + 1], scale=1 / 16,
                                 accum_out=psum_p[:, h, a:a + 1])
                last.then_inc(sems["x_exp"], 1)
                act.wait_ge(sems["xs_in"], l + 1)
                f(xs[:, :, :, :], xs[:, :, :, :], ACT.Exp, scale=1 / 16).then_inc(sems["xs_exp"], 1)
                square_x()
                with act.Fori(0, U_FF1 // SLOTS) as i:
                    for t in range(8):
                        act.wait_ge(sems["ff_in"], l * 32 + i * 8 + t + 1)
                        f(ffh[:, bass.ds(i * 8 + t, 1), :], y[:, 0:1056].rearrange("p (s t) -> p s t", s=4)[:, t % 4:t % 4 + 1, :],
                          ACT.Square).then_inc(sems["ff_done"], 1)
                assert own.n == ACT_STEPS, own.n
            act.wait_ge(stored, STORES * 16 * DEPTH)

        @block.vector
        def _(dve):
            at = Counts(sems, SIGNALS)
            own = Count(dve_step, DVE_STEPS, 0)
            v = nc.vector

            def step(ins):
                ins.then_inc(dve_step, 1)
                dve.wait_ge(dve_step, own.next())

            def wait(name):
                dve.wait_ge(sems[name], at[name].next())

            def tell(name):
                dve.sem_inc(sems[name], 1)

            def tile():
                wait("tile_ready")
                return ps[:, at["tile_ready"].slot, :]

            def freed(ins):
                ins.then_inc(sems["tile_free"], 1)
                dve.wait_ge(sems["tile_free"], at["tile_free"].next())

            def refine(rows, cols, out=None):
                tell("moment")
                wait("root")
                a, b, c = (t[0:rows, 0:cols] for t in (y, m, tmp))
                step(v.scalar_tensor_tensor(c, a, -0.5, a, ALU.mult, ALU.mult))
                step(v.tensor_tensor(c, c, b, ALU.mult))
                step(v.scalar_tensor_tensor(a if out is None else out, c, 1.5, a, ALU.add, ALU.mult))

            def norm_x(g):
                for k in range(KD):
                    v.tensor_scalar(xg[:, k, :], xT[:, k, :], gain[:, g + k:g + k + 1], None, ALU.mult).then_inc(sems["xg_ready"], 1)
                wait("x_sq")
                step(v.tensor_reduce(tmp[:, 0:T], sq[:, :, :].rearrange("p k t -> p t k"), AXX, ALU.add))
                tell("ssum_ready")
                wait("mean_ready")
                step(v.tensor_scalar(m[:, 0:T], ps[:, 4, 0:T], 1 / D, EPS, ALU.mult, ALU.add))
                refine(P, T, rB[:, :])

            def add_to_x(k):
                freed(v.tensor_tensor(xT[:, k, :], xT[:, k, :], tile()[:, 0:T], ALU.add))

            def soften(S4, width_of, name_in, name_exp):
                for a, (c0, c1) in enumerate(width_of):
                    step(v.tensor_reduce(nmx[:, :, a:a + 1], S4(c0, c1), AXX, ALU.max, negate=True))

            dve.wait_ge(once_in, 48)
            dve.sem_inc(sems["tile_free"], 4)
            dve.sem_inc(sems["pair_sc"], 2)
            dve.sem_inc(sems["pair_sum"], 2)
            dve.sem_inc(sems["kr_scaled"], 1)
            dve.sem_inc(sems["lat_used"], 2)
            dve.sem_inc(sems["x_new"], 1)

            with dve.Fori(0, DEPTH) as l:
                at.layer(l)
                own.base, own.n = l * DVE_STEPS, 0
                step(v.tensor_copy(gain[:, :], gall[:, bass.ds(l, 1), :].rearrange("p a n -> p (a n)")))
                norm_x(G_MIX)

                for i in range(NZ):
                    freed(v.tensor_tensor(z[:, i, :], tile()[:, 0:T], rB[:, :], ALU.mult))
                    tell("z_ready")
                for j, n in enumerate((384, 256)):
                    freed(v.tensor_scalar(m[:, j * T:j * T + T], tile()[:, 0:T], 1 / n, EPS, ALU.mult, ALU.add))
                refine(P, 2 * T)
                for k in range(5):
                    c0 = 0 if k < 3 else T
                    step(v.scalar_tensor_tensor(z[:, k, :], z[:, k, :], gain[:, G_QL + k:G_QL + k + 1], y[:, c0:c0 + T], ALU.mult, ALU.mult))
                tell("lat_ready")

                for h in range(H):
                    freed(v.tensor_copy(qkA[0:QK, h, :], tile()[0:QK, 0:T]))
                tell("qk_raw")
                for h in range(H):
                    freed(v.tensor_copy(qkA[0:NOPE, 4 + h, :], tile()[0:NOPE, 0:T]))
                    step(v.tensor_copy(qkA[NOPE:QK, 4 + h, :], z[NOPE:QK, KR, :]))
                tell("qk_raw")
                for j, g in enumerate((G_Q, G_K)):
                    for h in range(H):
                        freed(v.tensor_scalar(m[0:QK, h * T:h * T + T], tile()[0:QK, 0:T], 1 / QK, EPS, ALU.mult, ALU.add))
                    refine(QK, 4 * T)
                    step(v.scalar_tensor_tensor(qkB[0:QK, 4 * j:4 * j + 4, :], qkA[0:QK, 4 * j:4 * j + 4, :], gain[0:QK, g:g + 1],
                                                y[0:QK, :].rearrange("p (h t) -> p h t", h=4), ALU.mult, ALU.mult))
                tell("qk_norm")
                step(v.tensor_tensor(qkA[0:QK, :, :], qkB[0:QK, :, :], cos.unsqueeze(1).broadcast_to([QK, 8, T]), ALU.mult))
                for i in range(8):
                    freed(v.tensor_tensor(tmp[0:QK, 0:T], tile()[0:QK, 0:T], sin, ALU.mult))
                    step(v.tensor_tensor(qkB[0:QK, i, :], qkA[0:QK, i, :], tmp[0:QK, 0:T], ALU.add))
                tell("qk_ready")
                step(v.tensor_scalar(qg[:, :, :], qkB[0:NOPE, 0:4, TP:T], gain[0:NOPE, G_K:G_K + 1], None, ALU.mult))
                step(v.tensor_tensor(sprod[:, :, :], qkB[0:QK, 0:4, TP:T], qkB[0:QK, 4:8, TP:T], ALU.mult))
                tell("small_ready")
                for a in range(2):
                    freed(v.tensor_copy(vp[:, a, :], tile()))
                tell("vp_ready")
                freed(v.tensor_copy(qt[:, :, :, :], tile()[:, 0:64].rearrange("p (c h b) -> p c b h", c=2, h=H)))
                t = tile()
                for j in range(4):
                    ins = v.tensor_scalar(qblk[:, :, j, :], t[:, 0:32].rearrange("p (h b) -> p b h", h=H), hm[:, j:j + 1], None, ALU.mult)
                    if j < 3:
                        step(ins)
                freed(ins)
                freed(v.tensor_copy(snew[:, :, :], tile()[0:1, 0:32].rearrange("p (h b) -> p h b", h=H)))

                for h in range(H):
                    freed(v.tensor_tensor(sS[:, h, :], tile()[:, 0:384], con[:, C_MASK:C_MASK + 384], ALU.add))
                for a, (c0, c1) in enumerate(((0, P), (P, 384))):
                    step(v.tensor_reduce(nmx[:, :, a:a + 1], sS[:, :, c0:c1], AXX, ALU.max, negate=True))
                step(v.tensor_scalar(nmx[:, :, :], nmx[:, :, :], QK ** -0.5, None, ALU.mult))
                tell("soft_in")
                wait("soft_exp")
                step(v.reciprocal(psum_p[:, :, :], psum_p[:, :, :]))
                for h in range(H):
                    for a, (c0, c1) in enumerate(((0, P), (P, 384))):
                        step(v.tensor_scalar(sS[:, h, c0:c1], sS[:, h, c0:c1], psum_p[:, h, a:a + 1], None, ALU.mult))
                tell("soft_p")
                for h in range(H):
                    freed(v.tensor_copy(pT[:, h, :], tile()[:, 0:384]))
                tell("soft_t")
                for h in range(H):
                    freed(v.tensor_copy(mix[:, h, 0:TP], tile()[:, 0:TP]))
                tell("mla_done")

                freed(v.tensor_scalar(m[:, 0:T], tile()[:, 0:T], gain[:, B_GATE:B_GATE + 1], None, ALU.add))
                tell("gate_in")
                wait("gate_soft")
                step(v.scalar_tensor_tensor(xg[:, L_A, :], m[:, 0:T], 0.0, y[:, 0:T], ALU.min, ALU.subtract))
                for c in range(4):
                    step(v.tensor_tensor_scan(xg[:, L_BC, 64 * c:64 * c + 64], ones[:, 0:64], xg[:, L_A, 64 * c:64 * c + 64],
                                              0.0, ALU.mult, ALU.add))
                step(v.tensor_scalar(bl[:, :], xg[:, L_BC, 63:256:64], 1 / 16, None, ALU.mult))
                tell("gate_la")
                wait("gate_exp")
                step(v.scalar_tensor_tensor(xg[:, L_QD, 0:TP], z[:, GQ, 0:TP], 32 ** -0.5, xg[:, L_EB, 0:TP], ALU.mult, ALU.mult))
                step(v.tensor_tensor(xg[:, L_KD, 0:TP], z[:, GK, 0:TP], xg[:, L_ENB, 0:TP], ALU.mult))
                step(v.tensor_tensor(xg[:, L_KE, 0:TP], z[:, GK, 0:TP], xg[:, L_EKE, 0:TP], ALU.mult))
                for h in range(H):
                    step(v.tensor_scalar(qbd[:, h, :], xg[:, L_QD, 0:TP], hm[:, h:h + 1], None, ALU.mult))
                    step(v.tensor_scalar(qsb[:, :, h], z[:, GQ, TP:T], hm[:, h:h + 1], 32 ** -0.5, ALU.mult, ALU.mult))
                tell("gate_dec")
                for a in range(2):
                    freed(v.tensor_copy(gvn[0:64, 2 * a:2 * a + 2, :], tile()[0:64, :].rearrange("p (c n) -> p c n", c=2)))
                freed(v.tensor_copy(gvs_n[:, :], tile()[0:B, 0:256]))
                tell("gvs_ready")
                freed(v.tensor_copy(kendn[0:64, :, :], tile()[0:64, :].rearrange("p (c n) -> p c n", c=4)))
                for a in range(2):
                    freed(v.tensor_tensor(att[0:64, 2 * a:2 * a + 2, :], tile()[0:64, :].rearrange("p (c n) -> p c n", c=2),
                                          con[0:64, C_TRI:C_TRI + 256].unsqueeze(1).broadcast_to([64, 2, 256]), ALU.mult))
                tell("gla_nat")
                bm = con[:, C_BM:C_BM + 256]
                for c in range(4):
                    if c % 2 == 0:
                        t = tile()
                    upd = t[:, 256 * (c % 2):256 * (c % 2) + 256]
                    if c == 0:
                        step(v.tensor_copy(S[:, 0, :], upd))
                    elif c % 2:
                        freed(v.scalar_tensor_tensor(S[:, c, :], S[:, c - 1, :], xg[:, L_EB, 64 * c + 63:64 * c + 64], upd, ALU.mult, ALU.add))
                    else:
                        step(v.scalar_tensor_tensor(S[:, c, :], S[:, c - 1, :], xg[:, L_EB, 64 * c + 63:64 * c + 64], upd, ALU.mult, ALU.add))
                    step(v.tensor_tensor(S[:, c, :], S[:, c, :], bm, ALU.mult))
                dve.wait_ge(gvs_in, 64 * (l + 1))
                dve.wait_ge(layer_in, 64 * (l + 1))
                step(v.tensor_tensor(gst[:, :, :], gst[:, :, :], ea[:, :].unsqueeze(2).broadcast_to([P, B, 64]), ALU.mult))
                step(v.tensor_tensor(vb[:, :, :], vb[:, :, :], z[:, GK, TP:T].unsqueeze(2).broadcast_to([P, B, 64]), ALU.mult))
                step(v.tensor_tensor(gst[:, :, :], gst[:, :, :], vb[:, :, :], ALU.add))
                tell("gla_state")
                freed(v.tensor_copy(z[:, GV:GV + 2, 0:TP], tile().rearrange("p (c t) -> p c t", c=2)))
                freed(v.tensor_copy(z[:, GV:GV + 2, TP:T], tile()[:, 0:16].rearrange("p (c t) -> p c t", c=2)))
                tell("gla_raw")
                for c in range(2):
                    freed(v.tensor_scalar(m[:, c * T:c * T + T], tile()[:, 0:T], 1 / 64, EPS, ALU.mult, ALU.add))
                refine(P, 2 * T)
                step(v.tensor_scalar(sq[:, 4:6, :], sq[:, 4:6, :], 1.0, None, ALU.add))
                step(v.reciprocal(sq[:, 4:6, :], sq[:, 4:6, :]))
                step(v.tensor_tensor(sq[:, 4:6, :], sq[:, 4:6, :], z[:, GR:GR + 2, :], ALU.mult))
                step(v.scalar_tensor_tensor(z[:, GV:GV + 2, :], z[:, GV:GV + 2, :], gain[:, G_GLA:G_GLA + 1],
                                            y[:, 0:2 * T].rearrange("p (c t) -> p c t", c=2), ALU.mult, ALU.mult))
                step(v.tensor_tensor(mix[:, 4:6, :], z[:, GV:GV + 2, :], sq[:, 4:6, :], ALU.mult))
                for c in range(2):
                    freed(v.tensor_scalar(mix[:, 6 + c, :], tile()[:, 0:T], gain[:, G_POOL + c:G_POOL + c + 1], None, ALU.mult))
                for s in range(2):
                    step(v.tensor_copy(wuq_b[:, s, :, 0:256], w_uk))
                tell("mix_side")

                with dve.Fori(0, B // 2) as i:
                    at.enter(i, tile_ready=8, tile_free=8, pair_ready=16, pair_sq=16, root=2, dec_amax=2, dec_exp=2)
                    base, n = own.base, own.n
                    own.base, own.n = base + n + i * DEC_STEPS, 0

                    def keys(s, p0, p1):
                        for pair in range(p0, p1):
                            q = pair % 2
                            wait("pair_ready")
                            wait("pair_sq")
                            v.tensor_copy(sc[:, 2 * pair:2 * pair + 2, :], ps[:, 4 + 2 * q:6 + 2 * q, 256:260]).then_inc(sems["pair_sc"], 1)
                            v.tensor_reduce(ssn[:, 2 * pair:2 * pair + 2, :], psq[:, q, :].rearrange("p (g c) -> p g c", c=64),
                                            AXX, ALU.add).then_inc(sems["pair_sum"], 1)
                            if pair == 4:
                                dve.wait_ge(kr_in, 256 * (l * B + i * 2 + s + 1))
                                v.tensor_scalar(krC[:, :, :], krT[:, :, :], gain[:, G_KR4:G_KR4 + 1], None, ALU.mult).then_inc(sems["kr_scaled"], 1)

                    def values(s):
                        t = tile()
                        step(v.reciprocal(den[:, 0:4], t[:, 0:4]))
                        freed(v.tensor_copy(rs[:, 4:8], t[:, 4:8]))
                        t = tile()
                        for c in range(2):
                            ins = v.scalar_tensor_tensor(rs[:, 8 + 4 * c:12 + 4 * c], rs[:, 4:8], z[:, CKV + c, bass.ds(i * 2 + TP + s, 1)],
                                                         t[:, 4 * c:4 * c + 4], ALU.mult, ALU.add)
                            if c:
                                freed(ins)
                            else:
                                step(ins)
                        tell("lat_used")
                        for c in range(2):
                            step(v.tensor_tensor(olat[:, c, bass.ds(i * 2 + s, 1), :], rs[:, 8 + 4 * c:12 + 4 * c].unsqueeze(1),
                                                 den[:, 0:4].unsqueeze(1), ALU.mult))

                    for s in range(2):
                        step(v.tensor_copy(wuq_b[:, s, :, 256:260], qt[:, :, bass.ds(i * 2 + s, 1), :].rearrange("p c b h -> p c (b h)")))
                        step(v.tensor_copy(qbs[:, s, :], qblk[:, bass.ds(i * 2 + s, 1), :, :].rearrange("p b j h -> p (b j h)")))
                        tell("seq_in")
                        keys(s, 0, 4)
                        if s == 1:
                            values(0)
                        keys(s, 4, 8)
                        t = tile()
                        step(v.tensor_tensor(krS[:, :, :], krC[:, :, :], con[:, C_COS4:C_COS4 + 512].rearrange("p (g n) -> p g n", g=4), ALU.mult))
                        freed(v.tensor_tensor(tmp[:, 0:512], t, con[:, C_SIN4:C_SIN4 + 512], ALU.mult))
                        step(v.tensor_tensor(krS[:, :, :], krS[:, :, :], tmp[:, 0:512].rearrange("p (g n) -> p g n", g=4), ALU.add))
                        tell("kr_rot")
                        t = tile()
                        step(v.tensor_tensor(sc[:, 0:PAGES, :], sc[:, 0:PAGES, :], t[:, 0:64].rearrange("p (g h) -> p g h", h=H), ALU.add))
                        freed(v.tensor_tensor(m[:, 0:64].rearrange("p (g h) -> p g h", h=H), ssn[:, :, :],
                                              t[:, 64:80].unsqueeze(2).broadcast_to([P, PAGES, H]), ALU.add))
                        step(v.tensor_scalar(m[:, 0:64], m[:, 0:64], 1 / QK, EPS, ALU.mult, ALU.add))
                        refine(P, 64)
                        step(v.tensor_tensor(sc[:, 0:PAGES, :], sc[:, 0:PAGES, :], y[:, 0:64].rearrange("p (g h) -> p g h", h=H), ALU.mult))
                        step(v.memset(sc[:, PAGES, :], NEG))
                        step(v.tensor_copy(sc[0:1, PAGES, :], snew[0:1, :, bass.ds(i * 2 + s, 1)].rearrange("p h b -> p (h b)")))
                        step(v.tensor_reduce(mxp[:, 0:4], sc[:, :, :].rearrange("p g h -> p h g"), AXX, ALU.max))
                        tell("dec_max")
                        wait("dec_amax")
                        step(v.tensor_tensor(sc[:, :, :], sc[:, :, :], mx[:, 0:4].unsqueeze(1).broadcast_to([P, S_PAGES, H]), ALU.subtract))
                        tell("dec_in")
                        wait("dec_exp")
                        step(v.tensor_reduce(rs[:, 0:4], pr[:, :, :].rearrange("p g h -> p h g"), AXX, ALU.add))
                        tell("dec_sum")
                    values(1)
                    assert own.n == DEC_STEPS, own.n
                at.leave(B // 2)
                own.base, own.n = base, n + B // 2 * DEC_STEPS
                tell("dec_out")
                freed(v.tensor_copy(mix[:, 0:4, TP:T], tile()[:, 0:32].rearrange("p (h b) -> p h b", h=H)))
                tell("mix_ready")

                wait("mem_sq")
                step(v.tensor_reduce(tmp[:, 0:NM], sq[:, :, 0:NM].rearrange("p k t -> p t k"), AXX, ALU.add))
                tell("ssum_ready")
                for k in range(KD):
                    step(v.tensor_scalar(mg[:, k, 0:NM], mg[:, k, 0:NM], gain[:, G_MEM + k:G_MEM + k + 1], None, ALU.mult))
                tell("mg_ready")
                freed(v.tensor_scalar(m[:, 0:NM + 2], tile()[:, 0:NM + 2], 1 / D, EPS, ALU.mult, ALU.add))
                refine(P, NM + 2, rBm[:, :])
                for i in range(8):
                    freed(v.tensor_tensor(kraw[:, i, :], tile()[:, 0:NM], rBm[:, 0:NM], ALU.mult))
                tell("km_raw")
                for h in range(H):
                    for a in range(2):
                        freed(v.tensor_scalar(vm[:, a, 256 * h:256 * h + 256], tile()[:, 0:256], rBm[:, NM + a:NM + a + 1], None, ALU.mult))
                for h in range(H):
                    freed(v.tensor_scalar(m[:, h * NM:h * NM + NM], tile()[:, 0:NM], 1 / 256, EPS, ALU.mult, ALU.add))
                refine(P, 4 * NM)
                for i in range(8):
                    step(v.scalar_tensor_tensor(kmT[:, i, :], kraw[:, i, :], gain[:, G_XK + i % 2:G_XK + i % 2 + 1],
                                                y[:, (i // 2) * NM:(i // 2) * NM + NM], ALU.mult, ALU.mult))
                tell("km_ready")
                for k in range(KD):
                    add_to_x(k)
                tell("x_new")

                norm_x(G_XA)
                dve.wait_ge(stored, 16 * STORES * (l + 1))
                for i in range(8):
                    freed(v.tensor_tensor(z[:, i, :], tile()[:, 0:T], rB[:, :], ALU.mult))
                tell("xq_raw")
                for h in range(H):
                    freed(v.tensor_scalar(m[:, h * T:h * T + T], tile()[:, 0:T], 1 / 256, EPS, ALU.mult, ALU.add))
                refine(P, 4 * T)
                for i in range(8):
                    step(v.scalar_tensor_tensor(z[:, i, :], z[:, i, :], gain[:, G_XQ + i % 2:G_XQ + i % 2 + 1],
                                                y[:, (i // 2) * T:(i // 2) * T + T], ALU.mult, ALU.mult))
                tell("xq_ready")
                for h in range(H):
                    freed(v.tensor_copy(xS[:, h, :, :], tile().rearrange("p (a n) -> p a n", a=2)))
                step(v.tensor_reduce(nmx[:, :, :], xS[:, :, :, :], AXX, ALU.max, negate=True))
                step(v.tensor_scalar(nmx[:, :, :], nmx[:, :, :], 1 / 16, None, ALU.mult))
                tell("x_in")
                wait("x_exp")
                step(v.reciprocal(psum_p[:, :, :], psum_p[:, :, :]))
                for h in range(H):
                    for a in range(2):
                        step(v.tensor_scalar(xS[:, h, a, :], xS[:, h, a, :], psum_p[:, h, a:a + 1], None, ALU.mult))
                tell("x_p")
                for h in range(H):
                    freed(v.tensor_copy(xP[:, h, :, :], tile().rearrange("p (a n) -> p a n", a=2)))
                tell("x_t")
                for h in range(H):
                    freed(v.tensor_copy(mix[:, 2 * h:2 * h + 2, 0:TP], tile().rearrange("p (a n) -> p a n", a=2)))
                freed(v.tensor_copy(xs[:, :, :, :], tile()[:, 0:64].rearrange("p (b a h) -> p b a h", b=B, a=2)))
                step(v.tensor_tensor(mxp[:, :].rearrange("p (b h) -> p b h", b=B), xs[:, :, 0, :], xs[:, :, 1, :], ALU.max))
                tell("xs_max")
                wait("xs_amax")
                step(v.tensor_tensor(xs[:, :, :, :], xs[:, :, :, :],
                                     mx[:, :].rearrange("p (b h) -> p b h", b=B).unsqueeze(2).broadcast_to([P, B, 2, H]), ALU.subtract))
                tell("xs_in")
                wait("xs_exp")
                step(v.tensor_tensor(rs[:, :].rearrange("p (b h) -> p b h", b=B), xs[:, :, 0, :], xs[:, :, 1, :], ALU.add))
                tell("xs_sum")
                freed(v.reciprocal(den[:, :], tile()[:, 0:32]))
                t = tile()
                step(v.tensor_copy(rs[:, :], den[:, :]))
                for c in range(2):
                    ins = v.tensor_tensor(mix[:, c:8:2, TP:T], t[:, 0:64].rearrange("p (h c b) -> p h c b", h=H, c=2)[:, :, c, :],
                                          den[:, :].rearrange("p (b h) -> p h b", b=B), ALU.mult)
                    if c:
                        freed(ins)
                    else:
                        step(ins)
                tell("xo_ready")
                for k in range(KD):
                    add_to_x(k)
                tell("x_new")

                norm_x(G_MLP)
                dve.sem_inc(passed["dve"], 1)
                hid = y[:, 0:1056].rearrange("p (s t) -> p s t", s=4)
                with dve.Fori(0, U_FF1 // SLOTS) as i:
                    at.enter(i, tile_ready=8, tile_free=8, ff_done=8)
                    for t in range(8):
                        dve.wait_ge(sems["ff_done"], at["ff_done"].free())
                        freed(v.scalar_tensor_tensor(hid[:, t % 4, :], tile()[:, 0:T], 0.0, rB[:, :], ALU.max, ALU.mult))
                        tell("ff_in")
                at.leave(U_FF1 // SLOTS)
                with dve.Fori(0, 2) as i:
                    at.enter(i, tile_ready=4, tile_free=4)
                    for k in range(4):
                        t = tile()
                        x_k = xT[:, bass.ds(i * 4 + k, 1), :]
                        freed(v.tensor_tensor(x_k, x_k, t[:, 0:T].unsqueeze(1), ALU.add))
                at.leave(2)
                tell("x_new")
                dve.sem_inc(sems["tile_free"], 2)
                at["tile_free"].next(2)
                at["tile_ready"].next(2)
                assert own.n == DVE_STEPS, own.n

        @block.tensor
        def _(pe):
            at = Counts(sems, SIGNALS)
            mm = nc.tensor.matmul

            def wait(name):
                pe.wait_ge(sems[name], at[name].next())

            def bank():
                pe.wait_ge(sems["tile_free"], at["tile_free"].free())
                return ps[:, at["tile_free"].slot, :]

            owed = []

            def settle():
                while owed:
                    pe.wait_ge(sems["tile_ready"], owed.pop())
                    pe.sem_inc(sems["unit_used"], 1)

            def ready(ins, unit=False):
                ins.then_inc(sems["tile_ready"], 1)
                settle()
                n = at["tile_ready"].next()
                if unit:
                    owed.append(n)

            def unit():
                n = at["unit_used"].next()
                s = at["unit_used"].slot
                pe.wait_ge(unit_in[s], (n - SLOTS + (SLOTS - 1 - s)) * (16 // SLOTS))
                return ring[:, s, :]

            def used(ins):
                ins.then_inc(sems["unit_used"], 1)

            def product(out, pairs):
                for i, (a, b) in enumerate(pairs):
                    ins = mm(out, a, b, start=i == 0, stop=i == len(pairs) - 1)
                return ins

            def mean_x():
                wait("ssum_ready")
                product(ps[:, 4, 0:T], [(ones[:, :], tmp[:, 0:T])]).then_inc(sems["mean_ready"], 1)

            def normed_projection(n_units, tiles_last=2):
                for i in range(n_units):
                    tiles = tiles_last if i == n_units - 1 else 2
                    u = unit().rearrange("p (a k n) -> p a k n", a=2, k=KD)
                    for a in range(tiles):
                        t = bank()
                        for k in range(KD):
                            if i == 0 and a == 0:
                                wait("xg_ready")
                            ins = mm(t[:, 0:T], u[:, a, k, :], xg[:, k, :], start=k == 0, stop=k == KD - 1)
                        ready(ins, a == tiles - 1)
                    if i == 0:
                        mean_x()

            pe.sem_inc(sems["unit_used"], SLOTS)
            pe.sem_inc(sems["pair_ready"], PAGES // 2)
            pe.wait_ge(once_in, 48)
            with pe.Fori(0, DEPTH) as l:
                at.layer(l)
                normed_projection(U_IN, 1)
                wait("lat_sq")
                ready(product(bank()[:, 0:T], [(ones[:, :], xg[:, k, :]) for k in range(3)]))
                ready(product(bank()[:, 0:T], [(ones[:, :], xg[:, k, :]) for k in range(3, 5)]))
                pe.wait_ge(layer_in, 64 * (l + 1))
                wait("lat_ready")
                for h in range(H):
                    ready(product(bank()[0:QK, 0:T], [(w_uq[:, c, h, :], z[:, CQ + c, :]) for c in range(3)]))
                for h in range(H):
                    ready(product(bank()[0:NOPE, 0:T], [(w_uk[:, c, h * NOPE:h * NOPE + NOPE], z[:, CKV + c, :]) for c in range(2)]))
                for j in range(2):
                    wait("qk_sq")
                    for h in range(H):
                        ready(product(bank()[0:QK, 0:T], [(ones[0:QK, 0:QK], sq[0:QK, 4 * j + h, :])]))
                wait("qk_norm")
                for i in range(8):
                    ready(product(bank()[0:QK, 0:T], [(swap[0:QK, 0:QK], qkB[0:QK, i, :])]))
                for a in range(2):
                    ready(product(bank(), [(z[:, CKV + c, P * a:P * a + P], w_uv[:, c, :]) for c in range(2)]))
                wait("small_ready")
                t = bank()
                for c in range(2):
                    for h in range(H):
                        o = (c * H + h) * B
                        ins = mm(t[:, o:o + B], w_ukt[0:NOPE, h, P * c:P * c + P], qg[:, h, :], start=True, stop=True)
                ready(ins)
                ready(product(bank()[:, 0:32], [(rep[0:QK, :], qkB[0:QK, 0:4, TP:T])]))
                ready(product(bank()[0:1, 0:32], [(ones[0:QK, 0:1], sprod[:, :, :])]))
                wait("qk_ready")
                for h in range(H):
                    t = bank()
                    mm(t[:, 0:P], qkB[0:QK, h, 0:P], qkB[0:QK, 4 + h, 0:P], start=True, stop=True)
                    ready(mm(t[:, P:384], qkB[0:QK, h, P:TP], qkB[0:QK, 4 + h, 0:TP], start=True, stop=True))
                wait("soft_p")
                for h in range(H):
                    t = bank()
                    for a in range(3):
                        ins = nc.tensor.transpose(t[:, P * a:P * a + P], sS[:, h, P * a:P * a + P], ident)
                    ready(ins)
                wait("vp_ready")
                wait("soft_t")
                for h in range(H):
                    t = bank()
                    mm(t[:, 0:TP], vp[:, 0, P * h:P * h + P], pT[:, h, 0:TP], start=True, stop=False)
                    ready(mm(t[:, P:TP], vp[:, 1, P * h:P * h + P], pT[:, h, TP:384], start=False, stop=True))

                ready(product(bank()[:, 0:T], [(mat[0:16, M_GATE:M_GATE + P], z[0:16, GLOW, :])]))
                for a in range(2):
                    t = bank()
                    pe.sem_inc(passed["pe"], 1)
                    for c in range(2):
                        for k in range(2):
                            o = c * 256 + k * P
                            ins = nc.tensor.transpose(t[0:64, o:o + P], z[:, GV + k, (2 * a + c) * 64:(2 * a + c) * 64 + 64], ident)
                    ready(ins)
                t = bank()
                pe.sem_inc(passed["pe"], 1)
                for k in range(2):
                    ins = nc.tensor.transpose(t[0:B, k * P:k * P + P], z[:, GV + k, TP:T], ident)
                ready(ins)
                wait("gate_dec")
                t = bank()
                pe.sem_inc(passed["pe"], 1)
                for c in range(4):
                    ins = nc.tensor.transpose(t[0:64, c * P:c * P + P], xg[:, L_KE, 64 * c:64 * c + 64], ident)
                ready(ins)
                for a in range(2):
                    t = bank()
                    for c in range(2):
                        o = 64 * (2 * a + c)
                        ins = mm(t[0:64, 256 * c:256 * c + 256], xg[:, L_KD, o:o + 64], qbd[:, :, o:o + 64], start=True, stop=True)
                    ready(ins)
                wait("gla_nat")
                for a in range(2):
                    t = bank()
                    for c in range(2):
                        ins = mm(t[:, 256 * c:256 * c + 256], kendn[0:64, 2 * a + c, :], gvn[0:64, 2 * a + c, :], start=True, stop=True)
                    ready(ins)
                wait("gla_state")
                t = bank()
                pe.sem_inc(passed["pe"], 1)
                for k in range(2):
                    for c in range(4):
                        o = k * TP + 64 * c
                        if c:
                            mm(t[:, o:o + 64], S[:, c - 1, P * k:P * k + P], xg[:, L_QD, 64 * c:64 * c + 64], start=True, stop=True)
                        for j in range(2):
                            h = 2 * k + j
                            ins = mm(t[64 * j:64 * j + 64, o:o + 64], gvn[0:64, c, 64 * h:64 * h + 64], att[0:64, c, 64 * h:64 * h + 64],
                                     start=c == 0, stop=True, skip_group_check=True)
                ready(ins)
                t = bank()
                for b in range(B):
                    for j in range(2):
                        ins = mm(t[64 * j:64 * j + 64, b:16:B], gst[:, b, :], qsb[:, b, j:4:2], start=True, stop=True)
                ready(ins)
                wait("gla_sq")
                for c in range(2):
                    ready(product(bank()[:, 0:T], [(b64, sq[:, c, :])]))
                wait("pooled_ready")
                for c in range(2):
                    ready(product(bank()[:, 0:T], [(w_pool[:, c, :], pooled[:, c, :])]))

                with pe.Fori(0, B // 2) as i:
                    at.enter(i, tile_free=8, tile_ready=8, pair_sq=16, pair_sc=16, seq_in=2, kr_rot=2, dec_sum=2)

                    def keys(s, p0, p1):
                        for pair in range(p0, p1):
                            q = pair % 2
                            pe.wait_ge(sems["pair_sq"], at["pair_sq"].free())
                            pe.wait_ge(sems["pair_sc"], at["pair_sc"].free())
                            for pg in (2 * pair, 2 * pair + 1):
                                if pg % 4 == 0:
                                    pe.wait_ge(lt_in[pg // 4], 64 * (l * B + i * 2 + s + 1))
                                ins = product(ps[:, 4 + 2 * q + pg % 2, 0:260],
                                              [(latT[:, pg, P * c:P * c + P], wuq_b[:, s, c, :]) for c in range(2)])
                            ins.then_inc(sems["pair_ready"], 1)

                    def values(s):
                        wait("dec_sum")
                        t = bank()
                        mm(t[:, 0:4], ones[:, :], rs[:, 0:4], start=True, stop=True)
                        ready(mm(t[:, 4:8], ones[0:1, :], pr[0:1, PAGES, :], start=True, stop=True))
                        t = bank()
                        pe.wait_ge(lat_in[s], 256 * (l * (B // 2) + i + 1))
                        for c in range(2):
                            ins = product(t[:, 4 * c:4 * c + 4], [(lat[:, s, pg, P * c:P * c + P], pr[:, pg, :]) for pg in range(PAGES)])
                        ready(ins)

                    for s in range(2):
                        wait("seq_in")
                        keys(s, 0, 4)
                        if s == 1:
                            values(0)
                        keys(s, 4, 8)
                        pe.wait_ge(sems["kr_scaled"], l * B + i * 2 + s + 2)
                        ready(product(bank(), [(swap4, krC[:, :, :])]))
                        wait("kr_rot")
                        pe.wait_ge(sems["kr_sq"], l * B + i * 2 + s + 2)
                        t = bank()
                        for g in range(4):
                            mm(t[:, 16 * g:16 * g + 16], krS[:, g, :], qbs[:, s, :], start=True, stop=True)
                            ins = mm(t[:, 64 + 4 * g:68 + 4 * g], krQ[:, g, :], hm, start=True, stop=True)
                        ready(ins)
                    values(1)
                at.leave(B // 2)
                wait("dec_out")
                t = bank()
                for h in range(H):
                    ins = product(t[:, B * h:B * h + B], [(w_uv[:, c, P * h:P * h + P], olat[:, c, :, h]) for c in range(2)])
                ready(ins)

                wait("ssum_ready")
                t = bank()
                mm(t[:, 0:NM], ones[:, :], tmp[:, 0:NM], start=True, stop=True)
                for a in range(2):
                    ins = mm(t[:, NM + a:NM + a + 1], tmp[:, P * a:P * a + P], ones[:, 0:1], start=True, stop=True)
                ready(ins)
                wait("mg_ready")
                for i in range(U_MK):
                    u = unit().rearrange("p (a k n) -> p a k n", a=2, k=KD)
                    for a in range(2):
                        ready(product(bank()[:, 0:NM], [(u[:, a, k, :], mg[:, k, 0:NM]) for k in range(KD)]), a == 1)
                for h in range(U_MV):
                    u = unit().rearrange("p (k n) -> p k n", k=KD)
                    for a in range(2):
                        ready(product(bank()[:, 0:256], [(mg[:, k, P * a:P * a + P], u[:, k, :]) for k in range(KD)]), a == 1)
                wait("km_sq")
                for h in range(H):
                    ready(product(bank()[:, 0:NM], [(ones[:, :], sq[:, 2 * h + c, 0:NM]) for c in range(2)]))
                wait("mix_ready")

                def mixed():
                    for i in range(4):
                        u = unit().rearrange("p (a k n) -> p a k n", a=2, k=KD)
                        for a in range(2):
                            ready(product(bank()[:, 0:T], [(u[:, a, k, :], mix[:, k, :]) for k in range(KD)]), a == 1)

                mixed()
                normed_projection(U_XQ)
                wait("xq_sq")
                for h in range(H):
                    ready(product(bank()[:, 0:T], [(ones[:, :], sq[:, 2 * h + c, :]) for c in range(2)]))
                wait("xq_ready")
                pe.wait_ge(sems["km_ready"], l + 1)
                for h in range(H):
                    t = bank()
                    for a in range(2):
                        ins = product(t[:, NM * a:NM * a + NM], [(z[:, 2 * h + c, P * a:P * a + P], kmT[:, 2 * h + c, :]) for c in range(2)])
                    ready(ins)
                wait("x_p")
                for h in range(H):
                    t = bank()
                    for n in range(2):
                        for a in range(2):
                            o = n * NM + a * P
                            ins = nc.tensor.transpose(t[:, o:o + P], xS[:, h, a, P * n:P * n + P], ident)
                    ready(ins)
                wait("x_t")
                for h in range(H):
                    t = bank()
                    for c in range(2):
                        o = h * 256 + c * P
                        ins = product(t[:, TP * c:TP * c + TP], [(vm[:, n, o:o + P], xP[:, h, n, :]) for n in range(2)])
                    ready(ins)
                t = bank()
                for b in range(B):
                    u = unit().rearrange("p (k n) -> p k n", k=KD)
                    for n in range(2):
                        if n == 1:
                            settle()
                        for h in range(H):
                            o = b * 8 + n * 4 + h
                            ins = product(t[:, o:o + 1], [(u[:, 2 * h + c, P * n:P * n + P], z[:, 2 * h + c, TP + b:TP + b + 1]) for c in range(2)])
                    if b < B - 1:
                        ins.then_inc(sems["unit_used"], 1)
                ready(ins, True)
                wait("xs_sum")
                ready(product(bank()[:, 0:32], [(ones[:, :], rs[:, :])]))
                t = bank()
                for b in range(B):
                    u = unit().rearrange("p (n k) -> p n k", n=2)
                    for k in range(8):
                        if k == 4:
                            settle()
                        ins = product(t[:, k * B + b:k * B + b + 1], [(u[:, n, k * P:k * P + P], xs[:, b, n, k // 2:k // 2 + 1]) for n in range(2)])
                    if b < B - 1:
                        ins.then_inc(sems["unit_used"], 1)
                ready(ins, True)
                wait("xo_ready")
                mixed()

                normed_projection(SLOTS)
                settle()
                with pe.Fori(0, U_FF1 // SLOTS - 1) as i:
                    at.enter(i, tile_free=8, tile_ready=8, unit_used=SLOTS)
                    for j in range(SLOTS):
                        u = unit().rearrange("p (a k n) -> p a k n", a=2, k=KD)
                        for a in range(2):
                            ready(product(bank()[:, 0:T], [(u[:, a, k, :], xg[:, k, :]) for k in range(KD)]), a == 1)
                    settle()
                at.leave(U_FF1 // SLOTS - 1)
                settle()
                with pe.Fori(0, 2) as i:
                    at.enter(i, tile_free=4, tile_ready=4, unit_used=8)
                    for pair in range(2):
                        two = [bank(), bank()]
                        for g in range(4):
                            pe.wait_ge(sems["ff_done"], 32 * l + 8 * g + 12)
                            u = unit().rearrange("p (a k n) -> p a k n", a=2, k=KD)
                            for a in range(2):
                                for k in range(KD):
                                    ins = mm(two[a][:, 0:T], u[:, a, k, :], ffh[:, 8 * g + k, :], start=g == 0 and k == 0,
                                             stop=g == 3 and k == KD - 1)
                                if g == 3:
                                    ready(ins, a == 1)
                                elif a == 0:
                                    settle()
                            if g < 3:
                                ins.then_inc(sems["unit_used"], 1)
                    settle()
                at.leave(2)
                pe.wait_ge(sems["tile_ready"], at["tile_ready"].base + at["tile_ready"].n)
                pe.sem_inc(sems["tile_ready"], 2)
                at["tile_ready"].next(2)
                at["tile_free"].next(2)
                at.end_layer()


def _constants():
    import numpy as np
    c = np.zeros((P, NC), np.float32)
    p = np.arange(P)
    c[:, C_ID:C_ID + P] = np.eye(P)
    mask = np.where(p[None, :] <= p[:, None], 0.0, NEG)
    c[:, C_MASK:C_MASK + P] = mask
    c[:, C_MASK + 2 * P:C_MASK + 3 * P] = mask
    c[:, C_B64:C_B64 + P] = p[:, None] // 64 == p[None, :] // 64
    c[:, C_REP:C_REP + P] = p[:, None] == NOPE + p[None, :] % ROPE

    def swapped(n, first):
        m = np.zeros((P, P), np.float32)
        for g in range(first, n, ROPE):
            for i in range(ROPE // 2):
                m[g + ROPE // 2 + i, g + i] = -1
                m[g + i, g + ROPE // 2 + i] = 1
        return m

    c[:, C_SWAP:C_SWAP + P] = swapped(QK, NOPE)
    c[:, C_SWAP4:C_SWAP4 + P] = swapped(P, 0)
    half = ROPE // 2
    inv = np.float32(10000.0) ** (-np.arange(half, dtype=np.float32) / np.float32(half))
    pos = np.concatenate([np.arange(TP), np.full(B, PG * PAGES)]).astype(np.float32)
    ang = inv[np.arange(ROPE) % half][:, None] * pos[None, :]
    c[0:NOPE, C_COS:C_COS + T] = 1
    c[NOPE:QK, C_COS:C_COS + T] = np.cos(ang)
    c[NOPE:QK, C_SIN:C_SIN + T] = np.sin(ang)
    old = (PG * (4 * np.arange(4)[None, :, None] + (p // ROPE)[:, None, None]) + p[None, None, :]).astype(np.float32)
    ang = inv[p % half][:, None, None] * old
    c[:, C_COS4:C_COS4 + 512] = np.cos(ang).reshape(P, 512)
    c[:, C_SIN4:C_SIN4 + 512] = np.sin(ang).reshape(P, 512)
    c[:, C_HM:C_HM + 4] = p[:, None] // 32 == np.arange(4)[None, :]
    c[:, C_BM:C_BM + 256] = p[:, None] // 32 == np.arange(256)[None, :] // 64
    c[:, C_TRI:C_TRI + 256] = p[:, None] <= np.arange(256)[None, :] % 64
    t = np.concatenate([np.arange(TP), np.full(B, PG * PAGES)])
    for g, w in enumerate((2, 4, 8, 16)):
        c[64 * (g % 2):64 * (g % 2) + 64, C_INV + (g // 2) * T:C_INV + (g // 2 + 1) * T] = 1 / np.minimum(w, t + 1)
    return c


def kernel(**inputs):
    import numpy as np
    import concourse.bacc as _bacc
    from concourse import mybir as _mybir
    from concourse.bass_utils import run_bass_kernel_spmd as _run

    a = {k: np.asarray(v) for k, v in inputs.items()}
    f32 = np.float32

    def columns(v, n):
        return v.reshape(DEPTH, n, P).transpose(0, 2, 1)

    def tiled(w):
        k, n = w.shape[1:]
        v = w.reshape(DEPTH, k // D, KD, P, n // 256, 2, P)
        return v.transpose(0, 4, 1, 3, 5, 2, 6).reshape(DEPTH, -1, P, UNIT)

    off = np.cumsum([0, 384, 256, 32, 128, 128, 256, 16, 256, 256])
    w_in = np.zeros((DEPTH, D, 16 * P), f32)
    for tile, part, shift in ((CQ, 0, 0), (CKV, 1, 0), (KR, 2, NOPE), (GQ, 3, 0), (GK, 4, 0), (GV, 5, 0), (GLOW, 6, 0), (GR, 7, 0), (UU, 8, 0)):
        w = a["w_in"][:, :, off[part]:off[part + 1]]
        w_in[:, :, tile * P + shift:tile * P + shift + w.shape[2]] = w
    w_xv = a["w_xv"].reshape(DEPTH, KD, P, H, 256).transpose(0, 3, 2, 1, 4).reshape(DEPTH, H, P, UNIT)
    xk = a["cache_mem_k"].transpose(1, 0, 3, 4, 2).reshape(DEPTH, B, H * 2, P, NM).transpose(0, 1, 3, 2, 4).reshape(DEPTH, B, P, UNIT)
    xv = a["cache_mem_v"].transpose(1, 0, 2, 3, 4).reshape(DEPTH, B, 2, P, D).transpose(0, 1, 3, 2, 4).reshape(DEPTH, B, P, UNIT)
    units = np.concatenate([tiled(w_in), tiled(a["w_xk"]), w_xv, tiled(a["w_out"]), tiled(a["w_xq"]), xk, xv, tiled(a["w_xo"]),
                            tiled(a["w_ff1"]), tiled(a["w_ff2"])], axis=1).reshape(DEPTH * UNITS, P, UNIT)

    x = np.concatenate([a["x_prompt"].reshape(TP, D), a["x_sample"].reshape(B, D)])
    xt = x.reshape(T, KD, P).transpose(2, 1, 0)
    memt = a["mem_prompt"].reshape(NM, KD, P).transpose(2, 1, 0)
    lat = a["cache_mla_latent"]
    n_phys = lat.shape[0]
    lat_t = lat.transpose(0, 1, 3, 2).reshape(n_phys, DEPTH, 2, P, PG).transpose(0, 1, 3, 2, 4).reshape(n_phys, DEPTH, P, 256)
    pages = np.concatenate([lat_t, lat], axis=3).reshape(n_phys * DEPTH, P, 512)
    krope = a["cache_mla_krope"].transpose(0, 1, 3, 2).reshape(n_phys * DEPTH, ROPE, PG)
    table = a["page_table"].reshape(1, B * PAGES)

    gains = np.zeros((DEPTH, P, NG), f32)
    for c, name, n in ((G_MIX, "norm_mix", 8), (G_XA, "norm_xa", 8), (G_MLP, "norm_mlp", 8), (G_MEM, "norm_mem", 8), (G_QL, "g_q_lat", 3),
                       (G_KV, "g_kv_lat", 2), (B_GATE, "b_gate", 1), (G_POOL, "pool_scale", 2), (G_XQ, "g_xq", 2), (G_XK, "g_xk", 2)):
        gains[:, :, c:c + n] = columns(a[name], n)
    gains[:, 0:QK, G_Q] = a["g_qk_q"]
    gains[:, 0:QK, G_K] = a["g_qk_k"]
    gains[:, :, G_KR4] = np.tile(a["g_qk_k"][:, NOPE:], (1, 4))
    gains[:, :, G_GLA] = np.tile(a["g_gla_out"], (1, 2))
    gains = gains.transpose(1, 0, 2)

    mats = np.zeros((DEPTH, P, NMAT), f32)
    mats[:, :, M_UQ:M_UQ + 1152] = a["w_uq"].reshape(DEPTH, 3, P, H * QK).transpose(0, 2, 1, 3).reshape(DEPTH, P, -1)
    mats[:, :, M_UK:M_UK + 512] = a["w_uk"].reshape(DEPTH, 2, P, 256).transpose(0, 2, 1, 3).reshape(DEPTH, P, -1)
    mats[:, :, M_UV:M_UV + 1024] = a["w_uv"].reshape(DEPTH, 2, P, 512).transpose(0, 2, 1, 3).reshape(DEPTH, P, -1)
    mats[:, 0:NOPE, M_UKT:M_UKT + 1024] = a["w_uk"].transpose(0, 3, 2, 1).reshape(DEPTH, NOPE, 1024)
    mats[:, 0:16, M_GATE:M_GATE + P] = a["w_gate_up"]
    for g in range(4):
        r = 64 * (g % 2)
        o = M_POOL + (g // 2) * P + r
        mats[:, r:r + 64, o:o + 64] = a["w_pool"][:, g]

    gstate = a["state_gla"].reshape(B, DEPTH, P, 64).transpose(1, 2, 0, 3)
    pstate = a["state_pool"].transpose(1, 3, 0, 2).reshape(DEPTH, 2, P, B, 15).transpose(0, 2, 1, 3, 4)
    pstate_nat = a["state_pool"].transpose(1, 0, 2, 3)[:, :, 1:]

    nc = _bacc.Bacc("TRN2", target_bir_lowering=False, num_devices=1, dynamic_dma_scratch_size=8192)
    arrays, args = {}, []
    for name, v in dict(units=units, xt=xt, memt=memt, pages=pages, krope=krope, table=table, gains=gains, mats=mats,
                        consts=_constants(), gstate=gstate, pstate=pstate, pstate_nat=pstate_nat).items():
        v = np.ascontiguousarray(v)
        arrays[f"in_{name}"] = v
        args.append(nc.dram_tensor(f"in_{name}", v.shape, _mybir.dt.from_np(v.dtype), kind="ExternalInput").ap())
    outs = dict(y=(P, KD, T), lat=(DEPTH, P, 2, T), kr=(DEPTH, ROPE, T), glap=(DEPTH, P, 256), glas=(DEPTH, P, B, 64), u=(DEPTH, P, 2, T),
                pool=(DEPTH, B, 14, 256), mk=(DEPTH, P, 8, NM), mv=(DEPTH, P, 2, D))
    for name, shape in outs.items():
        args.append(nc.dram_tensor(f"out_{name}", shape, FP32, kind="ExternalOutput").ap())
    args.append(nc.dram_tensor("gla_values", (B, 256), FP32, kind="Internal").ap())
    decoder(nc, *args)
    r = _run(nc, [arrays], core_ids=[0]).results[0]
    o = {name: r[f"out_{name}"] for name in outs}

    y = o["y"].transpose(2, 1, 0).reshape(T, D)
    latent = o["lat"].transpose(0, 3, 2, 1).reshape(DEPTH, T, 256)
    kr = o["kr"].transpose(0, 2, 1)
    u = o["u"].transpose(0, 3, 2, 1).reshape(DEPTH, T, 256)
    glap = np.stack([o["glap"][:, 32 * h:32 * h + 32, 64 * h:64 * h + 64] for h in range(H)], axis=1)
    glas = o["glas"].reshape(DEPTH, H, 32, B, 64).transpose(3, 0, 1, 2, 4)
    mk = o["mk"].transpose(0, 3, 2, 1).reshape(1, DEPTH, NM, H, 256)
    mv = o["mv"].transpose(0, 2, 1, 3).reshape(1, DEPTH, NM, H, 256)
    pool_s = np.concatenate([o["pool"].transpose(1, 0, 2, 3), u[:, TP:].transpose(1, 0, 2)[:, :, None]], axis=2)
    return (y[None, :TP], y[TP:, None], latent[None, :, :TP], kr[None, :, :TP], glap[None], u[None, :, TP - 15:TP], mk, mv,
            latent[:, TP:].transpose(1, 0, 2)[:, :, None], kr[:, TP:].transpose(1, 0, 2)[:, :, None], glas, pool_s)
```

```python
import concourse.bass as bass
from concourse import mybir
from contextlib import ExitStack

FP32 = mybir.dt.float32
ALU = mybir.AluOpType
ACT = mybir.ActivationFunctionType
AXX = mybir.AxisListType.X
DEPTH, D, P = 2, 1024, 128
KD = D // P
TP, B = 256, 8
T = TP + B
H = 4
NOPE, ROPE = 64, 32
QK = NOPE + ROPE
PG, PAGES = 128, 16
S_PAGES = PAGES + 1
NM = 256
EPS = 1e-6
NEG = -1e30
SLOTS = 4
UNIT = 2048
U_IN, U_MK, U_MV, U_OUT, U_XQ, U_XK, U_XV, U_XO, U_FF1, U_FF2 = 8, 4, 4, 4, 4, 8, 8, 4, 16, 16
UNITS = U_IN + U_MK + U_MV + U_OUT + U_XQ + U_XK + U_XV + U_XO + U_FF1 + U_FF2
CQ, CKV, KR, GQ, GK, GV, GLOW, GR, UU, NZ = 0, 3, 5, 6, 7, 8, 10, 11, 13, 15
G_MIX, G_XA, G_MLP, G_MEM, G_QL, G_KV, G_Q, G_K, G_KR4, B_GATE, G_GLA, G_POOL, G_XQ, G_XK, NG = \
    0, 8, 16, 24, 32, 35, 37, 38, 39, 40, 41, 42, 44, 46, 48
M_UQ, M_UK, M_UV, M_UKT, M_GATE, M_POOL, NMAT = 0, 1152, 1664, 2688, 3712, 3840, 4096
C_ID, C_MASK, C_B64, C_REP, C_SWAP, C_SWAP4, C_COS, C_SIN, C_COS4, C_SIN4, C_HM, C_BM, C_TRI, C_INV, NC = \
    0, 128, 512, 640, 768, 896, 1024, 1288, 1552, 2064, 2576, 2580, 2836, 3092, 3620


class Count:

    def __init__(self, sem, per_layer, start):
        self.sem, self.per_layer, self.start = sem, per_layer, start
        self.base, self.n, self.done = start, 0, 0

    def next(self, k=1):
        self.n += k
        return self.base + self.n

    def free(self, k=1):
        return self.next(k) - self.start

    @property
    def slot(self):
        return (self.done + self.n - 1) % 4


class Counts:

    def __init__(self, sems, table):
        self.all = {name: Count(sems[name], *table[name]) for name in table}

    def __getitem__(self, name):
        return self.all[name]

    def layer(self, l):
        for c in self.all.values():
            c.base, c.n, c.done = l * c.per_layer + c.start, 0, 0

    def end_layer(self):
        for name, c in self.all.items():
            assert c.n in (0, c.per_layer), (name, c.n, c.per_layer)

    def enter(self, i, **per):
        self.kept = {name: (c.base, c.n) for name, c in self.all.items()}
        self.per = per
        for name, k in per.items():
            c = self.all[name]
            c.base, c.done, c.n = c.base + c.n + i * k, c.n, 0

    def leave(self, times):
        for name, c in self.all.items():
            base, n = self.kept[name]
            if name in self.per:
                assert c.n == self.per[name], (name, c.n, self.per[name])
                c.base, c.n, c.done = base, n + times * self.per[name], 0
            else:
                assert c.n == n, name


TILES, MOMENTS = 212, 10 + B
SIGNALS = dict(
    tile_ready=(TILES, 0),
    unit_used=(UNITS, SLOTS),
    pair_ready=(64, 8),
    mean_ready=(3, 0),
    x_sq=(3, 0), lat_sq=(1, 0), qk_sq=(2, 0), gla_sq=(1, 0), mem_sq=(1, 0), km_sq=(1, 0), xq_sq=(1, 0),
    kr_sq=(B, 0), pair_sq=(64, 2), ff_done=(32, 4),
    root=(MOMENTS, 0),
    gate_soft=(1, 0), gate_exp=(1, 0), soft_exp=(1, 0), dec_exp=(B, 0), x_exp=(1, 0), xs_exp=(1, 0),
    tile_free=(TILES, 4),
    lat_used=(B, 2),
    pair_sc=(64, 2), pair_sum=(64, 2),
    moment=(MOMENTS, 0),
    x_new=(3, 1), xg_ready=(24, 0), ssum_ready=(4, 0),
    z_ready=(15, 0), lat_ready=(1, 0), qk_raw=(2, 0), qk_norm=(1, 0), qk_ready=(1, 0), small_ready=(1, 0), vp_ready=(1, 0),
    soft_in=(1, 0), soft_p=(1, 0), soft_t=(1, 0), mla_done=(1, 0),
    gate_in=(1, 0), gate_la=(1, 0), gate_dec=(1, 0), gla_nat=(1, 0), gvs_ready=(1, 0), gla_state=(1, 0), gla_raw=(1, 0),
    mix_side=(1, 0), seq_in=(B, 0), kr_scaled=(B, 0), kr_rot=(B, 0), dec_max=(B, 0), dec_in=(B, 0), dec_sum=(B, 0),
    dec_out=(1, 0), olat_ready=(1, 0), mg_ready=(1, 0), mix_ready=(1, 0), km_raw=(1, 0), km_ready=(1, 0),
    xq_raw=(1, 0), xq_ready=(1, 0), x_in=(1, 0), x_p=(1, 0), x_t=(1, 0), hot_q=(1, 0), xs_in=(1, 0), hot_p=(1, 0), xs_out=(1, 0), xo_ready=(1, 0),
    ff_in=(32, 0),
    pooled_ready=(1, 0), dec_amax=(B, 0),
)
POOL_STEPS, ACT_STEPS, DVE_STEPS, DEC_STEPS = 16, 20, 274, 30


def decoder(nc, units, xt, memt, pages, table, gains, mats, consts, gstate, pstate, pstate_nat,
            o_y, o_lat, o_kr, o_glap, o_glas, o_u, o_pool, o_mk, o_mv, gvs):
    ctx = ExitStack()
    with ctx:
        def sb(name, shape, dt=FP32):
            return ctx.enter_context(nc.sbuf_tensor(name, shape, dt))

        def sem(name):
            return ctx.enter_context(nc.semaphore(name))

        ring = sb("ring", [P, SLOTS, UNIT])
        xT = sb("xT", [P, KD, T])
        xg = sb("xg", [P, KD, T])
        sq = sb("sq", [P, KD, T])
        rB = sb("rB", [P, T])
        z = sb("z", [P, NZ, T])
        qkA = sb("qkA", [P, 8, T])
        qkB = sb("qkB", [P, 8, T])
        mix = sb("mix", [P, KD, T])
        mat = sb("mat", [P, NMAT])
        con = sb("con", [P, NC])
        gall = sb("gall", [P, DEPTH, NG])
        gain = sb("gain", [P, NG])
        ones = sb("ones", [P, P])
        latT = sb("latT", [P, PAGES, 256])
        big = sb("big", [P, 2 * PAGES * 288])
        krQ = sb("krQ", [P, PAGES, ROPE])
        krN = sb("krN", [P, PAGES, ROPE])
        gvs_n = sb("gvs_n", [B, 256])
        m = sb("m", [P, 4 * T])
        y = sb("y", [P, 4 * T])
        tmp = sb("tmp", [P, 4 * T])
        rBm = sb("rBm", [P, NM + 2])
        wuq_b = sb("wuq_b", [P, 2, 2, 260])
        qt = sb("qt", [P, 2, B, H])
        qblk = sb("qblk", [P, B, 4, H])
        snew = sb("snew", [P, B, H])
        latn = sb("latn", [B, 256])
        ssn = sb("ssn", [P, 2, PAGES, H])
        ssr = sb("ssr", [P, PAGES])
        sc = sb("sc", [P, 2, PAGES, H])
        scw = sb("scw", [P, S_PAGES, H])
        pr = sb("pr", [P, S_PAGES, H])
        mxp = sb("mxp", [P, H])
        mx = sb("mx", [P, H])
        rs = sb("rs", [P, H])
        den = sb("den", [H, 1])
        olat = sb("olat", [P, 2, B, H])
        qg = sb("qg", [NOPE, H, B])
        qbs = sb("qbs", [P, 2, 16])
        sprod = sb("sprod", [QK, H, B])
        ptab = sb("ptab", [1, B * PAGES], mybir.dt.int32)
        nmx = sb("nmx", [P, H, 2])
        psum_p = sb("psum_p", [P, H, 2])
        bl = sb("bl", [P, 4])
        ea = sb("ea", [P, B])
        qsb = sb("qsb", [P, B, H])
        xs_max = sb("xs_max", [B * H, 1])
        xs_den = sb("xs_den", [B * H, 1])
        ue = sb("ue", [P, 2, 400])

        ps = ctx.enter_context(nc.psum_tensor("ps", [P, 8, 512], FP32))


        def within(t, at, *shape):
            names = "abc"[:len(shape)]
            n = 1
            for k in shape:
                n *= k
            v = t[:, at:at + n]
            return v.rearrange(f"p ({' '.join(names)}) -> p {' '.join(names)}", **dict(zip(names, shape)))

        sq_f, qkA_f, qkB_f, xg_f = (v[:, :, :].rearrange("p k t -> p (k t)") for v in (sq, qkA, qkB, xg))
        latT_f = latT[:, :, :].rearrange("p g c -> p (g c)")
        lat = within(big, 0, 2, PAGES, 288)
        ffh = within(big, 0, 32, T)
        gvn, S, vb, gst, kendn, pooled = (within(big, 4608, 4, 256), within(big, 5632, 4, 256), within(big, 6656, B, 64),
                                          within(big, 7168, B, 64), within(big, 7680, 4, P), within(big, 8192, 2, T))
        kmT, vm = within(latT_f, 0, 8, NM), within(latT_f, 2048, 2, D)
        kraw = within(qkA_f, 0, 8, NM)
        vp = within(m, 0, 2, 512)
        o4 = within(sq_f, 0, B, 256)[0:H]
        sS, pT = within(sq_f, 0, 4, 384), within(qkA_f, 0, 4, 384)
        qbd, att = within(y, 0, 4, TP), within(qkA_f, 0, 4, 256)
        psq = within(qkA_f, 0, 2, 512)
        krS, krC = within(qkB_f, 0, 4, PG), within(qkB_f, 512, 4, PG)
        wa, wb = within(qkB_f, 0, 2, 400), within(qkB_f, 800, 2, 400)
        xS, xP = within(qkA_f, 0, 4, 2, NM), within(qkB_f, 0, 4, 2, NM)
        hot = within(xg_f, 0, 2, B * H, B * H)
        hot_diag = within(xg_f, 0, 2, (B * H) ** 2)[:, :, ::B * H + 1]
        xsS, xsP, xsO = m[0:B * H, 0:NM], y[0:B * H, 0:NM], tmp[0:B * H, 0:NM]
        mg = xg
        L_BC, L_EB, L_ENB, L_EKE, L_QD, L_KD, L_KE, L_A = range(8)
        ident, swap, swap4, b64, rep = (con[:, c:c + P] for c in (C_ID, C_SWAP, C_SWAP4, C_B64, C_REP))
        hm = con[:, C_HM:C_HM + 4]
        cos, sin = con[0:QK, C_COS:C_COS + T], con[0:QK, C_SIN:C_SIN + T]
        w_uq = within(mat, M_UQ, 3, H, QK)
        w_uk, w_uv, w_ukt, w_pool = (within(mat, c, n, k) for c, n, k in
                                     ((M_UK, 2, 256), (M_UV, 2, 512), (M_UKT, 4, 256), (M_POOL, 2, P)))

        sems = {name: sem(name) for name in SIGNALS}
        dve_step, act_step, pool_step = sem("dve_step"), sem("act_own"), sem("pool_step")
        unit_in = [sem(f"unit_in{s}") for s in range(SLOTS)]
        lt_in = [sem(f"lt_in{g}") for g in range(4)]
        lat_in = [sem(f"lat_in{s}") for s in range(2)]
        STORES = 7
        once_in, layer_in, mg_in = (sem(n) for n in ("once_in", "layer_in", "mg_in"))
        y_out = sem("y_out")
        passed = {e: sem(f"passed_{e}") for e in ("pool", "sp", "pe", "dve")}
        stored, copied, gvs_out, gvs_in, tab_in = (sem(n) for n in ("stored", "copied", "gvs_out", "gvs_in", "tab_in"))
        block = ctx.enter_context(nc.Block())

        @block.sync
        def _(sp):
            at = Counts(sems, SIGNALS)
            sp.dma_start(ptab[:, :], table).then_inc(tab_in, 16)
            sp.wait_ge(tab_in, 16)
            with sp.Fori(0, DEPTH) as l:
                at.layer(l)

                def load_units(n):
                    first = at["unit_used"].n
                    with sp.Fori(0, n // SLOTS) as i:
                        at.enter(i, unit_used=SLOTS)
                        for s in range(SLOTS):
                            sp.wait_ge(sems["unit_used"], at["unit_used"].free())
                            sp.dma_start(ring[:, s, :], units[bass.ds(l * UNITS + first + i * SLOTS + s, 1), :, :]
                                         .rearrange("a p n -> p (a n)")).then_inc(unit_in[s], 16)
                    at.leave(n // SLOTS)

                load_units(U_IN)
                sp.wait_ge(sems["x_new"], 3 * l + 1)
                sp.sem_inc(passed["sp"], 1)
                with sp.Fori(0, B // 2) as i:
                    at.enter(i, pair_ready=PAGES)
                    for s in range(2):
                        for pg in range(PAGES):
                            page = sp.value_load(ptab[0:1, bass.ds(i * 2 * PAGES + s * PAGES + pg, 1)],
                                                 min_val=0, max_val=pages.shape[0] // DEPTH - 1)
                            src = pages[bass.ds(page * DEPTH + l, 1), :, :].rearrange("a p n -> p (a n)")
                            if pg % 2 == 0:
                                sp.wait_ge(sems["pair_ready"], at["pair_ready"].free())
                            sp.dma_start(latT[:, pg, :], src[:, 0:256]).then_inc(lt_in[pg // 4], 16)
                at.leave(B // 2)
                load_units(UNITS - U_IN)
                at.end_layer()
            sp.wait_ge(sems["x_new"], 3 * DEPTH + 1)
            sp.dma_start(o_y, xT[:, :, :]).then_inc(y_out, 16)
            sp.wait_ge(y_out, 16)

        @block.gpsimd
        def _(pool):
            at = Counts(sems, SIGNALS)
            steps = [0]

            def wait_ge(semaphore, value):
                pool.wait_ge(semaphore, value)
                pool.sem_inc(passed["pool"], 1)

            def step(ins):
                ins.then_inc(pool_step, 1)
                steps[0] += 1
                wait_ge(pool_step, at_step(steps[0]))

            at_step = lambda n: n
            step(pool.memset(ones[:, :], 1.0))
            step(pool.memset(ue[:, :, 0:16], 0.0))
            STEP0 = steps[0]
            pool.dma_start(xT[:, :, :], xt).then_inc(once_in, 16)
            pool.dma_start(con[:, :], consts).then_inc(once_in, 16)
            pool.dma_start(gall[:, :, :], gains).then_inc(once_in, 16)
            wait_ge(tab_in, 16)
            with pool.Fori(0, DEPTH) as l:
                at.layer(l)
                steps[0] = 0
                at_step = lambda n: STEP0 + l * POOL_STEPS + n
                wait_ge(sems["x_new"], 3 * l + 1)
                pool.dma_start(mat[:, :], mats[bass.ds(l, 1), :, :].rearrange("a p n -> p (a n)")).then_inc(layer_in, 16)
                pool.dma_start(gst[:, :, :], gstate[bass.ds(l, 1), :, :, :].rearrange("a p b v -> p (a b) v")).then_inc(layer_in, 16)
                for c in range(2):
                    pool.dma_start(ue[:, c, 272:400].rearrange("p (b j) -> p b j", b=B)[:, :, 0:15],
                                   pstate[bass.ds(l, 1), :, c, :, :].rearrange("a p b j -> p (a b) j")).then_inc(layer_in, 16)
                pool.dma_start(o_pool[bass.ds(l, 1), :, :, :].rearrange("a b j c -> (a b) j c"),
                               pstate_nat[bass.ds(l, 1), :, :, :].rearrange("a b j c -> (a b) j c")).then_inc(copied, 16)

                wait_ge(sems["z_ready"], 15 * l + 15)
                wait_ge(layer_in, 64 * (l + 1))
                step(pool.tensor_copy(ue[:, :, 16:272], z[:, UU:UU + 2, 0:TP]))
                step(pool.tensor_copy(ue[:, :, 272:400].rearrange("p c (b j) -> p c b j", b=B)[:, :, :, 15],
                                      z[:, UU:UU + 2, TP:T]))
                wait_ge(sems["mla_done"], l + 1)
                step(pool.tensor_tensor(wa[:, :, 1:400], ue[:, :, 1:400], ue[:, :, 0:399], ALU.add))
                src = wa
                for g, w in enumerate((2, 4, 8, 16)):
                    c, r = g // 2, 64 * (g % 2)
                    if g:
                        dst = wb if src is wa else wa
                        step(pool.tensor_tensor(dst[:, :, w - 1:400], src[:, :, w - 1:400],
                                                src[:, :, w // 2 - 1:400 - w // 2], ALU.add))
                        src = dst
                    step(pool.tensor_copy(pooled[r:r + 64, c, 0:TP], src[r:r + 64, c, 16:272]))
                    step(pool.tensor_copy(pooled[r:r + 64, c, TP:T],
                                          src[r:r + 64, c, 272:400].rearrange("p (b j) -> p b j", b=B)[:, :, 15]))
                inv = con[:, C_INV:C_INV + 2 * T].rearrange("p (c t) -> p c t", c=2)
                step(pool.tensor_tensor(pooled[:, :, :], pooled[:, :, :], inv, ALU.mult))
                step(pool.tensor_tensor(pooled[:, :, :], pooled[:, :, :], z[:, UU:UU + 2, :], ALU.subtract))
                pool.sem_inc(sems["pooled_ready"], 1)

                wait_ge(sems["gvs_ready"], l + 1)
                pool.dma_start(gvs, gvs_n[:, :]).then_inc(gvs_out, 16)
                wait_ge(gvs_out, 16 * (l + 1))
                for h in range(H):
                    pool.dma_start(vb[32 * h:32 * h + 32, :, :],
                                   gvs[:, 64 * h:64 * h + 64].unsqueeze(0).broadcast_to([32, B, 64])).then_inc(gvs_in, 16)

                wait_ge(sems["mix_side"], l + 1)
                pool.dma_start(mg[:, :, 0:NM], memt).then_inc(mg_in, 16)
                def load(j, s, pgs):
                    for pg in pgs:
                        page = pool.value_load(ptab[0:1, bass.ds((j * 2 + s) * PAGES + pg, 1)], min_val=0,
                                               max_val=pages.shape[0] // DEPTH - 1)
                        pool.dma_start(lat[:, s, pg, :], pages[bass.ds(page * DEPTH + l, 1), :, 256:544]
                                       .rearrange("a p n -> p (a n)")).then_inc(lat_in[s], 16)

                def maximum():
                    wait_ge(sems["dec_max"], at["dec_max"].next())
                    pool.partition_all_reduce(mx[:, :], mxp[:, :], P, bass.bass_isa.ReduceOp.max).then_inc(sems["dec_amax"], 1)

                def load_and_maximum(j, s):
                    wait_ge(sems["lat_used"], at["lat_used"].free())
                    load(j, s, range(0, 10))
                    maximum()
                    load(j, s, range(10, PAGES))

                wait_ge(sems["lat_used"], at["lat_used"].free())
                load(0, 0, range(PAGES))
                wait_ge(stored, 16 * (STORES * l + 5))
                with pool.Fori(0, B // 2 - 1) as i:
                    at.enter(i, dec_max=2, lat_used=2)
                    load_and_maximum(i, 1)
                    load_and_maximum(i + 1, 0)
                at.leave(B // 2 - 1)
                load_and_maximum(B // 2 - 1, 1)
                maximum()
                assert steps[0] == POOL_STEPS, steps
            wait_ge(copied, 16 * DEPTH)

        @block.scalar
        def _(act):
            at = Counts(sems, SIGNALS)
            act.preload_act_table_set("natural_log_exp_and_others")
            own = Count(act_step, ACT_STEPS, 0)

            def f(out, in_, func, **kw):
                return nc.scalar.activation(out, in_, func, **kw)

            def step(ins):
                ins.then_inc(act_step, 1)
                act.wait_ge(act_step, own.next())

            def power(rows, cols):
                act.wait_ge(sems["moment"], at["moment"].next())
                step(f(y[0:rows, 0:cols], m[0:rows, 0:cols], ACT.Ln))
                f(y[0:rows, 0:cols], y[0:rows, 0:cols], ACT.Exp, scale=-0.5).then_inc(sems["root"], 1)
                at["root"].next()

            def square_x():
                act.wait_ge(sems["x_new"], at["x_new"].free())
                f(sq[:, :, :], xT[:, :, :], ACT.Square).then_inc(sems["x_sq"], 1)
                power(P, T)

            act.sem_inc(sems["pair_sq"], 2)
            act.sem_inc(sems["ff_done"], 4)
            with act.Fori(0, DEPTH) as l:
                at.layer(l)
                own.base, own.n = l * ACT_STEPS, 0
                square_x()
                act.wait_ge(sems["z_ready"], 15 * l + 15)
                f(xg[:, 0:5, :], z[:, 0:5, :], ACT.Square).then_inc(sems["lat_sq"], 1)
                power(P, 2 * T)
                act.wait_ge(sems["lat_ready"], l + 1)
                act.dma_start(o_lat[bass.ds(l, 1), :, :, :].rearrange("a p c t -> (a p) c t"), z[:, CKV:CKV + 2, :]).then_inc(stored, 16)
                act.dma_start(o_kr[bass.ds(l, 1), :, :].rearrange("a p t -> (a p) t"), z[NOPE:QK, KR, :]).then_inc(stored, 16)
                act.dma_start(o_u[bass.ds(l, 1), :, :, :].rearrange("a p c t -> (a p) c t"), z[:, UU:UU + 2, :]).then_inc(stored, 16)
                for j in range(2):
                    act.wait_ge(sems["qk_raw"], 2 * l + j + 1)
                    f(sq[0:QK, 4 * j:4 * j + 4, :], qkA[0:QK, 4 * j:4 * j + 4, :], ACT.Square).then_inc(sems["qk_sq"], 1)
                power(QK, 4 * T)
                power(QK, 4 * T)
                act.wait_ge(sems["soft_in"], l + 1)
                for h in range(H):
                    for a, (c0, c1) in enumerate(((0, P), (P, 384))):
                        last = f(sS[:, h, c0:c1], sS[:, h, c0:c1], ACT.Exp, bias=nmx[:, h, a:a + 1],
                                 scale=QK ** -0.5, accum_out=psum_p[:, h, a:a + 1])
                last.then_inc(sems["soft_exp"], 1)
                act.wait_ge(sems["gate_in"], l + 1)
                step(f(y[:, 0:T], m[:, 0:T], ACT.Abs))
                step(f(y[:, 0:T], y[:, 0:T], ACT.Exp, scale=-1.0))
                f(y[:, 0:T], y[:, 0:T], ACT.Ln, bias=1.0).then_inc(sems["gate_soft"], 1)
                act.wait_ge(sems["gate_la"], l + 1)
                f(xg[:, L_EB, 0:TP], xg[:, L_BC, 0:TP], ACT.Exp, scale=1 / 16)
                f(xg[:, L_ENB, 0:TP], xg[:, L_BC, 0:TP], ACT.Exp, scale=-1 / 16)
                for c in range(4):
                    f(xg[:, L_EKE, 64 * c:64 * c + 64], xg[:, L_BC, 64 * c:64 * c + 64], ACT.Exp, bias=bl[:, c:c + 1], scale=-1 / 16)
                f(sq[:, 4:6, :], z[:, GR:GR + 2, :], ACT.Exp, scale=-1.0)
                f(ea[:, :], xg[:, L_A, TP:T], ACT.Exp, scale=1 / 16).then_inc(sems["gate_exp"], 1)
                act.wait_ge(sems["gla_raw"], l + 1)
                f(sq[:, 0:2, :], z[:, GV:GV + 2, :], ACT.Square).then_inc(sems["gla_sq"], 1)
                act.dma_start(o_glap[bass.ds(l, 1), :, :].rearrange("a p n -> (a p) n"), S[:, 3, :]).then_inc(stored, 16)
                act.dma_start(o_glas[bass.ds(l, 1), :, :, :].rearrange("a p b v -> (a p) b v"), gst[:, :, :]).then_inc(stored, 16)
                power(P, 2 * T)

                def keys(j, s, b):
                    for pair in range(PAGES // 2):
                        act.wait_ge(sems["pair_ready"], at["pair_ready"].next())
                        act.wait_ge(sems["pair_sum"], at["pair_sum"].free())
                        q = pair % 2
                        f(psq[:, q, :].rearrange("p (g c) -> p g c", g=2), ps[:, 4 + 2 * q:6 + 2 * q, 0:256],
                          ACT.Square).then_inc(sems["pair_sq"], 1)
                        at["pair_sq"].next()
                        if b and pair == 1:
                            power(P, 64)
                        if b and pair == 2:
                            exp()
                        if pair == 4:
                            act.wait_ge(lat_in[s], 16 * PAGES * (l * (B // 2) + j + 1))
                            f(krN[:, :, :], lat[:, s, :, 256:288], ACT.Copy)
                            f(krQ[:, :, :], lat[:, s, :, 256:288], ACT.Square).then_inc(sems["kr_sq"], 1)
                            at["kr_sq"].next()

                def exp():
                    act.wait_ge(sems["dec_in"], at["dec_in"].next())
                    f(pr[:, :, :], scw[:, :, :], ACT.Exp, scale=QK ** -0.5).then_inc(sems["dec_exp"], 1)
                    at["dec_exp"].next()

                keys(0, 0, 0)
                with act.Fori(0, B // 2 - 1) as i:
                    at.enter(i, pair_ready=16, pair_sum=16, pair_sq=16, moment=2, root=2, dec_in=2, dec_exp=2, kr_sq=2)
                    base, n = own.base, own.n
                    own.base, own.n = base + n + i * 2, 0
                    keys(i, 1, 1)
                    keys(i + 1, 0, 1)
                    assert own.n == 2
                at.leave(B // 2 - 1)
                own.base, own.n = base, n + B - 2
                keys(B // 2 - 1, 1, 1)
                power(P, 64)
                exp()

                act.wait_ge(sems["olat_ready"], l + 1)
                act.wait_ge(mg_in, 16 * (l + 1))
                f(sq[:, :, 0:NM], mg[:, :, 0:NM], ACT.Square).then_inc(sems["mem_sq"], 1)
                power(P, NM + 2)
                act.wait_ge(sems["km_raw"], l + 1)
                f(sq[:, :, 0:NM], kraw[:, :, :], ACT.Square).then_inc(sems["km_sq"], 1)
                power(P, 4 * NM)
                act.wait_ge(sems["km_ready"], l + 1)
                act.dma_start(o_mk[bass.ds(l, 1), :, :, :].rearrange("a p c n -> (a p) c n"), kmT[:, :, :]).then_inc(stored, 16)
                act.dma_start(o_mv[bass.ds(l, 1), :, :, :].rearrange("a p c n -> (a p) c n"), vm[:, :, :]).then_inc(stored, 16)
                square_x()
                act.wait_ge(sems["xq_raw"], l + 1)
                f(sq[:, :, :], z[:, 0:8, :], ACT.Square).then_inc(sems["xq_sq"], 1)
                power(P, 4 * T)
                act.wait_ge(sems["x_in"], l + 1)
                for h in range(H):
                    for a in range(2):
                        last = f(xS[:, h, a, :], xS[:, h, a, :], ACT.Exp, bias=nmx[:, h, a:a + 1], scale=1 / 16,
                                 accum_out=psum_p[:, h, a:a + 1])
                last.then_inc(sems["x_exp"], 1)
                act.wait_ge(sems["xs_in"], l + 1)
                f(xsP, xsS, ACT.Exp, bias=xs_max[:, :], scale=1 / 16, accum_out=xs_den[:, :]).then_inc(sems["xs_exp"], 1)
                square_x()
                with act.Fori(0, U_FF1 // SLOTS) as i:
                    for t in range(8):
                        act.wait_ge(sems["ff_in"], l * 32 + i * 8 + t + 1)
                        f(ffh[:, bass.ds(i * 8 + t, 1), :], y[:, 0:1056].rearrange("p (s t) -> p s t", s=4)[:, t % 4:t % 4 + 1, :],
                          ACT.Square).then_inc(sems["ff_done"], 1)
                assert own.n == ACT_STEPS, own.n
            act.wait_ge(stored, STORES * 16 * DEPTH)

        @block.vector
        def _(dve):
            at = Counts(sems, SIGNALS)
            own = Count(dve_step, DVE_STEPS, 0)
            v = nc.vector

            def step(ins):
                ins.then_inc(dve_step, 1)
                dve.wait_ge(dve_step, own.next())

            def wait(name):
                dve.wait_ge(sems[name], at[name].next())

            def tell(name):
                dve.sem_inc(sems[name], 1)

            def tile():
                wait("tile_ready")
                return ps[:, at["tile_ready"].slot, :]

            def freed(ins):
                ins.then_inc(sems["tile_free"], 1)
                dve.wait_ge(sems["tile_free"], at["tile_free"].next())

            def refine(rows, cols, out=None):
                tell("moment")
                newton(rows, cols, out)

            def newton(rows, cols, out=None):
                wait("root")
                a, b, c = (t[0:rows, 0:cols] for t in (y, m, tmp))
                step(v.scalar_tensor_tensor(c, a, -0.5, a, ALU.mult, ALU.mult))
                step(v.tensor_tensor(c, c, b, ALU.mult))
                step(v.scalar_tensor_tensor(a if out is None else out, c, 1.5, a, ALU.add, ALU.mult))

            def norm_x(g):
                for k in range(KD):
                    v.tensor_scalar(xg[:, k, :], xT[:, k, :], gain[:, g + k:g + k + 1], None, ALU.mult).then_inc(sems["xg_ready"], 1)
                wait("x_sq")
                step(v.tensor_reduce(tmp[:, 0:T], sq[:, :, :].rearrange("p k t -> p t k"), AXX, ALU.add))
                tell("ssum_ready")
                wait("mean_ready")
                step(v.tensor_scalar(m[:, 0:T], ps[:, 4, 0:T], 1 / D, EPS, ALU.mult, ALU.add))
                refine(P, T, rB[:, :])

            def add_to_x(k):
                freed(v.tensor_tensor(xT[:, k, :], xT[:, k, :], tile()[:, 0:T], ALU.add))

            def soften(S4, width_of, name_in, name_exp):
                for a, (c0, c1) in enumerate(width_of):
                    step(v.tensor_reduce(nmx[:, :, a:a + 1], S4(c0, c1), AXX, ALU.max, negate=True))

            dve.wait_ge(once_in, 48)
            v.memset(snew[:, :, :], NEG)
            dve.sem_inc(sems["tile_free"], 4)
            dve.sem_inc(sems["pair_sc"], 2)
            dve.sem_inc(sems["pair_sum"], 2)
            dve.sem_inc(sems["lat_used"], 2)
            dve.sem_inc(sems["x_new"], 1)

            with dve.Fori(0, DEPTH) as l:
                at.layer(l)
                own.base, own.n = l * DVE_STEPS, 0
                step(v.tensor_copy(gain[:, :], gall[:, bass.ds(l, 1), :].rearrange("p a n -> p (a n)")))
                norm_x(G_MIX)

                for i in range(NZ):
                    freed(v.tensor_tensor(z[:, i, :], tile()[:, 0:T], rB[:, :], ALU.mult))
                    tell("z_ready")
                for j, n in enumerate((384, 256)):
                    freed(v.tensor_scalar(m[:, j * T:j * T + T], tile()[:, 0:T], 1 / n, EPS, ALU.mult, ALU.add))
                refine(P, 2 * T)
                for k in range(5):
                    c0 = 0 if k < 3 else T
                    step(v.scalar_tensor_tensor(z[:, k, :], z[:, k, :], gain[:, G_QL + k:G_QL + k + 1], y[:, c0:c0 + T], ALU.mult, ALU.mult))
                tell("lat_ready")

                for h in range(H):
                    freed(v.tensor_copy(qkA[0:QK, h, :], tile()[0:QK, 0:T]))
                tell("qk_raw")
                for h in range(H):
                    freed(v.tensor_copy(qkA[0:NOPE, 4 + h, :], tile()[0:NOPE, 0:T]))
                    step(v.tensor_copy(qkA[NOPE:QK, 4 + h, :], z[NOPE:QK, KR, :]))
                tell("qk_raw")
                for j, g in enumerate((G_Q, G_K)):
                    for h in range(H):
                        freed(v.tensor_scalar(m[0:QK, h * T:h * T + T], tile()[0:QK, 0:T], 1 / QK, EPS, ALU.mult, ALU.add))
                    refine(QK, 4 * T)
                    step(v.scalar_tensor_tensor(qkB[0:QK, 4 * j:4 * j + 4, :], qkA[0:QK, 4 * j:4 * j + 4, :], gain[0:QK, g:g + 1],
                                                y[0:QK, :].rearrange("p (h t) -> p h t", h=4), ALU.mult, ALU.mult))
                tell("qk_norm")
                step(v.tensor_tensor(qkA[0:QK, :, :], qkB[0:QK, :, :], cos.unsqueeze(1).broadcast_to([QK, 8, T]), ALU.mult))
                for i in range(8):
                    freed(v.tensor_tensor(tmp[0:QK, 0:T], tile()[0:QK, 0:T], sin, ALU.mult))
                    step(v.tensor_tensor(qkB[0:QK, i, :], qkA[0:QK, i, :], tmp[0:QK, 0:T], ALU.add))
                tell("qk_ready")
                step(v.tensor_scalar(qg[:, :, :], qkB[0:NOPE, 0:4, TP:T], gain[0:NOPE, G_K:G_K + 1], None, ALU.mult))
                step(v.tensor_tensor(sprod[:, :, :], qkB[0:QK, 0:4, TP:T], qkB[0:QK, 4:8, TP:T], ALU.mult))
                tell("small_ready")
                for a in range(2):
                    freed(v.tensor_copy(vp[:, a, :], tile()))
                tell("vp_ready")
                freed(v.tensor_copy(qt[:, :, :, :], tile()[:, 0:64].rearrange("p (c h b) -> p c b h", c=2, h=H)))
                t = tile()
                for j in range(4):
                    ins = v.tensor_scalar(qblk[:, :, j, :], t[:, 0:32].rearrange("p (h b) -> p b h", h=H), hm[:, j:j + 1], None, ALU.mult)
                    if j < 3:
                        step(ins)
                freed(ins)
                t = tile()
                eye = ident[0:B, 0:B].unsqueeze(2).broadcast_to([B, B, H])
                step(v.tensor_tensor(snew[0:B, :, :], t[0:B, 0:32].rearrange("p (h b) -> p b h", h=H), eye, ALU.mult))
                step(v.tensor_scalar(tmp[0:B, 0:B], ident[0:B, 0:B], -1.0, -NEG, ALU.add, ALU.mult))
                step(v.tensor_tensor(snew[0:B, :, :], snew[0:B, :, :], tmp[0:B, 0:B].unsqueeze(2).broadcast_to([B, B, H]), ALU.add))
                freed(v.tensor_copy(latn[:, :], t[0:B, 64:320]))

                for h in range(H):
                    freed(v.tensor_tensor(sS[:, h, :], tile()[:, 0:384], con[:, C_MASK:C_MASK + 384], ALU.add))
                for a, (c0, c1) in enumerate(((0, P), (P, 384))):
                    step(v.tensor_reduce(nmx[:, :, a:a + 1], sS[:, :, c0:c1], AXX, ALU.max, negate=True))
                step(v.tensor_scalar(nmx[:, :, :], nmx[:, :, :], QK ** -0.5, None, ALU.mult))
                tell("soft_in")
                wait("soft_exp")
                step(v.reciprocal(psum_p[:, :, :], psum_p[:, :, :]))
                for h in range(H):
                    for a, (c0, c1) in enumerate(((0, P), (P, 384))):
                        step(v.tensor_scalar(sS[:, h, c0:c1], sS[:, h, c0:c1], psum_p[:, h, a:a + 1], None, ALU.mult))
                tell("soft_p")
                for h in range(H):
                    freed(v.tensor_copy(pT[:, h, :], tile()[:, 0:384]))
                tell("soft_t")
                for h in range(H):
                    freed(v.tensor_copy(mix[:, h, 0:TP], tile()[:, 0:TP]))
                tell("mla_done")

                freed(v.tensor_scalar(m[:, 0:T], tile()[:, 0:T], gain[:, B_GATE:B_GATE + 1], None, ALU.add))
                tell("gate_in")
                wait("gate_soft")
                step(v.scalar_tensor_tensor(xg[:, L_A, :], m[:, 0:T], 0.0, y[:, 0:T], ALU.min, ALU.subtract))
                for c in range(4):
                    step(v.tensor_tensor_scan(xg[:, L_BC, 64 * c:64 * c + 64], ones[:, 0:64], xg[:, L_A, 64 * c:64 * c + 64],
                                              0.0, ALU.mult, ALU.add))
                step(v.tensor_scalar(bl[:, :], xg[:, L_BC, 63:256:64], 1 / 16, None, ALU.mult))
                tell("gate_la")
                wait("gate_exp")
                step(v.scalar_tensor_tensor(xg[:, L_QD, 0:TP], z[:, GQ, 0:TP], 32 ** -0.5, xg[:, L_EB, 0:TP], ALU.mult, ALU.mult))
                step(v.tensor_tensor(xg[:, L_KD, 0:TP], z[:, GK, 0:TP], xg[:, L_ENB, 0:TP], ALU.mult))
                step(v.tensor_tensor(xg[:, L_KE, 0:TP], z[:, GK, 0:TP], xg[:, L_EKE, 0:TP], ALU.mult))
                for h in range(H):
                    step(v.tensor_scalar(qbd[:, h, :], xg[:, L_QD, 0:TP], hm[:, h:h + 1], None, ALU.mult))
                    step(v.tensor_scalar(qsb[:, :, h], z[:, GQ, TP:T], hm[:, h:h + 1], 32 ** -0.5, ALU.mult, ALU.mult))
                tell("gate_dec")
                for a in range(2):
                    freed(v.tensor_copy(gvn[0:64, 2 * a:2 * a + 2, :], tile()[0:64, :].rearrange("p (c n) -> p c n", c=2)))
                freed(v.tensor_copy(gvs_n[:, :], tile()[0:B, 0:256]))
                tell("gvs_ready")
                freed(v.tensor_copy(kendn[0:64, :, :], tile()[0:64, :].rearrange("p (c n) -> p c n", c=4)))
                for a in range(2):
                    freed(v.tensor_tensor(att[0:64, 2 * a:2 * a + 2, :], tile()[0:64, :].rearrange("p (c n) -> p c n", c=2),
                                          con[0:64, C_TRI:C_TRI + 256].unsqueeze(1).broadcast_to([64, 2, 256]), ALU.mult))
                tell("gla_nat")
                bm = con[:, C_BM:C_BM + 256]
                for c in range(4):
                    if c % 2 == 0:
                        t = tile()
                    upd = t[:, 256 * (c % 2):256 * (c % 2) + 256]
                    if c == 0:
                        step(v.tensor_copy(S[:, 0, :], upd))
                    elif c % 2:
                        freed(v.scalar_tensor_tensor(S[:, c, :], S[:, c - 1, :], xg[:, L_EB, 64 * c + 63:64 * c + 64], upd, ALU.mult, ALU.add))
                    else:
                        step(v.scalar_tensor_tensor(S[:, c, :], S[:, c - 1, :], xg[:, L_EB, 64 * c + 63:64 * c + 64], upd, ALU.mult, ALU.add))
                    step(v.tensor_tensor(S[:, c, :], S[:, c, :], bm, ALU.mult))
                dve.wait_ge(gvs_in, 64 * (l + 1))
                dve.wait_ge(layer_in, 64 * (l + 1))
                step(v.tensor_tensor(gst[:, :, :], gst[:, :, :], ea[:, :].unsqueeze(2).broadcast_to([P, B, 64]), ALU.mult))
                step(v.tensor_tensor(vb[:, :, :], vb[:, :, :], z[:, GK, TP:T].unsqueeze(2).broadcast_to([P, B, 64]), ALU.mult))
                step(v.tensor_tensor(gst[:, :, :], gst[:, :, :], vb[:, :, :], ALU.add))
                tell("gla_state")
                freed(v.tensor_copy(z[:, GV:GV + 2, 0:TP], tile().rearrange("p (c t) -> p c t", c=2)))
                freed(v.tensor_copy(z[:, GV:GV + 2, TP:T], tile()[:, 0:16].rearrange("p (c t) -> p c t", c=2)))
                tell("gla_raw")
                for c in range(2):
                    freed(v.tensor_scalar(m[:, c * T:c * T + T], tile()[:, 0:T], 1 / 64, EPS, ALU.mult, ALU.add))
                refine(P, 2 * T)
                step(v.tensor_scalar(sq[:, 4:6, :], sq[:, 4:6, :], 1.0, None, ALU.add))
                step(v.reciprocal(sq[:, 4:6, :], sq[:, 4:6, :]))
                step(v.tensor_tensor(sq[:, 4:6, :], sq[:, 4:6, :], z[:, GR:GR + 2, :], ALU.mult))
                step(v.scalar_tensor_tensor(z[:, GV:GV + 2, :], z[:, GV:GV + 2, :], gain[:, G_GLA:G_GLA + 1],
                                            y[:, 0:2 * T].rearrange("p (c t) -> p c t", c=2), ALU.mult, ALU.mult))
                step(v.tensor_tensor(mix[:, 4:6, :], z[:, GV:GV + 2, :], sq[:, 4:6, :], ALU.mult))
                for c in range(2):
                    freed(v.tensor_scalar(mix[:, 6 + c, :], tile()[:, 0:T], gain[:, G_POOL + c:G_POOL + c + 1], None, ALU.mult))
                for s in range(2):
                    step(v.tensor_copy(wuq_b[:, s, :, 0:256], w_uk))
                tell("mix_side")

                def prepare(j, s):
                    b = bass.ds(j * 2 + s, 1)
                    step(v.tensor_copy(wuq_b[:, s, :, 256:260], qt[:, :, b, :].rearrange("p c b h -> p c (b h)")))
                    step(v.tensor_copy(qbs[:, s, :], qblk[:, b, :, :].rearrange("p b j h -> p (b j h)")))
                    tell("seq_in")

                def pair(s, n):
                    q = n % 2
                    wait("pair_ready")
                    wait("pair_sq")
                    v.tensor_copy(sc[:, s, 2 * n:2 * n + 2, :], ps[:, 4 + 2 * q:6 + 2 * q, 256:260]).then_inc(sems["pair_sc"], 1)
                    v.tensor_reduce(ssn[:, s, 2 * n:2 * n + 2, :], psq[:, q, :].rearrange("p (g c) -> p g c", c=64),
                                    AXX, ALU.add).then_inc(sems["pair_sum"], 1)
                    at["pair_sum"].next()

                def scores(s):
                    t = tile()
                    dve.wait_ge(sems["pair_sum"], at["pair_sum"].next(0))
                    step(v.tensor_tensor(m[:, 0:64].rearrange("p (g h) -> p g h", h=H), ssn[:, s, :, :],
                                         ssr[:, :].unsqueeze(2).broadcast_to([P, PAGES, H]), ALU.add))
                    step(v.tensor_scalar(m[:, 0:64], m[:, 0:64], 1 / QK, EPS, ALU.mult, ALU.add))
                    tell("moment")
                    freed(v.tensor_tensor(scw[:, 0:PAGES, :], sc[:, s, :, :], t[:, 0:64].rearrange("p (g h) -> p g h", h=H), ALU.add))

                def maxima(j, s):
                    newton(P, 64)
                    step(v.tensor_tensor(scw[:, 0:PAGES, :], scw[:, 0:PAGES, :], y[:, 0:64].rearrange("p (g h) -> p g h", h=H), ALU.mult))
                    step(v.tensor_copy(scw[:, PAGES, :], snew[:, bass.ds(j * 2 + s, 1), :].rearrange("p b h -> p (b h)")))
                    step(v.tensor_reduce(mxp[:, :], scw[:, :, :].rearrange("p g h -> p h g"), AXX, ALU.max))
                    tell("dec_max")

                def exponents():
                    wait("dec_amax")
                    step(v.tensor_tensor(scw[:, :, :], scw[:, :, :], mx[:, :].unsqueeze(1).broadcast_to([P, S_PAGES, H]), ALU.subtract))
                    tell("dec_in")

                def sums():
                    wait("dec_exp")
                    step(v.tensor_reduce(rs[:, :], pr[:, :, :].rearrange("p g h -> p h g"), AXX, ALU.add))
                    tell("dec_sum")

                def values(j, s):
                    t = tile()
                    step(v.reciprocal(den[:, :], t[0:H, 256:257]))
                    freed(v.tensor_scalar(o4[:, bass.ds(j * 2 + s, 1), :], t[0:H, 0:256].unsqueeze(1), den[:, :], None, ALU.mult))
                    tell("lat_used")

                def keys(j, s, before):
                    pair(s, 0)
                    if before:
                        scores(1 - s)
                    pair(s, 1)
                    if before:
                        maxima(*before)
                    pair(s, 2)
                    if before:
                        exponents()
                    pair(s, 3)
                    if before:
                        sums()
                    pair(s, 4)
                    if before:
                        values(*before)
                    pair(s, 5)
                    freed(v.tensor_scalar(krC[:, :, :], tile().rearrange("p (g n) -> p g n", g=4), gain[:, G_KR4:G_KR4 + 1], None, ALU.mult))
                    tell("kr_scaled")
                    pair(s, 6)
                    step(v.tensor_tensor(krS[:, :, :], krC[:, :, :], con[:, C_COS4:C_COS4 + 512].rearrange("p (g n) -> p g n", g=4), ALU.mult))
                    wait("kr_sq")
                    v.tensor_reduce(ssr[:, :], krQ[:, :, :], AXX, ALU.add)
                    pair(s, 7)
                    freed(v.tensor_tensor(tmp[:, 0:512], tile(), con[:, C_SIN4:C_SIN4 + 512], ALU.mult))
                    step(v.tensor_tensor(krS[:, :, :], krS[:, :, :], tmp[:, 0:512].rearrange("p (g n) -> p g n", g=4), ALU.add))
                    tell("kr_rot")

                prepare(0, 0)
                prepare(0, 1)
                keys(0, 0, None)
                with dve.Fori(0, B // 2 - 1) as i:
                    at.enter(i, tile_ready=8, tile_free=8, pair_ready=16, pair_sq=16, pair_sum=16, kr_sq=2, root=2, dec_amax=2, dec_exp=2)
                    base, n = own.base, own.n
                    own.base, own.n = base + n + i * DEC_STEPS, 0
                    keys(i, 1, (i, 0))
                    prepare(i + 1, 0)
                    keys(i + 1, 0, (i, 1))
                    prepare(i + 1, 1)
                    assert own.n == DEC_STEPS, own.n
                at.leave(B // 2 - 1)
                own.base, own.n = base, n + (B // 2 - 1) * DEC_STEPS
                last = B // 2 - 1
                keys(last, 1, (last, 0))
                scores(1)
                maxima(last, 1)
                exponents()
                sums()
                values(last, 1)
                tell("dec_out")
                freed(v.tensor_copy(olat[:, :, :, :], tile()[:, 0:64].rearrange("p (c b h) -> p c b h", c=2, b=B)))
                tell("olat_ready")
                freed(v.tensor_copy(mix[:, 0:4, TP:T], tile()[:, 0:32].rearrange("p (h b) -> p h b", h=H)))
                tell("mix_ready")

                wait("mem_sq")
                step(v.tensor_reduce(tmp[:, 0:NM], sq[:, :, 0:NM].rearrange("p k t -> p t k"), AXX, ALU.add))
                tell("ssum_ready")
                for k in range(KD):
                    step(v.tensor_scalar(mg[:, k, 0:NM], mg[:, k, 0:NM], gain[:, G_MEM + k:G_MEM + k + 1], None, ALU.mult))
                tell("mg_ready")
                freed(v.tensor_scalar(m[:, 0:NM + 2], tile()[:, 0:NM + 2], 1 / D, EPS, ALU.mult, ALU.add))
                refine(P, NM + 2, rBm[:, :])
                for i in range(8):
                    freed(v.tensor_tensor(kraw[:, i, :], tile()[:, 0:NM], rBm[:, 0:NM], ALU.mult))
                tell("km_raw")
                for h in range(H):
                    for a in range(2):
                        freed(v.tensor_scalar(vm[:, a, 256 * h:256 * h + 256], tile()[:, 0:256], rBm[:, NM + a:NM + a + 1], None, ALU.mult))
                for h in range(H):
                    freed(v.tensor_scalar(m[:, h * NM:h * NM + NM], tile()[:, 0:NM], 1 / 256, EPS, ALU.mult, ALU.add))
                refine(P, 4 * NM)
                for i in range(8):
                    step(v.scalar_tensor_tensor(kmT[:, i, :], kraw[:, i, :], gain[:, G_XK + i % 2:G_XK + i % 2 + 1],
                                                y[:, (i // 2) * NM:(i // 2) * NM + NM], ALU.mult, ALU.mult))
                tell("km_ready")
                for k in range(KD):
                    add_to_x(k)
                tell("x_new")

                norm_x(G_XA)
                dve.wait_ge(stored, 16 * STORES * (l + 1))
                for i in range(8):
                    freed(v.tensor_tensor(z[:, i, :], tile()[:, 0:T], rB[:, :], ALU.mult))
                tell("xq_raw")
                for h in range(H):
                    freed(v.tensor_scalar(m[:, h * T:h * T + T], tile()[:, 0:T], 1 / 256, EPS, ALU.mult, ALU.add))
                refine(P, 4 * T)
                for i in range(8):
                    step(v.scalar_tensor_tensor(z[:, i, :], z[:, i, :], gain[:, G_XQ + i % 2:G_XQ + i % 2 + 1],
                                                y[:, (i // 2) * T:(i // 2) * T + T], ALU.mult, ALU.mult))
                tell("xq_ready")
                step(v.memset(hot, 0.0))
                step(v.tensor_copy(hot_diag.rearrange("p n (b h) -> p n b h", b=B), z[:, 0:8, TP:T].rearrange("p (h c) b -> p c b h", h=H)))
                tell("hot_q")
                for h in range(H):
                    freed(v.tensor_copy(xS[:, h, :, :], tile().rearrange("p (a n) -> p a n", a=2)))
                step(v.tensor_reduce(nmx[:, :, :], xS[:, :, :, :], AXX, ALU.max, negate=True))
                step(v.tensor_scalar(nmx[:, :, :], nmx[:, :, :], 1 / 16, None, ALU.mult))
                tell("x_in")
                wait("x_exp")
                step(v.reciprocal(psum_p[:, :, :], psum_p[:, :, :]))
                for h in range(H):
                    for a in range(2):
                        step(v.tensor_scalar(xS[:, h, a, :], xS[:, h, a, :], psum_p[:, h, a:a + 1], None, ALU.mult))
                tell("x_p")
                freed(v.tensor_copy(xsS, tile()[0:B * H, 0:NM]))
                step(v.tensor_reduce(xs_max[:, :], xsS, AXX, ALU.max, negate=True))
                step(v.tensor_scalar(xs_max[:, :], xs_max[:, :], 1 / 16, None, ALU.mult))
                tell("xs_in")
                for h in range(H):
                    freed(v.tensor_copy(xP[:, h, :, :], tile().rearrange("p (a n) -> p a n", a=2)))
                tell("x_t")
                for h in range(H):
                    freed(v.tensor_copy(mix[:, 2 * h:2 * h + 2, 0:TP], tile().rearrange("p (a n) -> p a n", a=2)))
                freed(v.tensor_copy(hot_diag, tile()[:, 0:64].rearrange("p (n j) -> p n j", n=2)))
                tell("hot_p")
                step(v.reciprocal(xs_den[:, :], xs_den[:, :]))
                freed(v.tensor_scalar(xsO, tile()[0:B * H, 0:256], xs_den[:, :], None, ALU.mult))
                tell("xs_out")
                t = tile()[:, 0:64].rearrange("p (c b h) -> p h c b", c=2, b=B)
                for h in range(H):
                    ins = v.tensor_copy(mix[:, 2 * h:2 * h + 2, TP:T], t[:, h, :, :])
                    if h < H - 1:
                        step(ins)
                freed(ins)
                tell("xo_ready")
                for k in range(KD):
                    add_to_x(k)
                tell("x_new")

                norm_x(G_MLP)
                dve.sem_inc(passed["dve"], 1)
                hid = y[:, 0:1056].rearrange("p (s t) -> p s t", s=4)
                with dve.Fori(0, U_FF1 // SLOTS) as i:
                    at.enter(i, tile_ready=8, tile_free=8, ff_done=8)
                    for t in range(8):
                        dve.wait_ge(sems["ff_done"], at["ff_done"].free())
                        freed(v.scalar_tensor_tensor(hid[:, t % 4, :], tile()[:, 0:T], 0.0, rB[:, :], ALU.max, ALU.mult))
                        tell("ff_in")
                at.leave(U_FF1 // SLOTS)
                with dve.Fori(0, 2) as i:
                    at.enter(i, tile_ready=4, tile_free=4)
                    for k in range(4):
                        t = tile()
                        x_k = xT[:, bass.ds(i * 4 + k, 1), :]
                        freed(v.tensor_tensor(x_k, x_k, t[:, 0:T].unsqueeze(1), ALU.add))
                at.leave(2)
                tell("x_new")

                assert own.n == DVE_STEPS, own.n

        @block.tensor
        def _(pe):
            at = Counts(sems, SIGNALS)
            mm = nc.tensor.matmul

            def wait(name):
                pe.wait_ge(sems[name], at[name].next())

            def bank():
                pe.wait_ge(sems["tile_free"], at["tile_free"].free())
                return ps[:, at["tile_free"].slot, :]

            owed = []

            def settle():
                while owed:
                    pe.wait_ge(sems["tile_ready"], owed.pop())
                    pe.sem_inc(sems["unit_used"], 1)

            def ready(ins, unit=False):
                ins.then_inc(sems["tile_ready"], 1)
                settle()
                n = at["tile_ready"].next()
                if unit:
                    owed.append(n)

            def unit():
                n = at["unit_used"].next()
                s = at["unit_used"].slot
                pe.wait_ge(unit_in[s], (n - SLOTS + (SLOTS - 1 - s)) * (16 // SLOTS))
                return ring[:, s, :]

            def used(ins):
                ins.then_inc(sems["unit_used"], 1)

            def product(out, pairs):
                for i, (a, b) in enumerate(pairs):
                    ins = mm(out, a, b, start=i == 0, stop=i == len(pairs) - 1)
                return ins

            def mean_x():
                wait("ssum_ready")
                product(ps[:, 4, 0:T], [(ones[:, :], tmp[:, 0:T])]).then_inc(sems["mean_ready"], 1)

            def normed_projection(n_units, tiles_last=2):
                for i in range(n_units):
                    tiles = tiles_last if i == n_units - 1 else 2
                    u = unit().rearrange("p (a k n) -> p a k n", a=2, k=KD)
                    for a in range(tiles):
                        t = bank()
                        for k in range(KD):
                            if i == 0 and a == 0:
                                wait("xg_ready")
                            ins = mm(t[:, 0:T], u[:, a, k, :], xg[:, k, :], start=k == 0, stop=k == KD - 1)
                        ready(ins, a == tiles - 1)
                    if i == 0:
                        mean_x()

            pe.sem_inc(sems["unit_used"], SLOTS)
            pe.sem_inc(sems["pair_ready"], PAGES // 2)
            pe.wait_ge(once_in, 48)
            with pe.Fori(0, DEPTH) as l:
                at.layer(l)
                normed_projection(U_IN, 1)
                wait("lat_sq")
                ready(product(bank()[:, 0:T], [(ones[:, :], xg[:, k, :]) for k in range(3)]))
                ready(product(bank()[:, 0:T], [(ones[:, :], xg[:, k, :]) for k in range(3, 5)]))
                pe.wait_ge(layer_in, 64 * (l + 1))
                wait("lat_ready")
                for h in range(H):
                    ready(product(bank()[0:QK, 0:T], [(w_uq[:, c, h, :], z[:, CQ + c, :]) for c in range(3)]))
                for h in range(H):
                    ready(product(bank()[0:NOPE, 0:T], [(w_uk[:, c, h * NOPE:h * NOPE + NOPE], z[:, CKV + c, :]) for c in range(2)]))
                for j in range(2):
                    wait("qk_sq")
                    for h in range(H):
                        ready(product(bank()[0:QK, 0:T], [(ones[0:QK, 0:QK], sq[0:QK, 4 * j + h, :])]))
                wait("qk_norm")
                for i in range(8):
                    ready(product(bank()[0:QK, 0:T], [(swap[0:QK, 0:QK], qkB[0:QK, i, :])]))
                for a in range(2):
                    ready(product(bank(), [(z[:, CKV + c, P * a:P * a + P], w_uv[:, c, :]) for c in range(2)]))
                wait("small_ready")
                t = bank()
                for c in range(2):
                    for h in range(H):
                        o = (c * H + h) * B
                        ins = mm(t[:, o:o + B], w_ukt[0:NOPE, h, P * c:P * c + P], qg[:, h, :], start=True, stop=True)
                ready(ins)
                ready(product(bank()[:, 0:32], [(rep[0:QK, :], qkB[0:QK, 0:4, TP:T])]))
                t = bank()
                mm(t[0:B, 0:32], ones[0:QK, 0:B], sprod[:, :, :], start=True, stop=True)
                for c in range(2):
                    ins = nc.tensor.transpose(t[0:B, 64 + P * c:64 + P * c + P], z[:, CKV + c, TP:T], ident)
                ready(ins)
                wait("qk_ready")
                for h in range(H):
                    t = bank()
                    mm(t[:, 0:P], qkB[0:QK, h, 0:P], qkB[0:QK, 4 + h, 0:P], start=True, stop=True)
                    ready(mm(t[:, P:384], qkB[0:QK, h, P:TP], qkB[0:QK, 4 + h, 0:TP], start=True, stop=True))
                wait("soft_p")
                for h in range(H):
                    t = bank()
                    for a in range(3):
                        ins = nc.tensor.transpose(t[:, P * a:P * a + P], sS[:, h, P * a:P * a + P], ident)
                    ready(ins)
                wait("vp_ready")
                wait("soft_t")
                for h in range(H):
                    t = bank()
                    mm(t[:, 0:TP], vp[:, 0, P * h:P * h + P], pT[:, h, 0:TP], start=True, stop=False)
                    ready(mm(t[:, P:TP], vp[:, 1, P * h:P * h + P], pT[:, h, TP:384], start=False, stop=True))

                ready(product(bank()[:, 0:T], [(mat[0:16, M_GATE:M_GATE + P], z[0:16, GLOW, :])]))
                for a in range(2):
                    t = bank()
                    pe.sem_inc(passed["pe"], 1)
                    for c in range(2):
                        for k in range(2):
                            o = c * 256 + k * P
                            ins = nc.tensor.transpose(t[0:64, o:o + P], z[:, GV + k, (2 * a + c) * 64:(2 * a + c) * 64 + 64], ident)
                    ready(ins)
                t = bank()
                pe.sem_inc(passed["pe"], 1)
                for k in range(2):
                    ins = nc.tensor.transpose(t[0:B, k * P:k * P + P], z[:, GV + k, TP:T], ident)
                ready(ins)
                wait("gate_dec")
                t = bank()
                pe.sem_inc(passed["pe"], 1)
                for c in range(4):
                    ins = nc.tensor.transpose(t[0:64, c * P:c * P + P], xg[:, L_KE, 64 * c:64 * c + 64], ident)
                ready(ins)
                for a in range(2):
                    t = bank()
                    for c in range(2):
                        o = 64 * (2 * a + c)
                        ins = mm(t[0:64, 256 * c:256 * c + 256], xg[:, L_KD, o:o + 64], qbd[:, :, o:o + 64], start=True, stop=True)
                    ready(ins)
                wait("gla_nat")
                for a in range(2):
                    t = bank()
                    for c in range(2):
                        ins = mm(t[:, 256 * c:256 * c + 256], kendn[0:64, 2 * a + c, :], gvn[0:64, 2 * a + c, :], start=True, stop=True)
                    ready(ins)
                wait("gla_state")
                t = bank()
                pe.sem_inc(passed["pe"], 1)
                for k in range(2):
                    for c in range(4):
                        o = k * TP + 64 * c
                        if c:
                            mm(t[:, o:o + 64], S[:, c - 1, P * k:P * k + P], xg[:, L_QD, 64 * c:64 * c + 64], start=True, stop=True)
                        for j in range(2):
                            h = 2 * k + j
                            ins = mm(t[64 * j:64 * j + 64, o:o + 64], gvn[0:64, c, 64 * h:64 * h + 64], att[0:64, c, 64 * h:64 * h + 64],
                                     start=c == 0, stop=True, skip_group_check=True)
                ready(ins)
                t = bank()
                for b in range(B):
                    for j in range(2):
                        ins = mm(t[64 * j:64 * j + 64, b:16:B], gst[:, b, :], qsb[:, b, j:4:2], start=True, stop=True)
                ready(ins)
                wait("gla_sq")
                for c in range(2):
                    ready(product(bank()[:, 0:T], [(b64, sq[:, c, :])]))
                wait("pooled_ready")
                for c in range(2):
                    ready(product(bank()[:, 0:T], [(w_pool[:, c, :], pooled[:, c, :])]))

                def pair(j, s, n):
                    q = n % 2
                    pe.wait_ge(sems["pair_sq"], at["pair_sq"].free())
                    pe.wait_ge(sems["pair_sc"], at["pair_sc"].free())
                    if n % 2 == 0:
                        pe.wait_ge(lt_in[n // 2], 64 * (l * B + j * 2 + s + 1))
                    for pg in (2 * n, 2 * n + 1):
                        ins = product(ps[:, 4 + 2 * q + pg % 2, 0:260],
                                      [(latT[:, pg, P * c:P * c + P], wuq_b[:, s, c, :]) for c in range(2)])
                    ins.then_inc(sems["pair_ready"], 1)

                def values(j, s):
                    wait("dec_sum")
                    pe.wait_ge(lat_in[s], 16 * PAGES * (l * (B // 2) + j + 1))
                    t = bank()
                    pe.sem_inc(passed["pe"], 1)
                    product(t[0:H, 0:256], [(pr[:, pg, :], lat[:, s, pg, 0:256]) for pg in range(PAGES)] + [(pr[0:B, PAGES, :], latn[:, :])])
                    ready(mm(t[0:H, 256:257], rs[:, :], ones[:, 0:1], start=True, stop=True))

                def keys(j, s, before):
                    wait("seq_in")
                    pair(j, s, 0)
                    if before:
                        rotary(1 - s)
                    for n in range(1, 5):
                        pair(j, s, n)
                    if before:
                        values(*before)
                    pair(j, s, 5)
                    pe.wait_ge(sems["kr_sq"], at["kr_sq"].next())
                    t = bank()
                    for g in range(4):
                        ins = nc.tensor.transpose(t[:, P * g:P * g + P], krN[:, 4 * g:4 * g + 4, :], ident)
                    ready(ins)
                    pair(j, s, 6)
                    pair(j, s, 7)
                    pe.wait_ge(sems["kr_scaled"], at["kr_scaled"].next())
                    ready(product(bank(), [(swap4, krC[:, :, :])]))

                def rotary(s):
                    wait("kr_rot")
                    t = bank()
                    for g in range(4):
                        ins = mm(t[:, 16 * g:16 * g + 16], krS[:, g, :], qbs[:, s, :], start=True, stop=True)
                    ready(ins)

                keys(0, 0, None)
                with pe.Fori(0, B // 2 - 1) as i:
                    at.enter(i, tile_free=8, tile_ready=8, pair_sq=16, pair_sc=16, seq_in=2, kr_sq=2, kr_scaled=2, kr_rot=2, dec_sum=2)
                    keys(i, 1, (i, 0))
                    keys(i + 1, 0, (i, 1))
                at.leave(B // 2 - 1)
                last = B // 2 - 1
                keys(last, 1, (last, 0))
                rotary(1)
                values(last, 1)
                wait("dec_out")
                t = bank()
                pe.sem_inc(passed["pe"], 1)
                for c in range(2):
                    for b in range(B):
                        o = (c * B + b) * H
                        ins = nc.tensor.transpose(t[:, o:o + H], o4[:, b, P * c:P * c + P], ident[0:H, 0:H])
                ready(ins)
                wait("olat_ready")
                t = bank()
                for h in range(H):
                    ins = product(t[:, B * h:B * h + B], [(w_uv[:, c, P * h:P * h + P], olat[:, c, :, h]) for c in range(2)])
                ready(ins)

                wait("ssum_ready")
                t = bank()
                mm(t[:, 0:NM], ones[:, :], tmp[:, 0:NM], start=True, stop=True)
                for a in range(2):
                    ins = mm(t[:, NM + a:NM + a + 1], tmp[:, P * a:P * a + P], ones[:, 0:1], start=True, stop=True)
                ready(ins)
                wait("mg_ready")
                for i in range(U_MK):
                    u = unit().rearrange("p (a k n) -> p a k n", a=2, k=KD)
                    for a in range(2):
                        ready(product(bank()[:, 0:NM], [(u[:, a, k, :], mg[:, k, 0:NM]) for k in range(KD)]), a == 1)
                for h in range(U_MV):
                    u = unit().rearrange("p (k n) -> p k n", k=KD)
                    for a in range(2):
                        ready(product(bank()[:, 0:256], [(mg[:, k, P * a:P * a + P], u[:, k, :]) for k in range(KD)]), a == 1)
                wait("km_sq")
                for h in range(H):
                    ready(product(bank()[:, 0:NM], [(ones[:, :], sq[:, 2 * h + c, 0:NM]) for c in range(2)]))
                wait("mix_ready")

                def mixed():
                    for i in range(4):
                        u = unit().rearrange("p (a k n) -> p a k n", a=2, k=KD)
                        for a in range(2):
                            ready(product(bank()[:, 0:T], [(u[:, a, k, :], mix[:, k, :]) for k in range(KD)]), a == 1)

                mixed()
                normed_projection(U_XQ)
                wait("xq_sq")
                for h in range(H):
                    ready(product(bank()[:, 0:T], [(ones[:, :], sq[:, 2 * h + c, :]) for c in range(2)]))
                wait("xq_ready")
                pe.wait_ge(sems["km_ready"], l + 1)
                for h in range(H):
                    t = bank()
                    for a in range(2):
                        ins = product(t[:, NM * a:NM * a + NM], [(z[:, 2 * h + c, P * a:P * a + P], kmT[:, 2 * h + c, :]) for c in range(2)])
                    ready(ins)
                wait("hot_q")
                t = bank()
                for b in range(B):
                    u = unit().rearrange("p (k n) -> p k n", k=KD)
                    for k in range(KD):
                        if k == 4:
                            settle()
                        ins = mm(t[0:B * H, 0:NM], hot[:, k % 2, b * H + k // 2, :], u[:, k, :], start=b + k == 0,
                                 stop=b + k == B - 1 + KD - 1)
                    if b < B - 1:
                        ins.then_inc(sems["unit_used"], 1)
                ready(ins, True)
                wait("x_p")
                for h in range(H):
                    t = bank()
                    for n in range(2):
                        for a in range(2):
                            o = n * NM + a * P
                            ins = nc.tensor.transpose(t[:, o:o + P], xS[:, h, a, P * n:P * n + P], ident)
                    ready(ins)
                wait("x_t")
                for h in range(H):
                    t = bank()
                    for c in range(2):
                        o = h * 256 + c * P
                        ins = product(t[:, TP * c:TP * c + TP], [(vm[:, n, o:o + P], xP[:, h, n, :]) for n in range(2)])
                    ready(ins)
                wait("xs_exp")
                t = bank()
                pe.sem_inc(passed["pe"], 1)
                for n in range(2):
                    ins = nc.tensor.transpose(t[:, B * H * n:B * H * n + B * H], xsP[:, P * n:P * n + P], ident[0:B * H, 0:B * H])
                ready(ins)
                wait("hot_p")
                t = bank()
                for b in range(B):
                    u = unit().rearrange("p (n h d) -> p n h d", n=2, h=H)
                    for n in range(2):
                        if n == 1:
                            settle()
                        for h in range(H):
                            ins = mm(t[0:B * H, 0:256], hot[:, n, b * H + h, :], u[:, n, h, :], start=b + n + h == 0,
                                     stop=b + n + h == B - 1 + 1 + H - 1)
                    if b < B - 1:
                        ins.then_inc(sems["unit_used"], 1)
                ready(ins, True)
                wait("xs_out")
                t = bank()
                pe.sem_inc(passed["pe"], 1)
                for c in range(2):
                    ins = nc.tensor.transpose(t[:, B * H * c:B * H * c + B * H], xsO[:, P * c:P * c + P], ident[0:B * H, 0:B * H])
                ready(ins)
                wait("xo_ready")
                mixed()

                normed_projection(SLOTS)
                settle()
                with pe.Fori(0, U_FF1 // SLOTS - 1) as i:
                    at.enter(i, tile_free=8, tile_ready=8, unit_used=SLOTS)
                    for j in range(SLOTS):
                        u = unit().rearrange("p (a k n) -> p a k n", a=2, k=KD)
                        for a in range(2):
                            ready(product(bank()[:, 0:T], [(u[:, a, k, :], xg[:, k, :]) for k in range(KD)]), a == 1)
                    settle()
                at.leave(U_FF1 // SLOTS - 1)
                settle()
                with pe.Fori(0, 2) as i:
                    at.enter(i, tile_free=4, tile_ready=4, unit_used=8)
                    for pair in range(2):
                        two = [bank(), bank()]
                        for g in range(4):
                            pe.wait_ge(sems["ff_done"], 32 * l + 8 * g + 12)
                            u = unit().rearrange("p (a k n) -> p a k n", a=2, k=KD)
                            for a in range(2):
                                for k in range(KD):
                                    ins = mm(two[a][:, 0:T], u[:, a, k, :], ffh[:, 8 * g + k, :], start=g == 0 and k == 0,
                                             stop=g == 3 and k == KD - 1)
                                if g == 3:
                                    ready(ins, a == 1)
                                elif a == 0:
                                    settle()
                            if g < 3:
                                ins.then_inc(sems["unit_used"], 1)
                    settle()
                at.leave(2)

                at.end_layer()


def _constants():
    import numpy as np
    c = np.zeros((P, NC), np.float32)
    p = np.arange(P)
    c[:, C_ID:C_ID + P] = np.eye(P)
    mask = np.where(p[None, :] <= p[:, None], 0.0, NEG)
    c[:, C_MASK:C_MASK + P] = mask
    c[:, C_MASK + 2 * P:C_MASK + 3 * P] = mask
    c[:, C_B64:C_B64 + P] = p[:, None] // 64 == p[None, :] // 64
    c[:, C_REP:C_REP + P] = p[:, None] == NOPE + p[None, :] % ROPE

    def swapped(n, first):
        m = np.zeros((P, P), np.float32)
        for g in range(first, n, ROPE):
            for i in range(ROPE // 2):
                m[g + ROPE // 2 + i, g + i] = -1
                m[g + i, g + ROPE // 2 + i] = 1
        return m

    c[:, C_SWAP:C_SWAP + P] = swapped(QK, NOPE)
    c[:, C_SWAP4:C_SWAP4 + P] = swapped(P, 0)
    half = ROPE // 2
    inv = np.float32(10000.0) ** (-np.arange(half, dtype=np.float32) / np.float32(half))
    pos = np.concatenate([np.arange(TP), np.full(B, PG * PAGES)]).astype(np.float32)
    ang = inv[np.arange(ROPE) % half][:, None] * pos[None, :]
    c[0:NOPE, C_COS:C_COS + T] = 1
    c[NOPE:QK, C_COS:C_COS + T] = np.cos(ang)
    c[NOPE:QK, C_SIN:C_SIN + T] = np.sin(ang)
    old = (PG * (4 * np.arange(4)[None, :, None] + (p // ROPE)[:, None, None]) + p[None, None, :]).astype(np.float32)
    ang = inv[p % half][:, None, None] * old
    c[:, C_COS4:C_COS4 + 512] = np.cos(ang).reshape(P, 512)
    c[:, C_SIN4:C_SIN4 + 512] = np.sin(ang).reshape(P, 512)
    c[:, C_HM:C_HM + 4] = p[:, None] // 32 == np.arange(4)[None, :]
    c[:, C_BM:C_BM + 256] = p[:, None] // 32 == np.arange(256)[None, :] // 64
    c[:, C_TRI:C_TRI + 256] = p[:, None] <= np.arange(256)[None, :] % 64
    t = np.concatenate([np.arange(TP), np.full(B, PG * PAGES)])
    for g, w in enumerate((2, 4, 8, 16)):
        c[64 * (g % 2):64 * (g % 2) + 64, C_INV + (g // 2) * T:C_INV + (g // 2 + 1) * T] = 1 / np.minimum(w, t + 1)
    return c


def kernel(**inputs):
    import numpy as np
    import concourse.bacc as _bacc
    from concourse import mybir as _mybir
    from concourse.bass_utils import run_bass_kernel_spmd as _run

    a = {k: np.asarray(v) for k, v in inputs.items()}
    f32 = np.float32

    def columns(v, n):
        return v.reshape(DEPTH, n, P).transpose(0, 2, 1)

    def tiled(w):
        k, n = w.shape[1:]
        v = w.reshape(DEPTH, k // D, KD, P, n // 256, 2, P)
        return v.transpose(0, 4, 1, 3, 5, 2, 6).reshape(DEPTH, -1, P, UNIT)

    off = np.cumsum([0, 384, 256, 32, 128, 128, 256, 16, 256, 256])
    w_in = np.zeros((DEPTH, D, 16 * P), f32)
    for tile, part, shift in ((CQ, 0, 0), (CKV, 1, 0), (KR, 2, NOPE), (GQ, 3, 0), (GK, 4, 0), (GV, 5, 0), (GLOW, 6, 0), (GR, 7, 0), (UU, 8, 0)):
        w = a["w_in"][:, :, off[part]:off[part + 1]]
        w_in[:, :, tile * P + shift:tile * P + shift + w.shape[2]] = w
    w_xv = a["w_xv"].reshape(DEPTH, KD, P, H, 256).transpose(0, 3, 2, 1, 4).reshape(DEPTH, H, P, UNIT)
    xk = a["cache_mem_k"].transpose(1, 0, 3, 4, 2).reshape(DEPTH, B, H * 2, P, NM).transpose(0, 1, 3, 2, 4).reshape(DEPTH, B, P, UNIT)
    xv = a["cache_mem_v"].transpose(1, 0, 2, 3, 4).reshape(DEPTH, B, 2, P, D).transpose(0, 1, 3, 2, 4).reshape(DEPTH, B, P, UNIT)
    units = np.concatenate([tiled(w_in), tiled(a["w_xk"]), w_xv, tiled(a["w_out"]), tiled(a["w_xq"]), xk, xv, tiled(a["w_xo"]),
                            tiled(a["w_ff1"]), tiled(a["w_ff2"])], axis=1).reshape(DEPTH * UNITS, P, UNIT)

    x = np.concatenate([a["x_prompt"].reshape(TP, D), a["x_sample"].reshape(B, D)])
    xt = x.reshape(T, KD, P).transpose(2, 1, 0)
    memt = a["mem_prompt"].reshape(NM, KD, P).transpose(2, 1, 0)
    lat = a["cache_mla_latent"]
    n_phys = lat.shape[0]
    lat_t = lat.transpose(0, 1, 3, 2).reshape(n_phys, DEPTH, 2, P, PG).transpose(0, 1, 3, 2, 4).reshape(n_phys, DEPTH, P, 256)
    pages = np.concatenate([lat_t, lat, a["cache_mla_krope"]], axis=3).reshape(n_phys * DEPTH, P, 544)
    table = a["page_table"].reshape(1, B * PAGES)

    gains = np.zeros((DEPTH, P, NG), f32)
    for c, name, n in ((G_MIX, "norm_mix", 8), (G_XA, "norm_xa", 8), (G_MLP, "norm_mlp", 8), (G_MEM, "norm_mem", 8), (G_QL, "g_q_lat", 3),
                       (G_KV, "g_kv_lat", 2), (B_GATE, "b_gate", 1), (G_POOL, "pool_scale", 2), (G_XQ, "g_xq", 2), (G_XK, "g_xk", 2)):
        gains[:, :, c:c + n] = columns(a[name], n)
    gains[:, 0:QK, G_Q] = a["g_qk_q"]
    gains[:, 0:QK, G_K] = a["g_qk_k"]
    gains[:, :, G_KR4] = np.tile(a["g_qk_k"][:, NOPE:], (1, 4))
    gains[:, :, G_GLA] = np.tile(a["g_gla_out"], (1, 2))
    gains = gains.transpose(1, 0, 2)

    mats = np.zeros((DEPTH, P, NMAT), f32)
    mats[:, :, M_UQ:M_UQ + 1152] = a["w_uq"].reshape(DEPTH, 3, P, H * QK).transpose(0, 2, 1, 3).reshape(DEPTH, P, -1)
    mats[:, :, M_UK:M_UK + 512] = a["w_uk"].reshape(DEPTH, 2, P, 256).transpose(0, 2, 1, 3).reshape(DEPTH, P, -1)
    mats[:, :, M_UV:M_UV + 1024] = a["w_uv"].reshape(DEPTH, 2, P, 512).transpose(0, 2, 1, 3).reshape(DEPTH, P, -1)
    mats[:, 0:NOPE, M_UKT:M_UKT + 1024] = a["w_uk"].transpose(0, 3, 2, 1).reshape(DEPTH, NOPE, 1024)
    mats[:, 0:16, M_GATE:M_GATE + P] = a["w_gate_up"]
    for g in range(4):
        r = 64 * (g % 2)
        o = M_POOL + (g // 2) * P + r
        mats[:, r:r + 64, o:o + 64] = a["w_pool"][:, g]

    gstate = a["state_gla"].reshape(B, DEPTH, P, 64).transpose(1, 2, 0, 3)
    pstate = a["state_pool"].transpose(1, 3, 0, 2).reshape(DEPTH, 2, P, B, 15).transpose(0, 2, 1, 3, 4)
    pstate_nat = a["state_pool"].transpose(1, 0, 2, 3)[:, :, 1:]

    nc = _bacc.Bacc("TRN2", target_bir_lowering=False, num_devices=1, dynamic_dma_scratch_size=8192)
    arrays, args = {}, []
    for name, v in dict(units=units, xt=xt, memt=memt, pages=pages, table=table, gains=gains, mats=mats,
                        consts=_constants(), gstate=gstate, pstate=pstate, pstate_nat=pstate_nat).items():
        v = np.ascontiguousarray(v)
        arrays[f"in_{name}"] = v
        args.append(nc.dram_tensor(f"in_{name}", v.shape, _mybir.dt.from_np(v.dtype), kind="ExternalInput").ap())
    outs = dict(y=(P, KD, T), lat=(DEPTH, P, 2, T), kr=(DEPTH, ROPE, T), glap=(DEPTH, P, 256), glas=(DEPTH, P, B, 64), u=(DEPTH, P, 2, T),
                pool=(DEPTH, B, 14, 256), mk=(DEPTH, P, 8, NM), mv=(DEPTH, P, 2, D))
    for name, shape in outs.items():
        args.append(nc.dram_tensor(f"out_{name}", shape, FP32, kind="ExternalOutput").ap())
    args.append(nc.dram_tensor("gla_values", (B, 256), FP32, kind="Internal").ap())
    decoder(nc, *args)
    r = _run(nc, [arrays], core_ids=[0]).results[0]
    o = {name: r[f"out_{name}"] for name in outs}

    y = o["y"].transpose(2, 1, 0).reshape(T, D)
    latent = o["lat"].transpose(0, 3, 2, 1).reshape(DEPTH, T, 256)
    kr = o["kr"].transpose(0, 2, 1)
    u = o["u"].transpose(0, 3, 2, 1).reshape(DEPTH, T, 256)
    glap = np.stack([o["glap"][:, 32 * h:32 * h + 32, 64 * h:64 * h + 64] for h in range(H)], axis=1)
    glas = o["glas"].reshape(DEPTH, H, 32, B, 64).transpose(3, 0, 1, 2, 4)
    mk = o["mk"].transpose(0, 3, 2, 1).reshape(1, DEPTH, NM, H, 256)
    mv = o["mv"].transpose(0, 2, 1, 3).reshape(1, DEPTH, NM, H, 256)
    pool_s = np.concatenate([o["pool"].transpose(1, 0, 2, 3), u[:, TP:].transpose(1, 0, 2)[:, :, None]], axis=2)
    return (y[None, :TP], y[TP:, None], latent[None, :, :TP], kr[None, :, :TP], glap[None], u[None, :, TP - 15:TP], mk, mv,
            latent[:, TP:].transpose(1, 0, 2)[:, :, None], kr[:, TP:].transpose(1, 0, 2)[:, :, None], glas, pool_s)
```

```python
import concourse.bass as bass
from concourse import mybir
from contextlib import ExitStack

FP32, F32R = mybir.dt.float32, mybir.dt.float32r
ALU = mybir.AluOpType
ACT = mybir.ActivationFunctionType
AXX = mybir.AxisListType.X
DEPTH, D, P = 2, 1024, 128
KD = D // P
TP, B = 256, 8
T = TP + B
H = 4
NOPE, ROPE = 64, 32
QK = NOPE + ROPE
PG, PAGES = 128, 16
S_PAGES = PAGES + 1
NM = 256
EPS = 1e-6
NEG = -1e30
SLOTS = 4
UNIT = 2048
U_IN, U_MK, U_MV, U_OUT, U_XQ, U_XK, U_XV, U_XO, U_FF1, U_FF2 = 8, 4, 4, 4, 4, 8, 8, 4, 16, 16
UNITS = U_IN + U_MK + U_MV + U_OUT + U_XQ + U_XK + U_XV + U_XO + U_FF1 + U_FF2
SPLIT = UNITS - U_XK - U_XV
CQ, CKV, KR, GQ, GK, GV, GLOW, GR, UU, NZ = 0, 3, 5, 6, 7, 8, 10, 11, 13, 15
G_MIX, G_XA, G_MLP, G_MEM, G_QL, G_KV, G_Q, G_K, G_KR4, B_GATE, G_GLA, G_POOL, G_XQ, G_XK, NG = \
    0, 8, 16, 24, 32, 35, 37, 38, 39, 40, 41, 42, 44, 46, 48
M_UQ, M_UK, M_UV, M_UKT, M_GATE, M_POOL, NMAT = 0, 1152, 1664, 2688, 3712, 3840, 4096
C_ID, C_MASK, C_B64, C_REP, C_SWAP, C_SWAP4, C_COS, C_SIN, C_COS4, C_SIN4, C_HM, C_BM, C_TRI, C_INV, C_BAND, NC = \
    0, 128, 512, 640, 768, 896, 1024, 1288, 1552, 2064, 2576, 2580, 2836, 3092, 3620, 3844


class Count:

    def __init__(self, sem, per_layer, start):
        self.sem, self.per_layer, self.start = sem, per_layer, start
        self.base, self.n, self.done = start, 0, 0

    def next(self, k=1):
        self.n += k
        return self.base + self.n

    def free(self, k=1):
        return self.next(k) - self.start

    @property
    def slot(self):
        return (self.done + self.n - 1) % 4


class Counts:

    def __init__(self, sems, table):
        self.all = {name: Count(sems[name], *table[name]) for name in table}

    def __getitem__(self, name):
        return self.all[name]

    def layer(self, l):
        for c in self.all.values():
            c.base, c.n, c.done = l * c.per_layer + c.start, 0, 0

    def end_layer(self):
        for name, c in self.all.items():
            assert c.n in (0, c.per_layer), (name, c.n, c.per_layer)

    def enter(self, i, **per):
        self.kept = {name: (c.base, c.n) for name, c in self.all.items()}
        self.per = per
        for name, k in per.items():
            c = self.all[name]
            c.base, c.done, c.n = c.base + c.n + i * k, c.n, 0

    def leave(self, times):
        for name, c in self.all.items():
            base, n = self.kept[name]
            if name in self.per:
                assert c.n == self.per[name], (name, c.n, self.per[name])
                c.base, c.n, c.done = base, n + times * self.per[name], 0
            else:
                assert c.n == n, name


TILES, MOMENTS = 216, 9 + B
SIGNALS = dict(
    tile_ready=(TILES, 0),
    unit_used=(UNITS, SLOTS),
    pair_ready=(64, 8),
    mean_ready=(3, 0),
    unit_hi=(SPLIT, 0), op_hi=(6 * KD, 0),
    x_sq=(3, 0), lat_sq=(1, 0), qk_sq=(2, 0), gla_sq=(1, 0), mem_sq=(1, 0), km_sq=(1, 0), xq_sq=(1, 0),
    kr_sq=(B, 0), pair_sq=(64, 2), ff_hi=(32, 0),
    root=(MOMENTS, 0),
    gate_soft=(1, 0), gate_exp=(1, 0), soft_exp=(1, 0), dec_exp=(B, 0), x_exp=(1, 0), xs_exp=(1, 0),
    tile_free=(TILES, 4),
    unit_lo=(SPLIT, 0), op_lo=(6 * KD, 0),
    lat_used=(B, 2),
    pair_sc=(64, 2), pair_sum=(64, 2),
    moment=(MOMENTS, 0),
    x_new=(3, 1), xg_ready=(24, 0), ssum_ready=(4, 0),
    z_ready=(15, 0), lat_ready=(1, 0), qk_raw=(2, 0), qk_norm=(1, 0), qk_ready=(1, 0), small_ready=(1, 0), vp_ready=(1, 0),
    soft_in=(1, 0), soft_p=(1, 0), soft_t=(1, 0),
    qbd_ready=(1, 0), gate_in=(1, 0), gate_la=(1, 0), gate_dec=(1, 0), gvs_ready=(1, 0), gla_state=(1, 0), gla_raw=(1, 0), head_root=(3, 0),
    mix_side=(1, 0), seq_in=(B, 0), kr_scaled=(B, 0), kr_rot=(B, 0), dec_max=(B, 0), dec_in=(B, 0), dec_sum=(B, 0),
    dec_out=(1, 0), olat_ready=(1, 0), mg_ready=(1, 0), km_raw=(1, 0), km_ready=(1, 0),
    xq_raw=(1, 0), xq_ready=(1, 0), x_in=(1, 0), x_p=(1, 0), x_t=(1, 0), hot_q=(1, 0), xs_in=(1, 0), hot_p=(1, 0), xs_out=(1, 0), xo_ready=(1, 0),
    ff_in=(32, 0), ff_done=(32, 0),
    pooled_ready=(1, 0), dec_amax=(B, 0),
)
POOL_STEPS, ACT_STEPS, DVE_STEPS, DEC_STEPS = 16, 51, 261, 30


def decoder(nc, units, xt, memt, pages, table, gains, mats, consts, gstate, pstate, pstate_nat,
            o_y, o_lat, o_kr, o_glap, o_glas, o_u, o_pool, o_mk, o_mv, gvs):
    ctx = ExitStack()
    with ctx:
        def sb(name, shape, dt=FP32):
            return ctx.enter_context(nc.sbuf_tensor(name, shape, dt))

        def twin(name, shape):
            with nc.sbuf_tensor(name, shape, FP32) as t:
                pass
            return t, sb(name + "_r", shape, F32R)

        def sem(name):
            return ctx.enter_context(nc.semaphore(name))

        ring, ring_r = twin("ring", [P, SLOTS, UNIT])
        xT = sb("xT", [P, KD, T])
        xg, xg_r = twin("xg", [P, KD, T])
        sq, sq_r = twin("sq", [P, KD, T])
        rB = sb("rB", [P, T])
        area, area_r = twin("area", [P, 32, T])
        z, z_r, mix, mix_r = area[:, 0:NZ, :], area_r[:, 0:NZ, :], area[:, NZ:NZ + KD, :], area_r[:, NZ:NZ + KD, :]
        m, tmp = (area[:, c:c + 4, :].rearrange("p k t -> p (k t)") for c in (NZ + KD, NZ + KD + 4))
        qkA, qkA_r = twin("qkA", [P, 8, T])
        qkB, qkB_r = twin("qkB", [P, 8, T])
        mat = sb("mat", [P, NMAT])
        con = sb("con", [P, NC])
        gall = sb("gall", [P, DEPTH, NG])
        gain = sb("gain", [P, NG])
        ones = sb("ones", [P, P])
        latT, latT_r = twin("latT", [P, PAGES, 256])
        big, big_r = twin("big", [P, 2 * PAGES * 288])
        krQ = sb("krQ", [P, PAGES, ROPE])
        krN = sb("krN", [P, PAGES, ROPE])
        gvs_n = sb("gvs_n", [B, 256])
        y = sb("y", [P, 4 * T])
        rBm = sb("rBm", [P, NM + 2])
        wuq_b = sb("wuq_b", [P, 2, 2, 260])
        qt = sb("qt", [P, 2, B, H])
        qblk = sb("qblk", [P, B, 4, H])
        snew = sb("snew", [P, B, H])
        latn = sb("latn", [B, 256])
        ssn = sb("ssn", [P, 2, PAGES, H])
        ssr = sb("ssr", [P, PAGES])
        sc = sb("sc", [P, 2, PAGES, H])
        scw = sb("scw", [P, S_PAGES, H])
        pr = sb("pr", [P, S_PAGES, H])
        mxp = sb("mxp", [P, H])
        mx = sb("mx", [P, H])
        rs = sb("rs", [P, H])
        den = sb("den", [H, 1])
        olat = sb("olat", [P, 2, B, H])
        qg = sb("qg", [NOPE, H, B])
        qbs = sb("qbs", [P, 2, 16])
        sprod = sb("sprod", [QK, H, B])
        ptab = sb("ptab", [1, B * PAGES], mybir.dt.int32)
        nmx = sb("nmx", [P, H, 2])
        psum_p = sb("psum_p", [P, H, 2])
        bl = sb("bl", [P, 4])
        ea = sb("ea", [P, B])
        qsb = sb("qsb", [P, B, H])
        xs_max = sb("xs_max", [B * H, 1])
        xs_den = sb("xs_den", [B * H, 1])
        ue = sb("ue", [P, 2, 400])

        ps = ctx.enter_context(nc.psum_tensor("ps", [P, 8, 512], FP32))

        def within(t, at, *shape):
            names = "abc"[:len(shape)]
            n = 1
            for k in shape:
                n *= k
            v = t[:, at:at + n]
            return v.rearrange(f"p ({' '.join(names)}) -> p {' '.join(names)}", **dict(zip(names, shape)))

        sq_f, qkA_f, qkB_f, xg_f, mix_f, z_f = (v[:, :, :].rearrange("p k t -> p (k t)") for v in (sq, qkA, qkB, xg, mix, z))
        latT_f = latT[:, :, :].rearrange("p g c -> p (g c)")
        lat = within(big, 0, 2, PAGES, 288)
        gvn, S, vb, gst, kendn, pooled = (within(big, 4608, 4, 256), within(big, 5632, 4, 256), within(big, 6656, B, 64),
                                          within(big, 7168, B, 64), within(big, 7680, 4, P), within(big, 8192, 2, T))
        kmT, vm = within(latT_f, 0, 8, NM), within(latT_f, 2048, 2, D)
        kraw = within(qkA_f, 0, 8, NM)
        vp = within(m, 0, 2, 512)
        o4 = [within(z_f, 8 * T, B // 2, 256)[0:H], within(qkB_f, 1024, B // 2, 256)[0:H]]
        ssm = tmp[:, 512:512 + NM]
        sS, pT = within(sq_f, 0, 4, 384), within(qkA_f, 0, 4, 384)
        qbd, att = within(y, 0, 4, TP), within(qkB_f, 0, 4, 256)
        psq = within(qkA_f, 0, 2, 512)
        krS, krC = within(qkB_f, 0, 4, PG), within(qkB_f, 512, 4, PG)
        wa, wb = within(big, 5632, 2, 400), within(mix_f, 4 * T, 2, 400)
        xS, xP = within(qkA_f, 0, 4, 2, NM), within(qkB_f, 0, 4, 2, NM)
        hot = within(xg_f, 0, 2, B * H, B * H)
        hot_diag = within(xg_f, 0, 2, (B * H) ** 2)[:, :, ::B * H + 1]
        xsS, xsP, xsO = m[0:B * H, 0:NM], y[0:B * H, 0:NM], tmp[0:B * H, 0:NM]
        mg = xg
        L_BC, L_EB, L_ENB, L_EKE, L_QD, L_KD, L_KE, L_A = range(8)
        L_SOFT = L_KE
        ident, swap, swap4, b64, rep = (con[:, c:c + P] for c in (C_ID, C_SWAP, C_SWAP4, C_B64, C_REP))
        hm = con[:, C_HM:C_HM + 4]
        band = [con[:, C_BAND + 96 - 32 * h:C_BAND + 224 - 32 * h] for h in range(H)]
        pick = [ident[:, 32 * h:32 * h + 1].broadcast_to([P, P]) for h in range(H)]
        cos, sin = con[0:QK, C_COS:C_COS + T], con[0:QK, C_SIN:C_SIN + T]
        w_uq = within(mat, M_UQ, 3, H, QK)
        w_uk, w_uv, w_ukt, w_pool = (within(mat, c, n, k) for c, n, k in
                                     ((M_UK, 2, 256), (M_UV, 2, 512), (M_UKT, 4, 256), (M_POOL, 2, P)))

        latT_rf, qkB_rf, sq_rf = (v[:, :, :].rearrange("p k t -> p (k t)") for v in (latT_r, qkB_r, sq_r))
        hi_mix = [within(big_r, UNIT * s, UNIT) for s in range(SLOTS)]
        hi_mk = hi_mix[0:2] + [within(sq_rf, 0, UNIT), within(latT_rf, 0, UNIT)]
        hi_in = [within(latT_rf, 0, UNIT), within(latT_rf, UNIT, UNIT), within(big_r, 0, UNIT), within(big_r, UNIT, UNIT)]
        hi_mlp = [within(latT_rf, 0, UNIT), within(latT_rf, UNIT, UNIT), within(qkB_rf, 0, UNIT), within(sq_rf, 0, UNIT)]
        hi_x, hi_out, hi_mem = qkA_r, qkB_r, z_r[:, 0:KD, 0:NM]
        mg_r = xg_r[:, :, 0:NM]
        hi_ff, lo_ff = within(big_r, 0, 32, T), area_r
        hid = within(y, 0, 4, T)

        sems = {name: sem(name) for name in SIGNALS}
        dve_step, act_step, pool_step = sem("dve_step"), sem("act_own"), sem("pool_step")
        unit_in = [sem(f"unit_in{s}") for s in range(SLOTS)]
        lt_in = [sem(f"lt_in{g}") for g in range(4)]
        lat_in = [sem(f"lat_in{s}") for s in range(2)]
        STORES = 7
        once_in, con_in, layer_in, mg_in = (sem(n) for n in ("once_in", "con_in", "layer_in", "mg_in"))
        y_out = sem("y_out")
        passed = {e: sem(f"passed_{e}") for e in ("pool", "sp", "pe", "dve", "act")}
        stored, copied, gvs_out, gvs_in, tab_in = (sem(n) for n in ("stored", "copied", "gvs_out", "gvs_in", "tab_in"))
        block = ctx.enter_context(nc.Block())

        @block.sync
        def _(sp):
            at = Counts(sems, SIGNALS)
            with sp.Fori(0, DEPTH) as l:
                at.layer(l)

                def load_units(n):
                    first = at["unit_used"].n
                    with sp.Fori(0, n // SLOTS) as i:
                        at.enter(i, unit_used=SLOTS)
                        for s in range(SLOTS):
                            sp.wait_ge(sems["unit_used"], at["unit_used"].free())
                            sp.dma_start(ring[:, s, :], units[bass.ds(l * UNITS + first + i * SLOTS + s, 1), :, :]
                                         .rearrange("a p n -> p (a n)")).then_inc(unit_in[s], 16)
                    at.leave(n // SLOTS)

                load_units(U_IN)
                sp.wait_ge(tab_in, 16)
                sp.wait_ge(sems["z_ready"], 15 * l + 15)
                sp.sem_inc(passed["sp"], 1)
                with sp.Fori(0, B // 2) as i:
                    at.enter(i, pair_ready=PAGES)
                    for s in range(2):
                        for pg in range(PAGES):
                            page = sp.value_load(ptab[0:1, bass.ds(i * 2 * PAGES + s * PAGES + pg, 1)],
                                                 min_val=0, max_val=pages.shape[0] // DEPTH - 1)
                            src = pages[bass.ds(page * DEPTH + l, 1), :, :].rearrange("a p n -> p (a n)")
                            if pg % 2 == 0:
                                sp.wait_ge(sems["pair_ready"], at["pair_ready"].free())
                            sp.dma_start(latT[:, pg, :], src[:, 0:256]).then_inc(lt_in[pg // 4], 16)
                at.leave(B // 2)
                load_units(UNITS - U_IN)
                at.end_layer()
            sp.wait_ge(sems["x_new"], 3 * DEPTH + 1)
            sp.dma_start(o_y, xT[:, :, :]).then_inc(y_out, 16)
            sp.wait_ge(y_out, 16)

        @block.gpsimd
        def _(pool):
            at = Counts(sems, SIGNALS)
            steps = [0]

            def wait_ge(semaphore, value):
                pool.wait_ge(semaphore, value)
                pool.sem_inc(passed["pool"], 1)

            def step(ins):
                ins.then_inc(pool_step, 1)
                steps[0] += 1
                wait_ge(pool_step, at_step(steps[0]))

            at_step = lambda n: n
            step(pool.memset(ones[:, :], 1.0))
            step(pool.memset(ue[:, :, 0:16], 0.0))
            STEP0 = steps[0]
            pool.dma_start(ptab[:, :], table).then_inc(tab_in, 16)
            wait_ge(tab_in, 16)
            wait_ge(unit_in[0], 16)
            pool.dma_start(con[:, :], consts).then_inc(con_in, 16)
            with pool.Fori(0, DEPTH) as l:
                at.layer(l)
                steps[0] = 0
                at_step = lambda n: STEP0 + l * POOL_STEPS + n
                wait_ge(sems["x_new"], 3 * l + 1)
                pool.dma_start(mat[:, :], mats[bass.ds(l, 1), :, :].rearrange("a p n -> p (a n)")).then_inc(layer_in, 16)
                pool.dma_start(gst[:, :, :], gstate[bass.ds(l, 1), :, :, :].rearrange("a p b v -> p (a b) v")).then_inc(layer_in, 16)
                for c in range(2):
                    pool.dma_start(ue[:, c, 272:400].rearrange("p (b j) -> p b j", b=B)[:, :, 0:15],
                                   pstate[bass.ds(l, 1), :, c, :, :].rearrange("a p b j -> p (a b) j")).then_inc(layer_in, 16)
                pool.dma_start(o_pool[bass.ds(l, 1), :, :, :].rearrange("a b j c -> (a b) j c"),
                               pstate_nat[bass.ds(l, 1), :, :, :].rearrange("a b j c -> (a b) j c")).then_inc(copied, 16)

                wait_ge(sems["z_ready"], 15 * l + 15)
                wait_ge(layer_in, 64 * (l + 1))
                step(pool.tensor_copy(ue[:, :, 16:272], z[:, UU:UU + 2, 0:TP]))
                step(pool.tensor_copy(ue[:, :, 272:400].rearrange("p c (b j) -> p c b j", b=B)[:, :, :, 15],
                                      z[:, UU:UU + 2, TP:T]))
                step(pool.tensor_tensor(wa[:, :, 1:400], ue[:, :, 1:400], ue[:, :, 0:399], ALU.add))
                src = wa
                for g, w in enumerate((2, 4, 8, 16)):
                    c, r = g // 2, 64 * (g % 2)
                    if g:
                        dst = wb if src is wa else wa
                        step(pool.tensor_tensor(dst[:, :, w - 1:400], src[:, :, w - 1:400],
                                                src[:, :, w // 2 - 1:400 - w // 2], ALU.add))
                        src = dst
                    step(pool.tensor_copy(pooled[r:r + 64, c, 0:TP], src[r:r + 64, c, 16:272]))
                    step(pool.tensor_copy(pooled[r:r + 64, c, TP:T],
                                          src[r:r + 64, c, 272:400].rearrange("p (b j) -> p b j", b=B)[:, :, 15]))
                inv = con[:, C_INV:C_INV + 2 * T].rearrange("p (c t) -> p c t", c=2)
                step(pool.tensor_tensor(pooled[:, :, :], pooled[:, :, :], inv, ALU.mult))
                step(pool.tensor_tensor(pooled[:, :, :], pooled[:, :, :], z[:, UU:UU + 2, :], ALU.subtract))
                pool.sem_inc(sems["pooled_ready"], 1)

                wait_ge(sems["gvs_ready"], l + 1)
                pool.dma_start(gvs, gvs_n[:, :]).then_inc(gvs_out, 16)
                wait_ge(gvs_out, 16 * (l + 1))
                for h in range(H):
                    pool.dma_start(vb[32 * h:32 * h + 32, :, :],
                                   gvs[:, 64 * h:64 * h + 64].unsqueeze(0).broadcast_to([32, B, 64])).then_inc(gvs_in, 16)

                def load(j, s, pgs):
                    for pg in pgs:
                        page = pool.value_load(ptab[0:1, bass.ds((j * 2 + s) * PAGES + pg, 1)], min_val=0,
                                               max_val=pages.shape[0] // DEPTH - 1)
                        pool.dma_start(lat[:, s, pg, :], pages[bass.ds(page * DEPTH + l, 1), :, 256:544]
                                       .rearrange("a p n -> p (a n)")).then_inc(lat_in[s], 16)

                def maximum():
                    wait_ge(sems["dec_max"], at["dec_max"].next())
                    pool.partition_all_reduce(mx[:, :], mxp[:, :], P, bass.bass_isa.ReduceOp.max).then_inc(sems["dec_amax"], 1)

                def load_and_maximum(j, s):
                    wait_ge(sems["lat_used"], at["lat_used"].free())
                    load(j, s, range(0, 10))
                    maximum()
                    load(j, s, range(10, PAGES))

                wait_ge(sems["lat_used"], at["lat_used"].free())
                load(0, 0, range(PAGES))
                wait_ge(sems["mix_side"], l + 1)
                pool.dma_start(mg[:, :, 0:NM], memt).then_inc(mg_in, 16)
                wait_ge(stored, 16 * (STORES * l + 5))
                with pool.Fori(0, B // 2 - 1) as i:
                    at.enter(i, dec_max=2, lat_used=2)
                    load_and_maximum(i, 1)
                    load_and_maximum(i + 1, 0)
                at.leave(B // 2 - 1)
                load_and_maximum(B // 2 - 1, 1)
                maximum()
                assert steps[0] == POOL_STEPS, steps
            wait_ge(copied, 16 * DEPTH)

        @block.scalar
        def _(act):
            at = Counts(sems, SIGNALS)
            act.dma_start(gall[:, :, :], gains).then_inc(once_in, 16)
            act.dma_start(xT[:, :, :], xt).then_inc(once_in, 16)
            act.preload_act_table_set("natural_log_exp_and_others")
            own = Count(act_step, ACT_STEPS, 0)

            def f(out, in_, func, **kw):
                return nc.scalar.activation(out, in_, func, **kw)

            def step(ins):
                ins.then_inc(act_step, 1)
                act.wait_ge(act_step, own.next())

            def power(rows, cols):
                act.wait_ge(sems["moment"], at["moment"].next())
                step(f(y[0:rows, 0:cols], m[0:rows, 0:cols], ACT.Ln))
                f(y[0:rows, 0:cols], y[0:rows, 0:cols], ACT.Exp, scale=-0.5).then_inc(sems["root"], 1)
                at["root"].next()

            def split_units(n, his):
                for _ in range(n):
                    count = at["unit_used"].next()
                    s = at["unit_used"].slot
                    act.wait_ge(unit_in[s], (count - SLOTS + (SLOTS - 1 - s)) * (16 // SLOTS))
                    f(his[s], ring[:, s, :], ACT.Copy).then_inc(sems["unit_hi"], 1)

            def split_operand(hi, x, gained=False):
                for k in range(KD):
                    if gained:
                        act.wait_ge(sems["xg_ready"], at["xg_ready"].next())
                    f(hi[:, k, :], x[:, k, :], ACT.Copy).then_inc(sems["op_hi"], 1)

            def square_x(units=0):
                act.wait_ge(sems["x_new"], at["x_new"].free())
                split_units(units, hi_in)
                split_operand(hi_x, xg, True)
                split_units(units, hi_in)
                f(sq[:, :, :], xT[:, :, :], ACT.Square).then_inc(sems["x_sq"], 1)
                power(P, T)

            act.sem_inc(sems["pair_sq"], 2)
            with act.Fori(0, DEPTH) as l:
                at.layer(l)
                own.base, own.n = l * ACT_STEPS, 0
                square_x(1)
                split_units(U_IN - 2, hi_in)
                act.wait_ge(sems["z_ready"], 15 * l + 15)
                f(xg[:, 0:5, :], z[:, 0:5, :], ACT.Square).then_inc(sems["lat_sq"], 1)
                power(P, 2 * T)
                act.wait_ge(sems["gate_in"], l + 1)
                soft = xg[:, L_SOFT, :]
                step(f(soft, xg[:, L_A, :], ACT.Abs))
                step(f(soft, soft, ACT.Exp, scale=-1.0))
                f(soft, soft, ACT.Ln, bias=1.0).then_inc(sems["gate_soft"], 1)
                act.wait_ge(sems["lat_ready"], l + 1)
                act.dma_start(o_lat[bass.ds(l, 1), :, :, :].rearrange("a p c t -> (a p) c t"), z[:, CKV:CKV + 2, :]).then_inc(stored, 16)
                act.dma_start(o_kr[bass.ds(l, 1), :, :].rearrange("a p t -> (a p) t"), z[NOPE:QK, KR, :]).then_inc(stored, 16)
                act.dma_start(o_u[bass.ds(l, 1), :, :, :].rearrange("a p c t -> (a p) c t"), z[:, UU:UU + 2, :]).then_inc(stored, 16)
                act.wait_ge(sems["gate_la"], l + 1)
                f(xg[:, L_EB, 0:TP], xg[:, L_BC, 0:TP], ACT.Exp, scale=1 / 16)
                f(xg[:, L_ENB, 0:TP], xg[:, L_BC, 0:TP], ACT.Exp, scale=-1 / 16)
                for c in range(4):
                    f(xg[:, L_EKE, 64 * c:64 * c + 64], xg[:, L_BC, 64 * c:64 * c + 64], ACT.Exp, bias=bl[:, c:c + 1], scale=-1 / 16)
                f(ea[:, :], xg[:, L_A, TP:T], ACT.Exp, scale=1 / 16).then_inc(sems["gate_exp"], 1)
                for j in range(2):
                    act.wait_ge(sems["qk_raw"], 2 * l + j + 1)
                    f(sq[0:QK, 4 * j:4 * j + 4, :], qkA[0:QK, 4 * j:4 * j + 4, :], ACT.Square).then_inc(sems["qk_sq"], 1)
                power(P, 2 * T)
                act.wait_ge(sems["soft_in"], l + 1)
                for h in range(H):
                    for a, (c0, c1) in enumerate(((0, P), (P, 384))):
                        last = f(sS[:, h, c0:c1], sS[:, h, c0:c1], ACT.Exp, bias=nmx[:, h, a:a + 1],
                                 scale=QK ** -0.5, accum_out=psum_p[:, h, a:a + 1])
                last.then_inc(sems["soft_exp"], 1)
                act.wait_ge(sems["gla_raw"], l + 1)
                f(sq[:, 0:2, :], z[:, GV:GV + 2, :], ACT.Square).then_inc(sems["gla_sq"], 1)
                f(sq[:, 4:6, :], z[:, GR:GR + 2, :], ACT.Exp, scale=-1.0)
                act.dma_start(o_glap[bass.ds(l, 1), :, :].rearrange("a p n -> (a p) n"), S[:, 3, :]).then_inc(stored, 16)
                act.dma_start(o_glas[bass.ds(l, 1), :, :, :].rearrange("a p b v -> (a p) b v"), gst[:, :, :]).then_inc(stored, 16)

                def keys(j, s, b, mem=False):
                    for pair in range(PAGES // 2):
                        act.wait_ge(sems["pair_ready"], at["pair_ready"].next())
                        act.wait_ge(sems["pair_sum"], at["pair_sum"].free())
                        q = pair % 2
                        f(psq[:, q, :].rearrange("p (g c) -> p g c", g=2), ps[:, 4 + 2 * q:6 + 2 * q, 0:256],
                          ACT.Square).then_inc(sems["pair_sq"], 1)
                        at["pair_sq"].next()
                        if pair == 1:
                            power(P, 64 if b else 2 * T)
                        if b and pair == 2:
                            exp()
                        if mem and pair == 2:
                            act.wait_ge(mg_in, 16 * (l + 1))
                            f(sq[:, :, 0:NM], mg[:, :, 0:NM], ACT.Square).then_inc(sems["mem_sq"], 1)
                        if mem and pair == 5:
                            power(P, NM + 2)
                        if pair == 4:
                            act.wait_ge(lat_in[s], 16 * PAGES * (l * (B // 2) + j + 1))
                            f(krN[:, :, :], lat[:, s, :, 256:288], ACT.Copy)
                            f(krQ[:, :, :], lat[:, s, :, 256:288], ACT.Square).then_inc(sems["kr_sq"], 1)
                            at["kr_sq"].next()
                        if mem and pair == 4:
                            act.wait_ge(stored, 16 * (STORES * l + 5))
                            act.sem_inc(passed["act"], 1)
                            act.wait_ge(sems["mg_ready"], l + 1)
                            split_operand(hi_mem, mg[:, :, 0:NM])

                def exp():
                    act.wait_ge(sems["dec_in"], at["dec_in"].next())
                    f(pr[:, :, :], scw[:, :, :], ACT.Exp, scale=QK ** -0.5).then_inc(sems["dec_exp"], 1)
                    at["dec_exp"].next()

                keys(0, 0, 0)
                with act.Fori(0, B // 2 - 1) as i:
                    at.enter(i, pair_ready=16, pair_sum=16, pair_sq=16, moment=2, root=2, dec_in=2, dec_exp=2, kr_sq=2)
                    base, n = own.base, own.n
                    own.base, own.n = base + n + i * 2, 0
                    keys(i, 1, 1)
                    keys(i + 1, 0, 1)
                    assert own.n == 2
                at.leave(B // 2 - 1)
                own.base, own.n = base, n + B - 2
                keys(B // 2 - 1, 1, 1, True)
                split_units(1, hi_mk)
                power(P, 64)
                split_units(1, hi_mk)
                exp()
                split_units(2, hi_mk)
                split_units(2, hi_mix)
                act.wait_ge(sems["km_raw"], l + 1)
                f(sq[:, :, 0:NM], kraw[:, :, :], ACT.Square).then_inc(sems["km_sq"], 1)
                split_operand(hi_out, mix)
                split_units(U_MV, hi_mix)
                power(P, NM)
                act.wait_ge(sems["km_ready"], l + 1)
                act.dma_start(o_mk[bass.ds(l, 1), :, :, :].rearrange("a p c n -> (a p) c n"), kmT[:, :, :]).then_inc(stored, 16)
                act.dma_start(o_mv[bass.ds(l, 1), :, :, :].rearrange("a p c n -> (a p) c n"), vm[:, :, :]).then_inc(stored, 16)
                split_units(U_OUT, hi_mix)
                square_x()
                split_units(U_XQ - 2, hi_mix)
                at["unit_used"].next(U_XK + U_XV)
                act.wait_ge(sems["xq_raw"], l + 1)
                f(sq[:, :, :], z[:, 0:8, :], ACT.Square).then_inc(sems["xq_sq"], 1)
                power(P, T)
                act.wait_ge(sems["x_in"], l + 1)
                for h in range(H):
                    for a in range(2):
                        last = f(xS[:, h, a, :], xS[:, h, a, :], ACT.Exp, bias=nmx[:, h, a:a + 1], scale=1 / 16,
                                 accum_out=psum_p[:, h, a:a + 1])
                last.then_inc(sems["x_exp"], 1)
                act.wait_ge(sems["xs_in"], l + 1)
                f(xsP, xsS, ACT.Exp, bias=xs_max[:, :], scale=1 / 16, accum_out=xs_den[:, :]).then_inc(sems["xs_exp"], 1)
                split_units(2, hi_mix)
                act.wait_ge(sems["xo_ready"], l + 1)
                split_operand(hi_out, mix)
                split_units(2, hi_mix)
                split_units(2, hi_mlp)
                square_x()

                split_units(1, hi_mlp)

                with act.Fori(0, U_FF1 // SLOTS) as i:
                    at.enter(i, unit_used=SLOTS)
                    base, n = own.base, own.n
                    own.base, own.n = base + n + i * 8, 0
                    for t in range(8):
                        if t % 2 == 0:
                            split_units(1, hi_mlp)
                        act.wait_ge(sems["ff_in"], l * 32 + i * 8 + t + 1)
                        step(f(hid[:, t % 4, :], hid[:, t % 4, :], ACT.Square))
                        f(hi_ff[:, bass.ds(i * 8 + t, 1), :], hid[:, t % 4:t % 4 + 1, :], ACT.Copy).then_inc(sems["ff_hi"], 1)
                at.leave(U_FF1 // SLOTS)
                own.base, own.n = base, n + 8 * (U_FF1 // SLOTS)
                split_units(U_FF2 - 3, hi_mlp)
                at.end_layer()
                assert own.n == ACT_STEPS, own.n
            act.wait_ge(stored, STORES * 16 * DEPTH)

        @block.vector
        def _(dve):
            at = Counts(sems, SIGNALS)
            own = Count(dve_step, DVE_STEPS, 0)
            v = nc.vector

            def step(ins):
                ins.then_inc(dve_step, 1)
                dve.wait_ge(dve_step, own.next())

            def wait(name):
                dve.wait_ge(sems[name], at[name].next())

            def tell(name):
                dve.sem_inc(sems[name], 1)

            def tile():
                wait("tile_ready")
                return ps[:, at["tile_ready"].slot, :]

            def freed(ins):
                ins.then_inc(sems["tile_free"], 1)
                dve.wait_ge(sems["tile_free"], at["tile_free"].next())

            def refine(rows, cols, out=None):
                tell("moment")
                newton(rows, cols, out)

            def newton(rows, cols, out=None):
                wait("root")
                a, b, c = (t[0:rows, 0:cols] for t in (y, m, tmp))
                step(v.scalar_tensor_tensor(c, a, -0.5, a, ALU.mult, ALU.mult))
                step(v.tensor_tensor(c, c, b, ALU.mult))
                step(v.scalar_tensor_tensor(a if out is None else out, c, 1.5, a, ALU.add, ALU.mult))

            def split_unit(his):
                wait("unit_hi")
                s = at["unit_hi"].slot
                v.tensor_tensor(ring_r[:, s, :], ring[:, s, :], his[s].bitcast(FP32), ALU.subtract).then_inc(sems["unit_lo"], 1)

            def split_operand(hi, x, x_r):
                for k in range(KD):
                    wait("op_hi")
                    v.tensor_tensor(x_r[:, k, :], x[:, k, :], hi[:, k, :].bitcast(FP32), ALU.subtract).then_inc(sems["op_lo"], 1)

            def norm_x(g, units=0):
                for k in range(KD):
                    v.tensor_scalar(xg[:, k, :], xT[:, k, :], gain[:, g + k:g + k + 1], None, ALU.mult).then_inc(sems["xg_ready"], 1)
                for _ in range(units):
                    split_unit(hi_in)
                split_operand(hi_x, xg, xg_r)
                for _ in range(units):
                    split_unit(hi_in)
                wait("x_sq")
                step(v.tensor_reduce(tmp[:, 0:T], sq[:, :, :].rearrange("p k t -> p t k"), AXX, ALU.add))
                tell("ssum_ready")
                wait("mean_ready")
                step(v.tensor_scalar(m[:, 0:T], ps[:, 4, 0:T], 1 / D, EPS, ALU.mult, ALU.add))
                refine(P, T, rB[:, :])

            def head_norms(out, x, g, cols):
                freed(v.tensor_scalar(m[:, 0:cols], tile()[:, 0:cols], 1 / 256, EPS, ALU.mult, ALU.add))
                refine(P, cols)
                tell("head_root")
                for h in range(H):
                    t = tile()
                    for c in range(2):
                        i = 2 * h + c
                        ins = v.scalar_tensor_tensor(out[:, i, 0:cols], x[:, i, 0:cols], gain[:, g + c:g + c + 1], t[:, 0:cols],
                                                     ALU.mult, ALU.mult)
                        if c == 0:
                            step(ins)
                    freed(ins)

            def add_to_x(k):
                freed(v.tensor_tensor(xT[:, k, :], xT[:, k, :], tile()[:, 0:T], ALU.add))

            dve.wait_ge(pool_step, 1)
            dve.wait_ge(once_in, 32)
            v.memset(snew[:, :, :], NEG)
            dve.sem_inc(sems["tile_free"], 4)
            dve.sem_inc(sems["pair_sc"], 2)
            dve.sem_inc(sems["pair_sum"], 2)
            dve.sem_inc(sems["lat_used"], 2)
            dve.sem_inc(sems["x_new"], 1)

            with dve.Fori(0, DEPTH) as l:
                at.layer(l)
                own.base, own.n = l * DVE_STEPS, 0
                step(v.tensor_copy(gain[:, :], gall[:, bass.ds(l, 1), :].rearrange("p a n -> p (a n)")))
                norm_x(G_MIX, 1)

                dve.wait_ge(con_in, 16)
                for i in range(NZ):
                    if i % 2 == 0 and i // 2 < U_IN - 2:
                        split_unit(hi_in)
                    freed(v.tensor_tensor(z[:, i, :], tile()[:, 0:T], rB[:, :], ALU.mult))
                    tell("z_ready")
                for a in range(2):
                    freed(v.tensor_copy(gvn[0:64, 2 * a:2 * a + 2, :], tile()[0:64, :].rearrange("p (c n) -> p c n", c=2)))
                freed(v.tensor_copy(gvs_n[:, :], tile()[0:B, 0:256]))
                tell("gvs_ready")
                for j, n in enumerate((384, 256)):
                    freed(v.tensor_scalar(m[:, j * T:j * T + T], tile()[:, 0:T], 1 / n, EPS, ALU.mult, ALU.add))
                tell("moment")
                freed(v.tensor_scalar(xg[:, L_A, :], tile()[:, 0:T], gain[:, B_GATE:B_GATE + 1], None, ALU.add))
                tell("gate_in")
                newton(P, 2 * T)
                for k in range(5):
                    c0 = 0 if k < 3 else T
                    step(v.scalar_tensor_tensor(z[:, k, :], z[:, k, :], gain[:, G_QL + k:G_QL + k + 1], y[:, c0:c0 + T], ALU.mult, ALU.mult))
                tell("lat_ready")
                wait("gate_soft")
                step(v.scalar_tensor_tensor(xg[:, L_A, :], xg[:, L_A, :], 0.0, xg[:, L_SOFT, :], ALU.min, ALU.subtract))
                for c in range(4):
                    step(v.tensor_tensor_scan(xg[:, L_BC, 64 * c:64 * c + 64], ones[:, 0:64], xg[:, L_A, 64 * c:64 * c + 64],
                                              0.0, ALU.mult, ALU.add))
                step(v.tensor_scalar(bl[:, :], xg[:, L_BC, 63:256:64], 1 / 16, None, ALU.mult))
                tell("gate_la")

                for h in range(H):
                    freed(v.tensor_copy(qkA[0:QK, h, :], tile()[0:QK, 0:T]))
                tell("qk_raw")
                for h in range(H):
                    freed(v.tensor_copy(qkA[0:NOPE, 4 + h, :], tile()[0:NOPE, 0:T]))
                    step(v.tensor_copy(qkA[NOPE:QK, 4 + h, :], z[NOPE:QK, KR, :]))
                tell("qk_raw")
                for j in range(2):
                    freed(v.tensor_scalar(m[:, j * T:j * T + T], tile()[:, 0:T], 1 / QK, EPS, ALU.mult, ALU.add))
                tell("moment")
                wait("gate_exp")
                step(v.tensor_tensor(xg[:, L_KE, 0:TP], z[:, GK, 0:TP], xg[:, L_EKE, 0:TP], ALU.mult))
                tell("gate_dec")
                step(v.scalar_tensor_tensor(xg[:, L_QD, 0:TP], z[:, GQ, 0:TP], 32 ** -0.5, xg[:, L_EB, 0:TP], ALU.mult, ALU.mult))
                step(v.tensor_tensor(xg[:, L_KD, 0:TP], z[:, GK, 0:TP], xg[:, L_ENB, 0:TP], ALU.mult))
                newton(P, 2 * T)
                tell("head_root")
                freed(v.tensor_copy(kendn[0:64, :, :], tile()[0:64, :].rearrange("p (c n) -> p c n", c=4)))
                for h in range(H):
                    step(v.tensor_scalar(qsb[:, :, h], z[:, GQ, TP:T], hm[:, h:h + 1], 32 ** -0.5, ALU.mult, ALU.mult))
                for j, g in enumerate((G_Q, G_K)):
                    for i in range(4 * j, 4 * j + 4):
                        freed(v.scalar_tensor_tensor(qkB[0:QK, i, :], qkA[0:QK, i, :], gain[0:QK, g:g + 1], tile()[0:QK, 0:T],
                                                     ALU.mult, ALU.mult))
                tell("qk_norm")
                step(v.tensor_tensor(qkA[0:QK, :, :], qkB[0:QK, :, :], cos.unsqueeze(1).broadcast_to([QK, 8, T]), ALU.mult))
                for i in range(8):
                    freed(v.tensor_tensor(tmp[0:QK, 0:T], tile()[0:QK, 0:T], sin, ALU.mult))
                    step(v.tensor_tensor(qkB[0:QK, i, :], qkA[0:QK, i, :], tmp[0:QK, 0:T], ALU.add))
                tell("qk_ready")
                step(v.tensor_scalar(qg[:, :, :], qkB[0:NOPE, 0:4, TP:T], gain[0:NOPE, G_K:G_K + 1], None, ALU.mult))
                step(v.tensor_tensor(sprod[:, :, :], qkB[0:QK, 0:4, TP:T], qkB[0:QK, 4:8, TP:T], ALU.mult))
                tell("small_ready")
                for a in range(2):
                    freed(v.tensor_copy(vp[:, a, :], tile()))
                tell("vp_ready")
                freed(v.tensor_copy(qt[:, :, :, :], tile()[:, 0:64].rearrange("p (c h b) -> p c b h", c=2, h=H)))
                t = tile()
                for j in range(4):
                    ins = v.tensor_scalar(qblk[:, :, j, :], t[:, 0:32].rearrange("p (h b) -> p b h", h=H), hm[:, j:j + 1], None, ALU.mult)
                    if j < 3:
                        step(ins)
                freed(ins)
                t = tile()
                eye = ident[0:B, 0:B].unsqueeze(2).broadcast_to([B, B, H])
                step(v.tensor_tensor(snew[0:B, :, :], t[0:B, 0:32].rearrange("p (h b) -> p b h", h=H), eye, ALU.mult))
                step(v.tensor_scalar(tmp[0:B, 0:B], ident[0:B, 0:B], -1.0, -NEG, ALU.add, ALU.mult))
                step(v.tensor_tensor(snew[0:B, :, :], snew[0:B, :, :], tmp[0:B, 0:B].unsqueeze(2).broadcast_to([B, B, H]), ALU.add))
                freed(v.tensor_copy(latn[:, :], t[0:B, 64:320]))

                for h in range(H):
                    freed(v.tensor_tensor(sS[:, h, :], tile()[:, 0:384], con[:, C_MASK:C_MASK + 384], ALU.add))
                for a, (c0, c1) in enumerate(((0, P), (P, 384))):
                    step(v.tensor_reduce(nmx[:, :, a:a + 1], sS[:, :, c0:c1], AXX, ALU.max, negate=True))
                step(v.tensor_scalar(nmx[:, :, :], nmx[:, :, :], QK ** -0.5, None, ALU.mult))
                tell("soft_in")
                for h in range(H):
                    step(v.tensor_scalar(qbd[:, h, :], xg[:, L_QD, 0:TP], hm[:, h:h + 1], None, ALU.mult))
                tell("qbd_ready")
                dve.wait_ge(gvs_in, 64 * (l + 1))
                dve.wait_ge(layer_in, 64 * (l + 1))
                step(v.tensor_tensor(gst[:, :, :], gst[:, :, :], ea[:, :].unsqueeze(2).broadcast_to([P, B, 64]), ALU.mult))
                step(v.tensor_tensor(vb[:, :, :], vb[:, :, :], z[:, GK, TP:T].unsqueeze(2).broadcast_to([P, B, 64]), ALU.mult))
                step(v.tensor_tensor(gst[:, :, :], gst[:, :, :], vb[:, :, :], ALU.add))
                for a in range(2):
                    freed(v.tensor_tensor(att[0:64, 2 * a:2 * a + 2, :], tile()[0:64, :].rearrange("p (c n) -> p c n", c=2),
                                          con[0:64, C_TRI:C_TRI + 256].unsqueeze(1).broadcast_to([64, 2, 256]), ALU.mult))
                wait("soft_exp")
                step(v.reciprocal(psum_p[:, :, :], psum_p[:, :, :]))
                for h in range(H):
                    for a, (c0, c1) in enumerate(((0, P), (P, 384))):
                        step(v.tensor_scalar(sS[:, h, c0:c1], sS[:, h, c0:c1], psum_p[:, h, a:a + 1], None, ALU.mult))
                tell("soft_p")
                dve.wait_ge(sems["pooled_ready"], l + 1)
                bm = con[:, C_BM:C_BM + 256]
                for c in range(4):
                    if c % 2 == 0:
                        t = tile()
                    upd = t[:, 256 * (c % 2):256 * (c % 2) + 256]
                    if c == 0:
                        step(v.tensor_copy(S[:, 0, :], upd))
                    elif c % 2:
                        freed(v.scalar_tensor_tensor(S[:, c, :], S[:, c - 1, :], xg[:, L_EB, 64 * c + 63:64 * c + 64], upd, ALU.mult, ALU.add))
                    else:
                        step(v.scalar_tensor_tensor(S[:, c, :], S[:, c - 1, :], xg[:, L_EB, 64 * c + 63:64 * c + 64], upd, ALU.mult, ALU.add))
                    step(v.tensor_tensor(S[:, c, :], S[:, c, :], bm, ALU.mult))
                tell("gla_state")
                for h in range(H):
                    freed(v.tensor_copy(pT[:, h, :], tile()[:, 0:384]))
                tell("soft_t")
                for s in range(2):
                    step(v.tensor_copy(wuq_b[:, s, :, 0:256], w_uk))
                freed(v.tensor_copy(z[:, GV:GV + 2, 0:TP], tile().rearrange("p (c t) -> p c t", c=2)))
                freed(v.tensor_copy(z[:, GV:GV + 2, TP:T], tile()[:, 0:16].rearrange("p (c t) -> p c t", c=2)))
                tell("gla_raw")
                for h in range(H):
                    freed(v.tensor_copy(mix[:, h, 0:TP], tile()[:, 0:TP]))

                def prepare(j, s):
                    b = bass.ds(j * 2 + s, 1)
                    step(v.tensor_copy(wuq_b[:, s, :, 256:260], qt[:, :, b, :].rearrange("p c b h -> p c (b h)")))
                    step(v.tensor_copy(qbs[:, s, :], qblk[:, b, :, :].rearrange("p b j h -> p (b j h)")))
                    tell("seq_in")

                def pair(s, n):
                    q = n % 2
                    wait("pair_ready")
                    wait("pair_sq")
                    v.tensor_copy(sc[:, s, 2 * n:2 * n + 2, :], ps[:, 4 + 2 * q:6 + 2 * q, 256:260]).then_inc(sems["pair_sc"], 1)
                    v.tensor_reduce(ssn[:, s, 2 * n:2 * n + 2, :], psq[:, q, :].rearrange("p (g c) -> p g c", c=64),
                                    AXX, ALU.add).then_inc(sems["pair_sum"], 1)
                    at["pair_sum"].next()

                def scores(s):
                    t = tile()
                    dve.wait_ge(sems["pair_sum"], at["pair_sum"].next(0))
                    step(v.tensor_tensor(m[:, 0:64].rearrange("p (g h) -> p g h", h=H), ssn[:, s, :, :],
                                         ssr[:, :].unsqueeze(2).broadcast_to([P, PAGES, H]), ALU.add))
                    step(v.tensor_scalar(m[:, 0:64], m[:, 0:64], 1 / QK, EPS, ALU.mult, ALU.add))
                    tell("moment")
                    freed(v.tensor_tensor(scw[:, 0:PAGES, :], sc[:, s, :, :], t[:, 0:64].rearrange("p (g h) -> p g h", h=H), ALU.add))

                def maxima(j, s):
                    newton(P, 64)
                    step(v.tensor_tensor(scw[:, 0:PAGES, :], scw[:, 0:PAGES, :], y[:, 0:64].rearrange("p (g h) -> p g h", h=H), ALU.mult))
                    step(v.tensor_copy(scw[:, PAGES, :], snew[:, bass.ds(j * 2 + s, 1), :].rearrange("p b h -> p (b h)")))
                    step(v.tensor_reduce(mxp[:, :], scw[:, :, :].rearrange("p g h -> p h g"), AXX, ALU.max))
                    tell("dec_max")

                def exponents():
                    wait("dec_amax")
                    step(v.tensor_tensor(scw[:, :, :], scw[:, :, :], mx[:, :].unsqueeze(1).broadcast_to([P, S_PAGES, H]), ALU.subtract))
                    tell("dec_in")

                def sums():
                    wait("dec_exp")
                    step(v.tensor_reduce(rs[:, :], pr[:, :, :].rearrange("p g h -> p h g"), AXX, ALU.add))
                    tell("dec_sum")

                def values(j, s):
                    t = tile()
                    step(v.reciprocal(den[:, :], t[0:H, 256:257]))
                    freed(v.tensor_scalar(o4[s][:, bass.ds(j, 1), :], t[0:H, 0:256].unsqueeze(1), den[:, :], None, ALU.mult))
                    tell("lat_used")

                def side(part):
                    if part == 0:
                        for c in range(2):
                            freed(v.tensor_scalar(m[:, c * T:c * T + T], tile()[:, 0:T], 1 / 64, EPS, ALU.mult, ALU.add))
                        tell("moment")
                        for c in range(2):
                            freed(v.tensor_scalar(mix[:, 6 + c, :], tile()[:, 0:T], gain[:, G_POOL + c:G_POOL + c + 1], None, ALU.mult))
                    elif part == 1:
                        newton(P, 2 * T)
                        step(v.tensor_scalar(sq[:, 4:6, :], sq[:, 4:6, :], 1.0, None, ALU.add))
                    elif part == 2:
                        step(v.reciprocal(sq[:, 4:6, :], sq[:, 4:6, :]))
                        step(v.tensor_tensor(sq[:, 4:6, :], sq[:, 4:6, :], z[:, GR:GR + 2, :], ALU.mult))
                    else:
                        step(v.scalar_tensor_tensor(z[:, GV:GV + 2, :], z[:, GV:GV + 2, :], gain[:, G_GLA:G_GLA + 1],
                                                    y[:, 0:2 * T].rearrange("p (c t) -> p c t", c=2), ALU.mult, ALU.mult))
                        step(v.tensor_tensor(mix[:, 4:6, :], z[:, GV:GV + 2, :], sq[:, 4:6, :], ALU.mult))
                        tell("mix_side")

                def keys(j, s, before, after=None, mem=False):
                    pair(s, 0)
                    scores(1 - s) if before else side(0)
                    pair(s, 1)
                    maxima(*before) if before else side(1)
                    pair(s, 2)
                    exponents() if before else side(2)
                    pair(s, 3)
                    sums() if before else side(3)
                    if after:
                        prepare(*after)
                    pair(s, 4)
                    if mem:
                        wait("mem_sq")
                        for k in range(KD):
                            step(v.tensor_scalar(mg[:, k, 0:NM], mg[:, k, 0:NM], gain[:, G_MEM + k:G_MEM + k + 1], None, ALU.mult))
                        tell("mg_ready")
                        step(v.tensor_reduce(ssm, sq[:, :, 0:NM].rearrange("p k t -> p t k"), AXX, ALU.add))
                        tell("ssum_ready")
                        split_operand(hi_mem, mg[:, :, 0:NM], mg_r)
                    pair(s, 5)
                    if before:
                        values(*before)
                    freed(v.tensor_scalar(krC[:, :, :], tile().rearrange("p (g n) -> p g n", g=4), gain[:, G_KR4:G_KR4 + 1], None, ALU.mult))
                    tell("kr_scaled")
                    if mem:
                        freed(v.tensor_scalar(m[:, 0:NM + 2], tile()[:, 0:NM + 2], 1 / D, EPS, ALU.mult, ALU.add))
                        tell("moment")
                    pair(s, 6)
                    step(v.tensor_tensor(krS[:, :, :], krC[:, :, :], con[:, C_COS4:C_COS4 + 512].rearrange("p (g n) -> p g n", g=4), ALU.mult))
                    wait("kr_sq")
                    v.tensor_reduce(ssr[:, :], krQ[:, :, :], AXX, ALU.add)
                    freed(v.tensor_tensor(tmp[:, 0:512], tile(), con[:, C_SIN4:C_SIN4 + 512], ALU.mult))
                    step(v.tensor_tensor(krS[:, :, :], krS[:, :, :], tmp[:, 0:512].rearrange("p (g n) -> p g n", g=4), ALU.add))
                    tell("kr_rot")
                    pair(s, 7)
                    if mem:
                        newton(P, NM + 2, rBm[:, :])

                prepare(0, 0)
                prepare(0, 1)
                keys(0, 0, None)
                dve.wait_ge(stored, 16 * (STORES * l + 5))
                dve.sem_inc(passed["dve"], 1)
                with dve.Fori(0, B // 2 - 1) as i:
                    at.enter(i, tile_ready=8, tile_free=8, pair_ready=16, pair_sq=16, pair_sum=16, kr_sq=2, root=2, dec_amax=2, dec_exp=2)
                    base, n = own.base, own.n
                    own.base, own.n = base + n + i * DEC_STEPS, 0
                    keys(i, 1, (i, 0), (i + 1, 0))
                    keys(i + 1, 0, (i, 1), (i + 1, 1))
                    assert own.n == DEC_STEPS, own.n
                at.leave(B // 2 - 1)
                own.base, own.n = base, n + (B // 2 - 1) * DEC_STEPS
                last = B // 2 - 1
                keys(last, 1, (last, 0), mem=True)

                def mem_keys(i):
                    for c in range(2):
                        freed(v.tensor_tensor(kraw[:, 2 * i + c, :], tile()[:, 0:NM], rBm[:, 0:NM], ALU.mult))

                split_unit(hi_mk)
                scores(1)
                split_unit(hi_mk)
                maxima(last, 1)
                exponents()
                sums()
                split_unit(hi_mk)
                mem_keys(0)
                split_unit(hi_mk)
                mem_keys(1)
                values(last, 1)
                tell("dec_out")
                split_unit(hi_mix)
                mem_keys(2)
                freed(v.tensor_copy(olat[:, :, :, :], tile()[:, 0:64].rearrange("p (c b h) -> p c b h", c=2, b=B)))
                tell("olat_ready")
                split_unit(hi_mix)
                mem_keys(3)
                freed(v.tensor_copy(mix[:, 0:4, TP:T], tile()[:, 0:32].rearrange("p (h b) -> p h b", h=H)))
                tell("km_raw")
                split_operand(hi_out, mix, mix_r)
                for h in range(H):
                    split_unit(hi_mix)
                    for a in range(2):
                        freed(v.tensor_scalar(vm[:, a, 256 * h:256 * h + 256], tile()[:, 0:256], rBm[:, NM + a:NM + a + 1], None, ALU.mult))
                head_norms(kmT, kraw, G_XK, NM)
                tell("km_ready")
                for k in range(KD):
                    if k % 2 == 0:
                        split_unit(hi_mix)
                    add_to_x(k)
                tell("x_new")

                norm_x(G_XA)
                dve.wait_ge(stored, 16 * STORES * (l + 1))
                for i in range(8):
                    if i % 2 == 0 and i // 2 < U_XQ - 2:
                        split_unit(hi_mix)
                    freed(v.tensor_tensor(z[:, i, :], tile()[:, 0:T], rB[:, :], ALU.mult))
                tell("xq_raw")
                head_norms(z, z, G_XQ, T)
                tell("xq_ready")
                step(v.memset(hot, 0.0))
                step(v.tensor_copy(hot_diag.rearrange("p n (b h) -> p n b h", b=B), z[:, 0:8, TP:T].rearrange("p (h c) b -> p c b h", h=H)))
                tell("hot_q")
                for h in range(H):
                    freed(v.tensor_copy(xS[:, h, :, :], tile().rearrange("p (a n) -> p a n", a=2)))
                step(v.tensor_reduce(nmx[:, :, :], xS[:, :, :, :], AXX, ALU.max, negate=True))
                step(v.tensor_scalar(nmx[:, :, :], nmx[:, :, :], 1 / 16, None, ALU.mult))
                tell("x_in")
                wait("x_exp")
                step(v.reciprocal(psum_p[:, :, :], psum_p[:, :, :]))
                for h in range(H):
                    for a in range(2):
                        step(v.tensor_scalar(xS[:, h, a, :], xS[:, h, a, :], psum_p[:, h, a:a + 1], None, ALU.mult))
                tell("x_p")
                freed(v.tensor_copy(xsS, tile()[0:B * H, 0:NM]))
                step(v.tensor_reduce(xs_max[:, :], xsS, AXX, ALU.max, negate=True))
                step(v.tensor_scalar(xs_max[:, :], xs_max[:, :], 1 / 16, None, ALU.mult))
                tell("xs_in")
                for h in range(H):
                    freed(v.tensor_copy(xP[:, h, :, :], tile().rearrange("p (a n) -> p a n", a=2)))
                tell("x_t")
                for h in range(H):
                    freed(v.tensor_copy(mix[:, 2 * h:2 * h + 2, 0:TP], tile().rearrange("p (a n) -> p a n", a=2)))
                freed(v.tensor_copy(hot_diag, tile()[:, 0:64].rearrange("p (n j) -> p n j", n=2)))
                tell("hot_p")
                split_unit(hi_mix)
                split_unit(hi_mix)
                step(v.reciprocal(xs_den[:, :], xs_den[:, :]))
                freed(v.tensor_scalar(xsO, tile()[0:B * H, 0:256], xs_den[:, :], None, ALU.mult))
                tell("xs_out")
                t = tile()[:, 0:64].rearrange("p (c b h) -> p h c b", c=2, b=B)
                for h in range(H):
                    ins = v.tensor_copy(mix[:, 2 * h:2 * h + 2, TP:T], t[:, h, :, :])
                    if h < H - 1:
                        step(ins)
                freed(ins)
                tell("xo_ready")
                split_operand(hi_out, mix, mix_r)
                for k in range(KD):
                    if k % 2 == 0:
                        split_unit(hi_mix if k < 4 else hi_mlp)
                    add_to_x(k)
                tell("x_new")

                norm_x(G_MLP)
                dve.sem_inc(passed["dve"], 1)
                with dve.Fori(0, U_FF1 // SLOTS) as i:
                    at.enter(i, tile_ready=8, tile_free=8, ff_hi=8, unit_hi=SLOTS)

                    def low(t):
                        wait("ff_hi")
                        chunk = bass.ds(i * 8 + t, 1)
                        v.tensor_tensor(lo_ff[:, chunk, :], hid[:, t % 4:t % 4 + 1, :], hi_ff[:, chunk, :].bitcast(FP32),
                                        ALU.subtract).then_inc(sems["ff_done"], 1)

                    for t in range(8):
                        if t % 2 == 0:
                            split_unit(hi_mlp)
                        freed(v.scalar_tensor_tensor(hid[:, t % 4, :], tile()[:, 0:T], 0.0, rB[:, :], ALU.max, ALU.mult))
                        tell("ff_in")
                        if t >= 2:
                            low(t - 2)
                    low(6)
                    low(7)
                at.leave(U_FF1 // SLOTS)
                for k in range(KD):
                    for _ in range(2 if k < 6 else 1):
                        split_unit(hi_mlp)
                    if k % 2:
                        add_to_x(k - 1)
                        add_to_x(k)
                tell("x_new")

                assert own.n == DVE_STEPS, own.n

        @block.tensor
        def _(pe):
            at = Counts(sems, SIGNALS)
            mm = nc.tensor.matmul

            def wait(name):
                pe.wait_ge(sems[name], at[name].next())

            def bank():
                pe.wait_ge(sems["tile_free"], at["tile_free"].free())
                return ps[:, at["tile_free"].slot, :]

            owed = []

            def settle():
                while owed:
                    pe.wait_ge(sems["tile_ready"], owed.pop())
                    pe.sem_inc(sems["unit_used"], 1)

            def ready(ins, unit=False):
                ins.then_inc(sems["tile_ready"], 1)
                settle()
                n = at["tile_ready"].next()
                if unit:
                    owed.append(n)

            def unit():
                n = at["unit_used"].next()
                s = at["unit_used"].slot
                pe.wait_ge(unit_in[s], (n - SLOTS + (SLOTS - 1 - s)) * (16 // SLOTS))
                return ring[:, s, :]

            def split_unit(his, pattern, **dims):
                wait("unit_lo")
                at["unit_used"].next()
                s = at["unit_used"].slot
                return [v.rearrange(pattern, **dims) for v in (his[s], ring_r[:, s, :])]

            def split_product(out, a, b, operand_new=False, first=True, last=True):
                for k in range(KD):
                    if operand_new:
                        wait("op_lo")
                    for n, (i, j) in enumerate(((0, 0), (0, 1), (1, 0))):
                        ins = mm(out, a(i, k), b(j, k), start=first and k + n == 0, stop=last and k == KD - 1 and n == 2)
                return ins

            def tiles_of(u, operand, a, width, new=False):
                return split_product(bank()[:, 0:width], lambda i, k: u[i][:, a, k, :], lambda j, k: operand[j][:, k, :], new)

            def product(out, pairs):
                for i, (a, b) in enumerate(pairs):
                    ins = mm(out, a, b, start=i == 0, stop=i == len(pairs) - 1)
                return ins

            def head_roots(cols):
                ready(product(bank()[:, 0:cols], [(band[i // 2], sq[:, i, 0:cols]) for i in range(KD)]))
                wait("head_root")
                for h in range(H):
                    ready(product(bank()[:, 0:cols], [(pick[h], y[:, 0:cols])]))

            def mean_x():
                wait("ssum_ready")
                product(ps[:, 4, 0:T], [(ones[:, :], tmp[:, 0:T])]).then_inc(sems["mean_ready"], 1)

            def normed_projection(n_units, his, tiles_last=2):
                for i in range(n_units):
                    tiles = tiles_last if i == n_units - 1 else 2
                    u = split_unit(his, "p (a k n) -> p a k n", a=2, k=KD)
                    for a in range(tiles):
                        ready(tiles_of(u, (hi_x, xg_r), a, T, i == 0 and a == 0), a == tiles - 1)
                    if i == 0:
                        mean_x()

            pe.wait_ge(pool_step, 1)
            pe.sem_inc(sems["unit_used"], SLOTS)
            pe.sem_inc(sems["pair_ready"], PAGES // 2)
            with pe.Fori(0, DEPTH) as l:
                at.layer(l)
                normed_projection(U_IN, hi_in, 1)
                for a in range(2):
                    t = bank()
                    pe.sem_inc(passed["pe"], 1)
                    for c in range(2):
                        for k in range(2):
                            o = c * 256 + k * P
                            ins = nc.tensor.transpose(t[0:64, o:o + P], z[:, GV + k, (2 * a + c) * 64:(2 * a + c) * 64 + 64], ident)
                    ready(ins)
                t = bank()
                pe.sem_inc(passed["pe"], 1)
                for k in range(2):
                    ins = nc.tensor.transpose(t[0:B, k * P:k * P + P], z[:, GV + k, TP:T], ident)
                ready(ins)
                wait("lat_sq")
                ready(product(bank()[:, 0:T], [(ones[:, :], xg[:, k, :]) for k in range(3)]))
                ready(product(bank()[:, 0:T], [(ones[:, :], xg[:, k, :]) for k in range(3, 5)]))
                pe.wait_ge(layer_in, 64 * (l + 1))
                ready(product(bank()[:, 0:T], [(mat[0:16, M_GATE:M_GATE + P], z[0:16, GLOW, :])]))
                wait("lat_ready")
                for h in range(H):
                    ready(product(bank()[0:QK, 0:T], [(w_uq[:, c, h, :], z[:, CQ + c, :]) for c in range(3)]))
                for h in range(H):
                    ready(product(bank()[0:NOPE, 0:T], [(w_uk[:, c, h * NOPE:h * NOPE + NOPE], z[:, CKV + c, :]) for c in range(2)]))
                for j in range(2):
                    wait("qk_sq")
                    ready(product(bank()[:, 0:T], [(band[h][0:QK, :], sq[0:QK, 4 * j + h, :]) for h in range(H)]))
                wait("gate_dec")
                t = bank()
                pe.sem_inc(passed["pe"], 1)
                for c in range(4):
                    ins = nc.tensor.transpose(t[0:64, c * P:c * P + P], xg[:, L_KE, 64 * c:64 * c + 64], ident)
                ready(ins)
                wait("head_root")
                for j in range(2):
                    for h in range(H):
                        ready(product(bank()[0:QK, 0:T], [(pick[h][:, 0:QK], y[:, j * T:j * T + T])]))
                wait("qk_norm")
                for i in range(8):
                    ready(product(bank()[0:QK, 0:T], [(swap[0:QK, 0:QK], qkB[0:QK, i, :])]))
                for a in range(2):
                    ready(product(bank(), [(z[:, CKV + c, P * a:P * a + P], w_uv[:, c, :]) for c in range(2)]))
                wait("small_ready")
                t = bank()
                for c in range(2):
                    for h in range(H):
                        o = (c * H + h) * B
                        ins = mm(t[:, o:o + B], w_ukt[0:NOPE, h, P * c:P * c + P], qg[:, h, :], start=True, stop=True)
                ready(ins)
                ready(product(bank()[:, 0:32], [(rep[0:QK, :], qkB[0:QK, 0:4, TP:T])]))
                t = bank()
                mm(t[0:B, 0:32], ones[0:QK, 0:B], sprod[:, :, :], start=True, stop=True)
                for c in range(2):
                    ins = nc.tensor.transpose(t[0:B, 64 + P * c:64 + P * c + P], z[:, CKV + c, TP:T], ident)
                ready(ins)
                wait("qk_ready")
                for h in range(H):
                    t = bank()
                    mm(t[:, 0:P], qkB[0:QK, h, 0:P], qkB[0:QK, 4 + h, 0:P], start=True, stop=True)
                    ready(mm(t[:, P:384], qkB[0:QK, h, P:TP], qkB[0:QK, 4 + h, 0:TP], start=True, stop=True))
                wait("qbd_ready")
                for a in range(2):
                    t = bank()
                    for c in range(2):
                        o = 64 * (2 * a + c)
                        ins = mm(t[0:64, 256 * c:256 * c + 256], xg[:, L_KD, o:o + 64], qbd[:, :, o:o + 64], start=True, stop=True)
                    ready(ins)
                for a in range(2):
                    t = bank()
                    for c in range(2):
                        ins = mm(t[:, 256 * c:256 * c + 256], kendn[0:64, 2 * a + c, :], gvn[0:64, 2 * a + c, :], start=True, stop=True)
                    ready(ins)
                wait("soft_p")
                for h in range(H):
                    t = bank()
                    for a in range(3):
                        ins = nc.tensor.transpose(t[:, P * a:P * a + P], sS[:, h, P * a:P * a + P], ident)
                    ready(ins)
                wait("gla_state")
                t = bank()
                pe.sem_inc(passed["pe"], 1)
                for k in range(2):
                    for c in range(4):
                        o = k * TP + 64 * c
                        if c:
                            mm(t[:, o:o + 64], S[:, c - 1, P * k:P * k + P], xg[:, L_QD, 64 * c:64 * c + 64], start=True, stop=True)
                        for j in range(2):
                            h = 2 * k + j
                            ins = mm(t[64 * j:64 * j + 64, o:o + 64], gvn[0:64, c, 64 * h:64 * h + 64], att[0:64, c, 64 * h:64 * h + 64],
                                     start=c == 0, stop=True, skip_group_check=True)
                ready(ins)
                t = bank()
                for b in range(B):
                    for j in range(2):
                        ins = mm(t[64 * j:64 * j + 64, b:16:B], gst[:, b, :], qsb[:, b, j:4:2], start=True, stop=True)
                ready(ins)
                wait("vp_ready")
                wait("soft_t")
                for h in range(H):
                    t = bank()
                    mm(t[:, 0:TP], vp[:, 0, P * h:P * h + P], pT[:, h, 0:TP], start=True, stop=False)
                    ready(mm(t[:, P:TP], vp[:, 1, P * h:P * h + P], pT[:, h, TP:384], start=False, stop=True))

                def pair(j, s, n):
                    q = n % 2
                    pe.wait_ge(sems["pair_sq"], at["pair_sq"].free())
                    pe.wait_ge(sems["pair_sc"], at["pair_sc"].free())
                    if n % 2 == 0:
                        pe.wait_ge(lt_in[n // 2], 64 * (l * B + j * 2 + s + 1))
                    for pg in (2 * n, 2 * n + 1):
                        ins = product(ps[:, 4 + 2 * q + pg % 2, 0:260],
                                      [(latT[:, pg, P * c:P * c + P], wuq_b[:, s, c, :]) for c in range(2)])
                    ins.then_inc(sems["pair_ready"], 1)

                def values(j, s):
                    wait("dec_sum")
                    pe.wait_ge(lat_in[s], 16 * PAGES * (l * (B // 2) + j + 1))
                    t = bank()
                    pe.sem_inc(passed["pe"], 1)
                    product(t[0:H, 0:256], [(pr[:, pg, :], lat[:, s, pg, 0:256]) for pg in range(PAGES)] + [(pr[0:B, PAGES, :], latn[:, :])])
                    ready(mm(t[0:H, 256:257], rs[:, :], ones[:, 0:1], start=True, stop=True))

                def keys(j, s, before, mem=False):
                    wait("seq_in")
                    pair(j, s, 0)
                    rotary(1 - s) if before else side()
                    for n in range(1, 6):
                        pair(j, s, n)
                    if before:
                        values(*before)
                    pe.wait_ge(sems["kr_sq"], at["kr_sq"].next())
                    t = bank()
                    for g in range(4):
                        ins = nc.tensor.transpose(t[:, P * g:P * g + P], krN[:, 4 * g:4 * g + 4, :], ident)
                    ready(ins)
                    if mem:
                        wait("ssum_ready")
                        t = bank()
                        mm(t[:, 0:NM], ones[:, :], ssm, start=True, stop=True)
                        for a in range(2):
                            ins = mm(t[:, NM + a:NM + a + 1], ssm[:, P * a:P * a + P], ones[:, 0:1], start=True, stop=True)
                        ready(ins)
                    pair(j, s, 6)
                    pe.wait_ge(sems["kr_scaled"], at["kr_scaled"].next())
                    ready(product(bank(), [(swap4, krC[:, :, :])]))
                    pair(j, s, 7)

                def side():
                    wait("gla_sq")
                    for c in range(2):
                        ready(product(bank()[:, 0:T], [(b64, sq[:, c, :])]))
                    wait("pooled_ready")
                    for c in range(2):
                        ready(product(bank()[:, 0:T], [(w_pool[:, c, :], pooled[:, c, :])]))

                def rotary(s):
                    wait("kr_rot")
                    t = bank()
                    for g in range(4):
                        ins = mm(t[:, 16 * g:16 * g + 16], krS[:, g, :], qbs[:, s, :], start=True, stop=True)
                    ready(ins)

                keys(0, 0, None)
                with pe.Fori(0, B // 2 - 1) as i:
                    at.enter(i, tile_free=8, tile_ready=8, pair_sq=16, pair_sc=16, seq_in=2, kr_sq=2, kr_scaled=2, kr_rot=2, dec_sum=2)
                    keys(i, 1, (i, 0))
                    keys(i + 1, 0, (i, 1))
                at.leave(B // 2 - 1)
                last = B // 2 - 1
                keys(last, 1, (last, 0), True)
                tokens = (hi_mem, mg_r)

                def mem_keys(i):
                    u = split_unit(hi_mk, "p (a k n) -> p a k n", a=2, k=KD)
                    for a in range(2):
                        ready(tiles_of(u, tokens, a, NM, i + a == 0), a == 1)

                rotary(1)
                mem_keys(0)
                mem_keys(1)
                values(last, 1)
                mem_keys(2)
                wait("dec_out")
                t = bank()
                pe.sem_inc(passed["pe"], 1)
                for c in range(2):
                    for b in range(B):
                        o = (c * B + b) * H
                        ins = nc.tensor.transpose(t[:, o:o + H], o4[b % 2][:, b // 2, P * c:P * c + P], ident[0:H, 0:H])
                ready(ins)
                mem_keys(3)
                wait("olat_ready")
                t = bank()
                for h in range(H):
                    ins = product(t[:, B * h:B * h + B], [(w_uv[:, c, P * h:P * h + P], olat[:, c, :, h]) for c in range(2)])
                ready(ins)
                for h in range(U_MV):
                    u = split_unit(hi_mix, "p (k n) -> p k n", k=KD)
                    for a in range(2):
                        ready(split_product(bank()[:, 0:256], lambda i, k: tokens[i][:, k, P * a:P * a + P],
                                            lambda j, k: u[j][:, k, :]), a == 1)
                wait("km_sq")
                head_roots(NM)

                def mixed():
                    for i in range(4):
                        u = split_unit(hi_mix, "p (a k n) -> p a k n", a=2, k=KD)
                        for a in range(2):
                            ready(tiles_of(u, (hi_out, mix_r), a, T, i + a == 0), a == 1)

                mixed()
                normed_projection(U_XQ, hi_mix)
                wait("xq_sq")
                head_roots(T)
                wait("xq_ready")
                pe.wait_ge(sems["km_ready"], l + 1)
                for h in range(H):
                    t = bank()
                    for a in range(2):
                        ins = product(t[:, NM * a:NM * a + NM], [(z[:, 2 * h + c, P * a:P * a + P], kmT[:, 2 * h + c, :]) for c in range(2)])
                    ready(ins)
                wait("hot_q")
                t = bank()
                for b in range(B):
                    u = unit().rearrange("p (k n) -> p k n", k=KD)
                    for k in range(KD):
                        if k == 4:
                            settle()
                        ins = mm(t[0:B * H, 0:NM], hot[:, k % 2, b * H + k // 2, :], u[:, k, :], start=b + k == 0,
                                 stop=b + k == B - 1 + KD - 1)
                    if b < B - 1:
                        ins.then_inc(sems["unit_used"], 1)
                ready(ins, True)
                wait("x_p")
                for h in range(H):
                    t = bank()
                    for n in range(2):
                        for a in range(2):
                            o = n * NM + a * P
                            ins = nc.tensor.transpose(t[:, o:o + P], xS[:, h, a, P * n:P * n + P], ident)
                    ready(ins)
                wait("x_t")
                for h in range(H):
                    t = bank()
                    for c in range(2):
                        o = h * 256 + c * P
                        ins = product(t[:, TP * c:TP * c + TP], [(vm[:, n, o:o + P], xP[:, h, n, :]) for n in range(2)])
                    ready(ins)
                wait("xs_exp")
                t = bank()
                pe.sem_inc(passed["pe"], 1)
                for n in range(2):
                    ins = nc.tensor.transpose(t[:, B * H * n:B * H * n + B * H], xsP[:, P * n:P * n + P], ident[0:B * H, 0:B * H])
                ready(ins)
                wait("hot_p")
                t = bank()
                for b in range(B):
                    u = unit().rearrange("p (n h d) -> p n h d", n=2, h=H)
                    for n in range(2):
                        if n == 1:
                            settle()
                        for h in range(H):
                            ins = mm(t[0:B * H, 0:256], hot[:, n, b * H + h, :], u[:, n, h, :], start=b + n + h == 0,
                                     stop=b + n + h == B - 1 + 1 + H - 1)
                    if b < B - 1:
                        ins.then_inc(sems["unit_used"], 1)
                ready(ins, True)
                wait("xs_out")
                t = bank()
                pe.sem_inc(passed["pe"], 1)
                for c in range(2):
                    ins = nc.tensor.transpose(t[:, B * H * c:B * H * c + B * H], xsO[:, P * c:P * c + P], ident[0:B * H, 0:B * H])
                ready(ins)
                wait("xo_ready")
                mixed()

                normed_projection(SLOTS, hi_mlp)
                settle()
                with pe.Fori(0, U_FF1 // SLOTS - 1) as i:
                    at.enter(i, tile_free=8, tile_ready=8, unit_used=SLOTS, unit_lo=SLOTS)
                    for j in range(SLOTS):
                        u = split_unit(hi_mlp, "p (a k n) -> p a k n", a=2, k=KD)
                        for a in range(2):
                            ready(tiles_of(u, (hi_x, xg_r), a, T), a == 1)
                    settle()
                at.leave(U_FF1 // SLOTS - 1)
                settle()
                with pe.Fori(0, 2) as i:
                    at.enter(i, tile_free=4, tile_ready=4, unit_used=8, unit_lo=8)
                    for pair in range(2):
                        two = [bank(), bank()]
                        for g in range(4):
                            pe.wait_ge(sems["ff_done"], 32 * l + 8 * g + 8)
                            u = split_unit(hi_mlp, "p (a k n) -> p a k n", a=2, k=KD)
                            for a in range(2):
                                ins = split_product(two[a][:, 0:T], lambda i, k: u[i][:, a, k, :],
                                                    lambda j, k: (hi_ff, lo_ff)[j][:, 8 * g + k, :], first=g == 0, last=g == 3)
                                if g == 3:
                                    ready(ins, a == 1)
                                elif a == 0:
                                    settle()
                            if g < 3:
                                ins.then_inc(sems["unit_used"], 1)
                    settle()
                at.leave(2)
                at.end_layer()


def _constants():
    import numpy as np
    c = np.zeros((P, NC), np.float32)
    p = np.arange(P)
    c[:, C_ID:C_ID + P] = np.eye(P)
    mask = np.where(p[None, :] <= p[:, None], 0.0, NEG)
    c[:, C_MASK:C_MASK + P] = mask
    c[:, C_MASK + 2 * P:C_MASK + 3 * P] = mask
    c[:, C_B64:C_B64 + P] = p[:, None] // 64 == p[None, :] // 64
    c[:, C_REP:C_REP + P] = p[:, None] == NOPE + p[None, :] % ROPE

    def swapped(n, first):
        m = np.zeros((P, P), np.float32)
        for g in range(first, n, ROPE):
            for i in range(ROPE // 2):
                m[g + ROPE // 2 + i, g + i] = -1
                m[g + i, g + ROPE // 2 + i] = 1
        return m

    c[:, C_SWAP:C_SWAP + P] = swapped(QK, NOPE)
    c[:, C_SWAP4:C_SWAP4 + P] = swapped(P, 0)
    half = ROPE // 2
    inv = np.float32(10000.0) ** (-np.arange(half, dtype=np.float32) / np.float32(half))
    pos = np.concatenate([np.arange(TP), np.full(B, PG * PAGES)]).astype(np.float32)
    ang = inv[np.arange(ROPE) % half][:, None] * pos[None, :]
    c[0:NOPE, C_COS:C_COS + T] = 1
    c[NOPE:QK, C_COS:C_COS + T] = np.cos(ang)
    c[NOPE:QK, C_SIN:C_SIN + T] = np.sin(ang)
    old = (PG * (4 * np.arange(4)[None, :, None] + (p // ROPE)[:, None, None]) + p[None, None, :]).astype(np.float32)
    ang = inv[p % half][:, None, None] * old
    c[:, C_COS4:C_COS4 + 512] = np.cos(ang).reshape(P, 512)
    c[:, C_SIN4:C_SIN4 + 512] = np.sin(ang).reshape(P, 512)
    c[:, C_HM:C_HM + 4] = p[:, None] // 32 == np.arange(4)[None, :]
    c[:, C_BM:C_BM + 256] = p[:, None] // 32 == np.arange(256)[None, :] // 64
    c[:, C_TRI:C_TRI + 256] = p[:, None] <= np.arange(256)[None, :] % 64
    c[:, C_BAND + 96:C_BAND + 128] = 1
    t = np.concatenate([np.arange(TP), np.full(B, PG * PAGES)])
    for g, w in enumerate((2, 4, 8, 16)):
        c[64 * (g % 2):64 * (g % 2) + 64, C_INV + (g // 2) * T:C_INV + (g // 2 + 1) * T] = 1 / np.minimum(w, t + 1)
    return c


def kernel(**inputs):
    import numpy as np
    import concourse.bacc as _bacc
    from concourse import mybir as _mybir
    from concourse.bass_utils import run_bass_kernel_spmd as _run

    a = {k: np.asarray(v) for k, v in inputs.items()}
    f32 = np.float32

    def columns(v, n):
        return v.reshape(DEPTH, n, P).transpose(0, 2, 1)

    def tiled(w):
        k, n = w.shape[1:]
        v = w.reshape(DEPTH, k // D, KD, P, n // 256, 2, P)
        return v.transpose(0, 4, 1, 3, 5, 2, 6).reshape(DEPTH, -1, P, UNIT)

    off = np.cumsum([0, 384, 256, 32, 128, 128, 256, 16, 256, 256])
    w_in = np.zeros((DEPTH, D, 16 * P), f32)
    for tile, part, shift in ((CQ, 0, 0), (CKV, 1, 0), (KR, 2, NOPE), (GQ, 3, 0), (GK, 4, 0), (GV, 5, 0), (GLOW, 6, 0), (GR, 7, 0), (UU, 8, 0)):
        w = a["w_in"][:, :, off[part]:off[part + 1]]
        w_in[:, :, tile * P + shift:tile * P + shift + w.shape[2]] = w
    w_xv = a["w_xv"].reshape(DEPTH, KD, P, H, 256).transpose(0, 3, 2, 1, 4).reshape(DEPTH, H, P, UNIT)
    xk = a["cache_mem_k"].transpose(1, 0, 3, 4, 2).reshape(DEPTH, B, H * 2, P, NM).transpose(0, 1, 3, 2, 4).reshape(DEPTH, B, P, UNIT)
    xv = a["cache_mem_v"].transpose(1, 0, 2, 3, 4).reshape(DEPTH, B, 2, P, D).transpose(0, 1, 3, 2, 4).reshape(DEPTH, B, P, UNIT)
    units = np.concatenate([tiled(w_in), tiled(a["w_xk"]), w_xv, tiled(a["w_out"]), tiled(a["w_xq"]), xk, xv, tiled(a["w_xo"]),
                            tiled(a["w_ff1"]), tiled(a["w_ff2"])], axis=1).reshape(DEPTH * UNITS, P, UNIT)

    x = np.concatenate([a["x_prompt"].reshape(TP, D), a["x_sample"].reshape(B, D)])
    xt = x.reshape(T, KD, P).transpose(2, 1, 0)
    memt = a["mem_prompt"].reshape(NM, KD, P).transpose(2, 1, 0)
    lat = a["cache_mla_latent"]
    n_phys = lat.shape[0]
    lat_t = lat.transpose(0, 1, 3, 2).reshape(n_phys, DEPTH, 2, P, PG).transpose(0, 1, 3, 2, 4).reshape(n_phys, DEPTH, P, 256)
    pages = np.concatenate([lat_t, lat, a["cache_mla_krope"]], axis=3).reshape(n_phys * DEPTH, P, 544)
    table = a["page_table"].reshape(1, B * PAGES)

    gains = np.zeros((DEPTH, P, NG), f32)
    for c, name, n in ((G_MIX, "norm_mix", 8), (G_XA, "norm_xa", 8), (G_MLP, "norm_mlp", 8), (G_MEM, "norm_mem", 8), (G_QL, "g_q_lat", 3),
                       (G_KV, "g_kv_lat", 2), (B_GATE, "b_gate", 1), (G_POOL, "pool_scale", 2), (G_XQ, "g_xq", 2), (G_XK, "g_xk", 2)):
        gains[:, :, c:c + n] = columns(a[name], n)
    gains[:, 0:QK, G_Q] = a["g_qk_q"]
    gains[:, 0:QK, G_K] = a["g_qk_k"]
    gains[:, :, G_KR4] = np.tile(a["g_qk_k"][:, NOPE:], (1, 4))
    gains[:, :, G_GLA] = np.tile(a["g_gla_out"], (1, 2))
    gains = gains.transpose(1, 0, 2)

    mats = np.zeros((DEPTH, P, NMAT), f32)
    mats[:, :, M_UQ:M_UQ + 1152] = a["w_uq"].reshape(DEPTH, 3, P, H * QK).transpose(0, 2, 1, 3).reshape(DEPTH, P, -1)
    mats[:, :, M_UK:M_UK + 512] = a["w_uk"].reshape(DEPTH, 2, P, 256).transpose(0, 2, 1, 3).reshape(DEPTH, P, -1)
    mats[:, :, M_UV:M_UV + 1024] = a["w_uv"].reshape(DEPTH, 2, P, 512).transpose(0, 2, 1, 3).reshape(DEPTH, P, -1)
    mats[:, 0:NOPE, M_UKT:M_UKT + 1024] = a["w_uk"].transpose(0, 3, 2, 1).reshape(DEPTH, NOPE, 1024)
    mats[:, 0:16, M_GATE:M_GATE + P] = a["w_gate_up"]
    for g in range(4):
        r = 64 * (g % 2)
        o = M_POOL + (g // 2) * P + r
        mats[:, r:r + 64, o:o + 64] = a["w_pool"][:, g]

    gstate = a["state_gla"].reshape(B, DEPTH, P, 64).transpose(1, 2, 0, 3)
    pstate = a["state_pool"].transpose(1, 3, 0, 2).reshape(DEPTH, 2, P, B, 15).transpose(0, 2, 1, 3, 4)
    pstate_nat = a["state_pool"].transpose(1, 0, 2, 3)[:, :, 1:]

    nc = _bacc.Bacc("TRN2", target_bir_lowering=False, num_devices=1, dynamic_dma_scratch_size=8192)
    arrays, args = {}, []
    for name, v in dict(units=units, xt=xt, memt=memt, pages=pages, table=table, gains=gains, mats=mats,
                        consts=_constants(), gstate=gstate, pstate=pstate, pstate_nat=pstate_nat).items():
        v = np.ascontiguousarray(v)
        arrays[f"in_{name}"] = v
        args.append(nc.dram_tensor(f"in_{name}", v.shape, _mybir.dt.from_np(v.dtype), kind="ExternalInput").ap())
    outs = dict(y=(P, KD, T), lat=(DEPTH, P, 2, T), kr=(DEPTH, ROPE, T), glap=(DEPTH, P, 256), glas=(DEPTH, P, B, 64), u=(DEPTH, P, 2, T),
                pool=(DEPTH, B, 14, 256), mk=(DEPTH, P, 8, NM), mv=(DEPTH, P, 2, D))
    for name, shape in outs.items():
        args.append(nc.dram_tensor(f"out_{name}", shape, FP32, kind="ExternalOutput").ap())
    args.append(nc.dram_tensor("gla_values", (B, 256), FP32, kind="Internal").ap())
    decoder(nc, *args)
    r = _run(nc, [arrays], core_ids=[0]).results[0]
    o = {name: r[f"out_{name}"] for name in outs}

    y = o["y"].transpose(2, 1, 0).reshape(T, D)
    latent = o["lat"].transpose(0, 3, 2, 1).reshape(DEPTH, T, 256)
    kr = o["kr"].transpose(0, 2, 1)
    u = o["u"].transpose(0, 3, 2, 1).reshape(DEPTH, T, 256)
    glap = np.stack([o["glap"][:, 32 * h:32 * h + 32, 64 * h:64 * h + 64] for h in range(H)], axis=1)
    glas = o["glas"].reshape(DEPTH, H, 32, B, 64).transpose(3, 0, 1, 2, 4)
    mk = o["mk"].transpose(0, 3, 2, 1).reshape(1, DEPTH, NM, H, 256)
    mv = o["mv"].transpose(0, 2, 1, 3).reshape(1, DEPTH, NM, H, 256)
    pool_s = np.concatenate([o["pool"].transpose(1, 0, 2, 3), u[:, TP:].transpose(1, 0, 2)[:, :, None]], axis=2)
    return (y[None, :TP], y[TP:, None], latent[None, :, :TP], kr[None, :, :TP], glap[None], u[None, :, TP - 15:TP], mk, mv,
            latent[:, TP:].transpose(1, 0, 2)[:, :, None], kr[:, TP:].transpose(1, 0, 2)[:, :, None], glas, pool_s)
```
